# Optimizing a Trainium2 kernel written in Bass

```python
import jax, jax.numpy as jnp
from jax import lax
import numpy as np

D_MODEL = 1024
BATCH = 1
SEQ = 256
DEPTH = 1

N_MIXERS = 2
D_RNN = 1280
LRU_BLOCKS = 16
LRU_BLOCK_W = D_RNN // LRU_BLOCKS
CONV_W = 4
LRU_C = 8.0
N_HEADS = 16
N_KV_HEADS = 4
HEAD_DIM = 64
GROUP = N_HEADS // N_KV_HEADS
WINDOW = 128
ATT_BLOCK = WINDOW
Q_DIM = N_HEADS * HEAD_DIM
KV_DIM = N_KV_HEADS * HEAD_DIM
QKV_DIM = Q_DIM + 2 * KV_DIM
N_GROUPS = 4
EXPERTS_PER_GROUP = 8
N_EXPERTS = N_GROUPS * EXPERTS_PER_GROUP
TOP_K = 2
D_EXPERT = 512
MOE_BLOCK = 128
ALPHA = (2 * DEPTH) ** 0.25
BETA = (8 * DEPTH) ** -0.25
LN_EPS = 1e-5
N_REC_LAYERS = (DEPTH + N_MIXERS - 1) // N_MIXERS
N_ATT_LAYERS = DEPTH // N_MIXERS


def layer_norm(x, g, b):
    xf = x.astype(jnp.float32)
    mu = jnp.mean(xf, axis=-1, keepdims=True)
    xc = xf - mu
    var = jnp.mean(xc * xc, axis=-1, keepdims=True)
    y = xc * lax.rsqrt(var + LN_EPS) * g.astype(jnp.float32) + b.astype(jnp.float32)
    return y.astype(x.dtype)

def _linear_recurrence_combine(c1, c2):
    a1, b1 = c1
    a2, b2 = c2
    return a1 * a2, a2 * b1 + b2

def rglru_block(x, w_in, conv_w, conv_b, w_r, b_r, w_i, b_i, lam, w_out):
    B, S, _ = x.shape
    gate, xr = jnp.split(x @ w_in, 2, axis=-1)
    xp = jnp.pad(xr, ((0, 0), (CONV_W - 1, 0), (0, 0)))
    xc = conv_b + sum(xp[:, k:k + S] * conv_w[k] for k in range(CONV_W))
    xb = xc.reshape(B, S, LRU_BLOCKS, LRU_BLOCK_W)
    r = jax.nn.sigmoid(jnp.einsum('bsnk,nkj->bsnj', xb, w_r).reshape(B, S, D_RNN) + b_r)
    i = jax.nn.sigmoid(jnp.einsum('bsnk,nkj->bsnj', xb, w_i).reshape(B, S, D_RNN) + b_i)
    log_a = -LRU_C * r.astype(jnp.float32) * jax.nn.softplus(-lam.astype(jnp.float32))
    a = jnp.exp(log_a)
    u = jnp.sqrt(-jnp.expm1(2.0 * log_a)) * (i * xc).astype(jnp.float32)
    _, h = lax.associative_scan(_linear_recurrence_combine, (a, u), axis=1)
    y = h.astype(x.dtype) * jax.nn.gelu(gate)
    return y @ w_out

def alibi_slopes():
    return 2.0 ** (-8.0 * jnp.arange(1, N_HEADS + 1, dtype=jnp.float32) / N_HEADS)

def _with_prev_block(t):
    prev = jnp.concatenate([jnp.zeros_like(t[:, :1]), t[:, :-1]], axis=1)
    return jnp.concatenate([prev, t], axis=2)

def swa_sink_alibi(x, w_qkv, sinks, w_o):
    B, S, _ = x.shape
    NB = S // ATT_BLOCK
    qkv = x @ w_qkv
    q = qkv[..., :Q_DIM].reshape(B, NB, ATT_BLOCK, N_KV_HEADS, GROUP, HEAD_DIM) * (HEAD_DIM ** -0.5)
    k = qkv[..., Q_DIM:Q_DIM + KV_DIM].reshape(B, NB, ATT_BLOCK, N_KV_HEADS, HEAD_DIM)
    v = qkv[..., Q_DIM + KV_DIM:].reshape(B, NB, ATT_BLOCK, N_KV_HEADS, HEAD_DIM)
    kk = _with_prev_block(k)
    vv = _with_prev_block(v)
    s = jnp.einsum('bnqkgd,bnskd->bnkgqs', q, kk).astype(jnp.float32)
    qi = jnp.arange(ATT_BLOCK)[:, None]
    sj = jnp.arange(2 * ATT_BLOCK)[None, :]
    dist = qi - sj + ATT_BLOCK
    valid = (dist >= 0) & (dist < WINDOW)
    not_before_start = (jnp.arange(NB)[:, None, None] > 0) | (sj[None] >= ATT_BLOCK)
    mask = valid[None] & not_before_start
    slopes = alibi_slopes().reshape(N_KV_HEADS, GROUP)
    s = s - slopes[:, :, None, None] * dist.astype(jnp.float32)
    s = jnp.where(mask[None, :, None, None], s, -jnp.inf)
    sink = sinks.astype(jnp.float32).reshape(N_KV_HEADS, GROUP)[None, None, :, :, None, None]
    m = jnp.maximum(jnp.max(s, axis=-1, keepdims=True), sink)
    p = jnp.exp(s - m)
    denom = jnp.sum(p, axis=-1, keepdims=True) + jnp.exp(sink - m)
    o = jnp.einsum('bnkgqs,bnskd->bnqkgd', (p / denom).astype(x.dtype), vv)
    return o.reshape(B, S, Q_DIM) @ w_o

def hier_moe(x, w_rg, b_rg, w_re, b_re, w1, w3, w2):
    B, S, D = x.shape
    T = B * S
    TK = T * TOP_K
    xf = x.reshape(T, D)
    g_logits = (xf @ w_rg + b_rg).astype(jnp.float32)
    g_idx = jnp.argmax(g_logits, axis=-1)
    g_gate = jnp.take_along_axis(jax.nn.softmax(g_logits, axis=-1), g_idx[:, None], axis=1)
    e_logits = (xf @ w_re + b_re).astype(jnp.float32).reshape(T, N_GROUPS, EXPERTS_PER_GROUP)
    e_in_group = jnp.take_along_axis(e_logits, g_idx[:, None, None], axis=1)[:, 0]
    top_v, top_i = lax.top_k(e_in_group, TOP_K)
    gates = jax.nn.softmax(top_v, axis=-1) * g_gate
    expert = g_idx[:, None] * EXPERTS_PER_GROUP + top_i
    flat_e = expert.reshape(TK)
    order = jnp.argsort(flat_e)
    sorted_e = flat_e[order]
    counts = jnp.bincount(flat_e, length=N_EXPERTS)
    padded = ((counts + MOE_BLOCK - 1) // MOE_BLOCK) * MOE_BLOCK
    starts = jnp.cumsum(counts) - counts
    pends = jnp.cumsum(padded)
    pstarts = pends - padded
    dest = pstarts[sorted_e] + (jnp.arange(TK) - starts[sorted_e])
    slot_dest = jnp.zeros_like(dest).at[order].set(dest)
    n_blocks = -(-(TK + N_EXPERTS * (MOE_BLOCK - 1)) // MOE_BLOCK)
    n_rows = n_blocks * MOE_BLOCK
    xbuf = jnp.zeros((n_rows, D), x.dtype).at[slot_dest].set(jnp.repeat(xf, TOP_K, axis=0))
    block_start = jnp.arange(n_blocks) * MOE_BLOCK
    block_e = jnp.minimum(jnp.sum(block_start[:, None] >= pends[None, :], axis=1), N_EXPERTS - 1)

    def expert_block(args):
        xb, e = args
        hdn = jax.nn.silu(xb @ w1[e]) * (xb @ w3[e])
        return hdn @ w2[e]

    ybuf = lax.map(expert_block, (xbuf.reshape(n_blocks, MOE_BLOCK, D), block_e)).reshape(n_rows, D)
    y_slots = ybuf[slot_dest].reshape(T, TOP_K, D)
    out = jnp.einsum('tk,tkd->td', gates.astype(x.dtype), y_slots)
    return out.reshape(B, S, D)

def first_inputs(seed: int = 0) -> dict:
    key = jax.random.key(seed)
    ks = jax.random.split(key, 24)

    def nrm(k, shape, scale):
        return jax.random.normal(k, shape, jnp.float32) * scale

    x = nrm(ks[0], (BATCH, SEQ, D_MODEL), 1.0)
    rec_w_in = nrm(ks[1], (N_REC_LAYERS, D_MODEL, 2 * D_RNN), D_MODEL ** -0.5)
    rec_conv_w = nrm(ks[2], (N_REC_LAYERS, CONV_W, D_RNN), CONV_W ** -0.5)
    rec_conv_b = nrm(ks[3], (N_REC_LAYERS, D_RNN), 0.01)
    rec_w_r = nrm(ks[4], (N_REC_LAYERS, LRU_BLOCKS, LRU_BLOCK_W, LRU_BLOCK_W), LRU_BLOCK_W ** -0.5)
    rec_b_r = nrm(ks[5], (N_REC_LAYERS, D_RNN), 0.01)
    rec_w_i = nrm(ks[6], (N_REC_LAYERS, LRU_BLOCKS, LRU_BLOCK_W, LRU_BLOCK_W), LRU_BLOCK_W ** -0.5)
    rec_b_i = nrm(ks[7], (N_REC_LAYERS, D_RNN), 0.01)
    a_c = jax.random.uniform(ks[8], (N_REC_LAYERS, D_RNN), jnp.float32, minval=0.9, maxval=0.999)
    a0 = a_c ** (1.0 / LRU_C)
    rec_lambda = jnp.log(a0) - jnp.log1p(-a0)
    rec_w_out = nrm(ks[9], (N_REC_LAYERS, D_RNN, D_MODEL), BETA * D_RNN ** -0.5)
    col_scale = jnp.concatenate([jnp.ones((Q_DIM + KV_DIM,), jnp.float32), jnp.full((KV_DIM,), BETA, jnp.float32)])
    att_w_qkv = nrm(ks[10], (N_ATT_LAYERS, D_MODEL, QKV_DIM), D_MODEL ** -0.5) * col_scale
    att_sinks = nrm(ks[11], (N_ATT_LAYERS, N_HEADS), 0.5)
    att_w_o = nrm(ks[12], (N_ATT_LAYERS, Q_DIM, D_MODEL), BETA * Q_DIM ** -0.5)
    moe_w_group = nrm(ks[13], (DEPTH, D_MODEL, N_GROUPS), D_MODEL ** -0.5)
    moe_b_group = nrm(ks[14], (DEPTH, N_GROUPS), 0.01)
    moe_w_expert = nrm(ks[15], (DEPTH, D_MODEL, N_EXPERTS), D_MODEL ** -0.5)
    moe_b_expert = nrm(ks[16], (DEPTH, N_EXPERTS), 0.01)
    moe_w1 = nrm(ks[17], (DEPTH, N_EXPERTS, D_MODEL, D_EXPERT), D_MODEL ** -0.5)
    moe_w3 = nrm(ks[18], (DEPTH, N_EXPERTS, D_MODEL, D_EXPERT), D_MODEL ** -0.5)
    moe_w2 = nrm(ks[19], (DEPTH, N_EXPERTS, D_EXPERT, D_MODEL), BETA * D_EXPERT ** -0.5)
    ln_g = 1.0 + nrm(ks[20], (DEPTH, 2, D_MODEL), 0.02)
    ln_b = nrm(ks[21], (DEPTH, 2, D_MODEL), 0.02)
    return {'x': x, 'rec_w_in': rec_w_in, 'rec_conv_w': rec_conv_w, 'rec_conv_b': rec_conv_b,
            'rec_w_r': rec_w_r, 'rec_b_r': rec_b_r, 'rec_w_i': rec_w_i, 'rec_b_i': rec_b_i,
            'rec_lambda': rec_lambda, 'rec_w_out': rec_w_out, 'att_w_qkv': att_w_qkv,
            'att_sinks': att_sinks, 'att_w_o': att_w_o, 'moe_w_group': moe_w_group,
            'moe_b_group': moe_b_group, 'moe_w_expert': moe_w_expert, 'moe_b_expert': moe_b_expert,
            'moe_w1': moe_w1, 'moe_w3': moe_w3, 'moe_w2': moe_w2, 'ln_g': ln_g, 'ln_b': ln_b}

def first_block(x, rec_w_in, rec_conv_w, rec_conv_b, rec_w_r, rec_b_r, rec_w_i, rec_b_i, rec_lambda,
              rec_w_out, att_w_qkv, att_sinks, att_w_o, moe_w_group, moe_b_group, moe_w_expert,
              moe_b_expert, moe_w1, moe_w3, moe_w2, ln_g, ln_b):
    for layer in range(DEPTH):
        j = layer // N_MIXERS
        if layer % N_MIXERS == 0:
            h = rglru_block(x, rec_w_in[j], rec_conv_w[j], rec_conv_b[j], rec_w_r[j], rec_b_r[j],
                            rec_w_i[j], rec_b_i[j], rec_lambda[j], rec_w_out[j])
        else:
            h = swa_sink_alibi(x, att_w_qkv[j], att_sinks[j], att_w_o[j])
        x = layer_norm(ALPHA * x + h, ln_g[layer, 0], ln_b[layer, 0])
        f = hier_moe(x, moe_w_group[layer], moe_b_group[layer], moe_w_expert[layer], moe_b_expert[layer],
                     moe_w1[layer], moe_w3[layer], moe_w2[layer])
        x = layer_norm(ALPHA * x + f, ln_g[layer, 1], ln_b[layer, 1])
    return x


DEPTH_2 = 2

ALPHA_2 = (2 * DEPTH_2) ** 0.25
BETA_2 = (8 * DEPTH_2) ** -0.25
N_A = (DEPTH_2 + 1) // 2
N_B = DEPTH_2 // 2
D_FF = 2816
ML_HEADS = 4
ML_DQK = D_MODEL // (2 * ML_HEADS)
ML_DV = D_MODEL // ML_HEADS
ML_QK = ML_HEADS * ML_DQK
ML_PROJ = 2 * ML_QK + 2 * D_MODEL + 4 * ML_HEADS
CHUNK = 64
N_Q_HEADS = D_MODEL // HEAD_DIM
GROUP_2 = N_Q_HEADS // N_KV_HEADS
BLOCK = 128
AT_PROJ = (N_Q_HEADS + 2 * N_KV_HEADS) * HEAD_DIM
MASK_VALUE = -1e30


def layer_norm_2(x, g, b):
    xf = x.astype(jnp.float32)
    mu = jnp.mean(xf, axis=-1, keepdims=True)
    var = jnp.mean(jnp.square(xf - mu), axis=-1, keepdims=True)
    return ((xf - mu) * lax.rsqrt(var + LN_EPS) * g + b).astype(x.dtype)

def swiglu(x, w_in, w_out):
    gu = x @ w_in
    g, u = gu[..., :D_FF], gu[..., D_FF:]
    return (jax.nn.silu(g) * u) @ w_out

def mlstm_chunkwise(q, k, v, i_pre, f_pre):
    B, H, S, dk = q.shape
    dv = v.shape[-1]
    nc = S // CHUNK
    q = q.astype(jnp.float32).reshape(B, H, nc, CHUNK, dk)
    k = k.astype(jnp.float32).reshape(B, H, nc, CHUNK, dk)
    v = v.astype(jnp.float32).reshape(B, H, nc, CHUNK, dv)
    logf = jax.nn.log_sigmoid(f_pre.astype(jnp.float32)).reshape(B, H, nc, CHUNK)
    ig = i_pre.astype(jnp.float32).reshape(B, H, nc, CHUNK)
    g = jnp.cumsum(logf, axis=-1)
    G = g[..., -1]
    w_end = G[..., None] - g + ig
    a = jnp.max(w_end, axis=-1)
    e_end = jnp.exp(w_end - a[..., None])
    K_c = jnp.einsum('bhcl,bhclv,bhclk->bhcvk', e_end, v, k)
    N_c = jnp.einsum('bhcl,bhclk->bhck', e_end, k)

    def step(carry, inp):
        C, n, m = carry
        Gc, ac, Kc, Nc = inp
        m_new = jnp.maximum(Gc + m, ac)
        sp = jnp.exp(Gc + m - m_new)
        sc = jnp.exp(ac - m_new)
        C_new = sp[..., None, None] * C + sc[..., None, None] * Kc
        n_new = sp[..., None] * n + sc[..., None] * Nc
        return (C_new, n_new, m_new), (C, n, m)

    init = (jnp.zeros((B, H, dv, dk), jnp.float32), jnp.zeros((B, H, dk), jnp.float32),
            jnp.zeros((B, H), jnp.float32))
    xs = (jnp.moveaxis(G, 2, 0), jnp.moveaxis(a, 2, 0), jnp.moveaxis(K_c, 2, 0), jnp.moveaxis(N_c, 2, 0))
    _, (C0, n0, m0) = lax.scan(step, init, xs)
    C0 = jnp.moveaxis(C0, 0, 2)
    n0 = jnp.moveaxis(n0, 0, 2)
    m0 = jnp.moveaxis(m0, 0, 2)

    tril = jnp.tril(jnp.ones((CHUNK, CHUNK), dtype=bool))
    dmat = g[..., :, None] - g[..., None, :] + ig[..., None, :]
    dmat = jnp.where(tril, dmat, MASK_VALUE)
    inter_log = g + m0[..., None]
    m_out = jnp.maximum(inter_log, jnp.max(dmat, axis=-1))
    wts = jnp.exp(dmat - m_out[..., None])
    s_inter = jnp.exp(inter_log - m_out)
    s_qk = jnp.einsum('bhcjd,bhcsd->bhcjs', q, k) * wts
    num = jnp.einsum('bhcjs,bhcsv->bhcjv', s_qk, v) + s_inter[..., None] * jnp.einsum('bhcvd,bhcjd->bhcjv', C0, q)
    den = jnp.sum(s_qk, axis=-1) + s_inter * jnp.einsum('bhcd,bhcjd->bhcj', n0, q)
    den = jnp.maximum(jnp.abs(den), jnp.exp(-m_out))
    h = num / den[..., None]
    return h.reshape(B, H, S, dv)

def mlstm_mixer(x, w_in, gate_b, norm_g, w_out):
    B, S, _ = x.shape
    p = x @ w_in
    q = p[..., :ML_QK].reshape(B, S, ML_HEADS, ML_DQK).transpose(0, 2, 1, 3)
    k = p[..., ML_QK:2 * ML_QK].reshape(B, S, ML_HEADS, ML_DQK).transpose(0, 2, 1, 3) * (ML_DQK ** -0.5)
    v = p[..., 2 * ML_QK:2 * ML_QK + D_MODEL].reshape(B, S, ML_HEADS, ML_DV).transpose(0, 2, 1, 3)
    o = p[..., 2 * ML_QK + D_MODEL:2 * ML_QK + 2 * D_MODEL]
    gates = (p[..., 2 * ML_QK + 2 * D_MODEL:] + gate_b).reshape(B, S, 4, ML_HEADS).transpose(2, 0, 3, 1)
    h_f = mlstm_chunkwise(q, k, v, gates[0], gates[1])
    flip = lambda a: jnp.flip(a, axis=2)
    h_b = flip(mlstm_chunkwise(flip(q), flip(k), flip(v), flip(gates[2]), flip(gates[3])))
    h = h_f + h_b
    mu = jnp.mean(h, axis=-1, keepdims=True)
    var = jnp.mean(jnp.square(h - mu), axis=-1, keepdims=True)
    h = (h - mu) * lax.rsqrt(var + LN_EPS)
    h = h.transpose(0, 2, 1, 3).reshape(B, S, D_MODEL) * norm_g
    out = jax.nn.sigmoid(o.astype(jnp.float32)) * h
    return out.astype(x.dtype) @ w_out

def alibi_slopes_2():
    return jnp.exp2(-8.0 * jnp.arange(1, N_Q_HEADS + 1, dtype=jnp.float32) / N_Q_HEADS)

def window_attention(x, w_in, sink, w_out):
    B, S, _ = x.shape
    nb = S // BLOCK
    p = x @ w_in
    nq = N_Q_HEADS * HEAD_DIM
    nk = N_KV_HEADS * HEAD_DIM
    q = p[..., :nq].reshape(B, nb, BLOCK, N_KV_HEADS, GROUP_2, HEAD_DIM)
    k = p[..., nq:nq + nk].reshape(B, S, N_KV_HEADS, HEAD_DIM)
    v = p[..., nq + nk:].reshape(B, S, N_KV_HEADS, HEAD_DIM)
    pad = ((0, 0), (BLOCK, BLOCK), (0, 0), (0, 0))
    kp = jnp.pad(k, pad).reshape(B, nb + 2, BLOCK, N_KV_HEADS, HEAD_DIM)
    vp = jnp.pad(v, pad).reshape(B, nb + 2, BLOCK, N_KV_HEADS, HEAD_DIM)
    kw = jnp.concatenate([kp[:, :-2], kp[:, 1:-1], kp[:, 2:]], axis=2)
    vw = jnp.concatenate([vp[:, :-2], vp[:, 1:-1], vp[:, 2:]], axis=2)
    s = jnp.einsum('bnqkgd,bnskd->bnkgqs', q, kw).astype(jnp.float32) * (HEAD_DIM ** -0.5)
    qi = jnp.arange(BLOCK)[:, None]
    kj = jnp.arange(3 * BLOCK)[None, :]
    rel = qi - kj + BLOCK
    dist = jnp.abs(rel).astype(jnp.float32)
    key_pos = jnp.arange(nb)[:, None] * BLOCK - BLOCK + jnp.arange(3 * BLOCK)[None, :]
    valid = (jnp.abs(rel) <= WINDOW)[None] & ((key_pos >= 0) & (key_pos < S))[:, None, :]
    slopes = alibi_slopes_2().reshape(N_KV_HEADS, GROUP_2)
    s = s - slopes[:, :, None, None] * dist
    s = jnp.where(valid[None, :, None, None], s, MASK_VALUE)
    sink_l = sink.astype(jnp.float32).reshape(N_KV_HEADS, GROUP_2)[None, None, :, :, None, None]
    m = jnp.maximum(jnp.max(s, axis=-1, keepdims=True), sink_l)
    pe = jnp.exp(s - m)
    attn = pe / (jnp.sum(pe, axis=-1, keepdims=True) + jnp.exp(sink_l - m))
    o = jnp.einsum('bnkgqs,bnskd->bnqkgd', attn, vw.astype(jnp.float32)).reshape(B, S, nq)
    return o.astype(x.dtype) @ w_out

def second_inputs(seed: int = 0) -> dict:
    key = jax.random.key(seed)
    ks = jax.random.split(key, 16)
    nrm = jax.random.normal
    x = nrm(ks[0], (BATCH, SEQ, D_MODEL), jnp.float32)
    ffn_w_in = nrm(ks[1], (DEPTH_2, 2, D_MODEL, 2 * D_FF), jnp.float32) * D_MODEL ** -0.5
    ffn_w_out = nrm(ks[2], (DEPTH_2, 2, D_FF, D_MODEL), jnp.float32) * (D_FF ** -0.5 * BETA_2)
    ln_g = 1.0 + 0.02 * nrm(ks[3], (DEPTH_2, 3, D_MODEL), jnp.float32)
    ln_b = 0.02 * nrm(ks[4], (DEPTH_2, 3, D_MODEL), jnp.float32)
    ml_w_in = nrm(ks[5], (N_A, D_MODEL, ML_PROJ), jnp.float32) * D_MODEL ** -0.5
    ml_w_in = ml_w_in.at[..., 2 * ML_QK:2 * ML_QK + D_MODEL].multiply(BETA_2)
    f_off = jnp.linspace(3.0, 6.0, ML_HEADS, dtype=jnp.float32)
    zero = jnp.zeros((ML_HEADS,), jnp.float32)
    gate_off = jnp.stack([zero, f_off, zero, f_off])
    ml_gate_b = (0.1 * nrm(ks[6], (N_A, 4, ML_HEADS), jnp.float32) + gate_off).reshape(N_A, 4 * ML_HEADS)
    ml_norm_g = 1.0 + 0.02 * nrm(ks[7], (N_A, D_MODEL), jnp.float32)
    ml_w_out = nrm(ks[8], (N_A, D_MODEL, D_MODEL), jnp.float32) * (D_MODEL ** -0.5 * BETA_2)
    at_w_in = nrm(ks[9], (N_B, D_MODEL, AT_PROJ), jnp.float32) * D_MODEL ** -0.5
    at_w_in = at_w_in.at[..., (N_Q_HEADS + N_KV_HEADS) * HEAD_DIM:].multiply(BETA_2)
    at_sink = 0.5 * nrm(ks[10], (N_B, N_Q_HEADS), jnp.float32)
    at_w_out = nrm(ks[11], (N_B, D_MODEL, D_MODEL), jnp.float32) * (D_MODEL ** -0.5 * BETA_2)
    return {"x": x, "ffn_w_in": ffn_w_in, "ffn_w_out": ffn_w_out, "ln_g": ln_g, "ln_b": ln_b,
            "ml_w_in": ml_w_in, "ml_gate_b": ml_gate_b, "ml_norm_g": ml_norm_g, "ml_w_out": ml_w_out,
            "at_w_in": at_w_in, "at_sink": at_sink, "at_w_out": at_w_out}

def second_block(x, ffn_w_in, ffn_w_out, ln_g, ln_b, ml_w_in, ml_gate_b, ml_norm_g, ml_w_out,
              at_w_in, at_sink, at_w_out):
    for l in range(DEPTH_2):
        x = layer_norm_2(ALPHA_2 * x + 0.5 * swiglu(x, ffn_w_in[l, 0], ffn_w_out[l, 0]), ln_g[l, 0], ln_b[l, 0])
        j = l // N_MIXERS
        if l % N_MIXERS == 0:
            y = mlstm_mixer(x, ml_w_in[j], ml_gate_b[j], ml_norm_g[j], ml_w_out[j])
        else:
            y = window_attention(x, at_w_in[j], at_sink[j], at_w_out[j])
        x = layer_norm_2(ALPHA_2 * x + y, ln_g[l, 1], ln_b[l, 1])
        x = layer_norm_2(ALPHA_2 * x + 0.5 * swiglu(x, ffn_w_in[l, 1], ffn_w_out[l, 1]), ln_g[l, 2], ln_b[l, 2])
    return x


def setup_inputs(seed=0):
    out = dict(first_inputs(seed))
    for name, value in second_inputs(seed + 1).items():
        if name != "x":
            out[name + "_2"] = value
    return out


def reference(
    x, rec_w_in, rec_conv_w, rec_conv_b, rec_w_r, rec_b_r, rec_w_i, rec_b_i, rec_lambda,
    rec_w_out, att_w_qkv, att_sinks, att_w_o, moe_w_group, moe_b_group, moe_w_expert,
    moe_b_expert, moe_w1, moe_w3, moe_w2, ln_g, ln_b, ffn_w_in_2, ffn_w_out_2, ln_g_2, ln_b_2,
    ml_w_in_2, ml_gate_b_2, ml_norm_g_2, ml_w_out_2, at_w_in_2, at_sink_2, at_w_out_2,
):
    x = first_block(
        x, rec_w_in, rec_conv_w, rec_conv_b, rec_w_r, rec_b_r, rec_w_i, rec_b_i, rec_lambda,
        rec_w_out, att_w_qkv, att_sinks, att_w_o, moe_w_group, moe_b_group, moe_w_expert,
        moe_b_expert, moe_w1, moe_w3, moe_w2, ln_g, ln_b,
    )
    return second_block(
        x, ffn_w_in_2, ffn_w_out_2, ln_g_2, ln_b_2, ml_w_in_2, ml_gate_b_2, ml_norm_g_2,
        ml_w_out_2, at_w_in_2, at_sink_2, at_w_out_2,
    )


_drawn_inputs = setup_inputs


def setup_inputs(seed=0):
    import zlib

    import numpy as np

    out = dict(_drawn_inputs(seed))
    spreads = {}
    factors = {'rec_conv_b': 2.821,
     'rec_b_r': 34.006,
     'rec_b_i': 26.102,
     'moe_b_group': 4.853,
     'moe_b_expert': 4.93,
     'ml_norm_g_2': 26.488,
     'at_sink_2': 31.648}
    for name, (base, spread) in spreads.items():
        noise = np.random.default_rng([zlib.crc32(name.encode()), seed]).standard_normal(out[name].shape)
        drawn = base * np.exp(spread * noise) if base else spread * noise
        out[name] = __import__('jax').numpy.asarray(drawn.astype(out[name].dtype))
    for name, factor in factors.items():
        out[name] = (out[name] * factor).astype(out[name].dtype)
    return out
```

```python
from contextlib import ExitStack

import numpy as np

import concourse.bass as bass
from concourse import mybir

F32 = mybir.dt.float32
F32R = mybir.dt.float32r
I32 = mybir.dt.int32
U32 = mybir.dt.uint32
ALU = mybir.AluOpType
ACT = mybir.ActivationFunctionType
AX_X = mybir.AxisListType.X

P = 128
T = 256
TT = T // P
D = 1024
KT = D // P
HALF = 512

D_RNN, NB, BW, CONV = 1280, 16, 80, 4
GROUPS = NB // 2
ALPHA = 2.0 ** 0.25
EPS = 1e-5

NG, EPG, NE, FE = 4, 8, 32, 512
C = 64
SLOTS = 2 * T
BLOCKS = T // C
BROWS = NE * 2 * C

ALPHA_2 = 4.0 ** 0.25
FF, FSTEP = 2816, 256
NSTEP = FF // FSTEP
MLH, DQK, DV = 4, 128, 256
NH, HD, NKV = 16, 64, 4
WINDOW = 128
NEG = -1e30

UNIT = 2048
RING = 12
N_LN = 8
SPLIT_NORMS = (1, 3, 4, 6)


class Own:

    def __init__(self, eng, sem):
        self.eng, self.sem, self.n = eng, sem, 0

    def did(self, ins):
        ins.then_inc(self.sem, 1)
        self.n += 1
        return self.n

    def then(self, ins):
        self.eng.wait_ge(self.sem, self.did(ins))


def build(nc, A, out, dbg=None, stages=99):
    ctx = ExitStack()
    with ctx:
        def sb(name, shape, dt=F32):
            return ctx.enter_context(nc.sbuf_tensor(name, shape, dt))

        def sem(name):
            return ctx.enter_context(nc.semaphore(name))

        ring = sb("ring", [P, RING, UNIT])
        arena_at = nc.sbuf_base
        arena = sb("arena", [P, 6 * UNIT])
        split = [[nc.alloc_sbuf_tensor_at(f"split_{kind}_{part}", [P, UNIT], F32R,
                                          offset=arena_at + (2 * j + i) * UNIT * 4)
                  for i, part in enumerate(("hi", "lo"))] for j, kind in enumerate("gud")]
        x_tok = sb("x_tok", [P, TT, D])
        xT = sb("xT", [P, KT, T])
        parts_at = nc.sbuf_base
        x_parts = sb("x_parts", [P, 2 * KT * T])
        x_hi, x_lo = [nc.alloc_sbuf_tensor_at(f"x_{part}", [P, KT, T], F32R, offset=parts_at + i * KT * T * 4)
                      for i, part in enumerate(("hi", "lo"))]
        h_hi = sb("h_hi", [P, 2, 2, T], F32R)
        h_lo = sb("h_lo", [P, 2, 2, T], F32R)
        work = sb("work", [P, 4 * T])
        silu = work[:, 0:2 * T].rearrange("p (a t) -> p a t", a=2)
        h_raw = work[:, 2 * T:].rearrange("p (a t) -> p a t", a=2)
        gb_row = sb("gb_row", [P, 2, D])
        ident = sb("ident", [P, P])
        upper = sb("upper", [P, P])
        lower = sb("lower", [P, P])
        strict = sb("strict", [P, P])
        ones = sb("ones", [P, P])
        gb_raw = sb("gb_raw", [P, P])
        gbT = sb("gbT", [P, P])
        misc_raw = sb("misc_raw", [P, BW])
        misc = sb("misc", [BW, P])
        ng_raw = sb("ng_raw", [KT, P])
        ngT = sb("ngT", [P, KT])
        small = sb("small", [P, 64])
        stats = sb("stats", [P, 2, 2, 6])
        mean_var = sb("mean_var", [P, 2, 2])
        rstd = sb("rstd", [P, 2])
        var_eps = sb("var_eps", [P, 2])
        neg_half = sb("neg_half", [P, 8])
        bank = [ctx.enter_context(nc.psum_tensor(f"bank{i}", [P, HALF], F32)) for i in range(8)]

        landed = [sem(f"landed{i}") for i in range(RING)]
        s_x, s_misc, s_gbrow, s_out = sem("s_x"), sem("s_misc"), sem("s_gbrow"), sem("s_out")
        consts, own_dve, own_pool = sem("consts"), sem("own_dve"), sem("own_pool")

        arena_v = lambda a, n: arena[:, a:a + n]
        unit = lambda n: ring[:, n % RING, :]

        rec_w_in = A["rec_w_in"][0].rearrange("(k p) n -> p k n", p=P)
        rec_w_out = A["rec_w_out"][0].rearrange("(n p) d -> p n d", p=BW)
        w1 = A["moe_w1"][0].rearrange("e (k p) f -> e p k f", p=P)
        w3 = A["moe_w3"][0].rearrange("e (k p) f -> e p k f", p=P)
        w2 = A["moe_w2"][0].rearrange("e (k p) d -> e p k d", p=P)

        UA = 3 * GROUPS
        UM = 6 * NE

        def unit_view(n, k):
            return unit(n).rearrange("p (k n) -> p k n", k=k)

        recA_used = sem("recA_used")

        if True:
            block = ctx.enter_context(nc.Block())

            g_ln = {}
            for name in ("ln_in", "ln_var", "ln_rstd", "ln_hat", "ln_tr", "ln_evac_act", "ln_evac_dve",
                         "ln_hi", "ln_lo", "ln_tok"):
                g_ln[name] = sem(name)
            G = g_ln

            r = {n: sem("rec_" + n) for n in ("gelu", "x_sb", "conv", "ri_mm", "tanh", "sqrt",
                                              "t", "y", "const", "q")}
            gelu = arena[0:BW, 8192:8192 + NB * T].rearrange("p (n t) -> p n t", n=NB)
            buf = lambda a: [arena[0:BW, a + g * 512:a + g * 512 + 512].rearrange("p (b t) -> p b t", b=2)
                             for g in range(2)]
            xp = [arena[0:BW, g * 518:g * 518 + 518].rearrange("p (b t) -> p b t", b=2) for g in range(2)]
            xc, th_r, th_i, root, rec_b = buf(1040), buf(2064), buf(3088), buf(4112), buf(5136)
            h_b = buf(6160)
            lam_q = sb("lam_q", [BW, 12, NB])

            mo = {n: sem("moe_" + n) for n in (
                "logit", "e1", "e2", "exp1", "exp2", "assign", "rank", "pos", "gath", "gath_ev", "start", "xe",
                "ha", "hb", "silu", "h", "tr", "hT", "y", "ysb", "h0", "diag", "rows", "rows_sb", "sel", "comb")}
            xs = arena[:, 0:KT * 768].rearrange("p (k s) -> p k s", k=KT)
            onehot = arena[:, 6144:7168].rearrange("p (t s) -> p t s", t=TT)
            xe = [arena[:, 7168 + i * 512:7680 + i * 512].rearrange("p (k c) -> p k c", k=KT) for i in range(2)]
            sil_e, h_e = arena[:, 8192:8704], arena[:, 8704:9216]
            hT_e = [arena[:, 9216 + i * 256:9472 + i * 256].rearrange("p (k c) -> p k c", k=4) for i in range(2)]
            y_e = [arena[:, 9728 + i * 512:10240 + i * 512] for i in range(2)]
            rows_b = arena[:, 10752:11776].rearrange("p (v t) -> p v t", v=4)
            rows_diag = arena[:, 8192:9216].rearrange("p (v t j) -> p v t j", v=4, t=TT)
            pick_e = [arena[:, 11776 + i * 256:12032 + i * 256] for i in range(2)]
            route_w = sb("route_w", [P, KT, NG + NE])
            route_b = sb("route_b", [P, NG + NE])
            RT = work
            iota_s = sb("iota_s", [P, SLOTS])
            start_i = sb("start_i", [1, NE + 1], I32)
            s_route, own_sel = sem("s_route"), sem("own_sel")
            sel_tmp = work[:, 0:T]

            def rt(a, *shape):
                n = int(np.prod(shape))
                v = RT[:, a:a + n]
                if len(shape) == 2:
                    return v.rearrange("p (a b) -> p a b", b=shape[1])
                if len(shape) == 3:
                    return v.rearrange("p (a b c) -> p a b c", b=shape[1], c=shape[2])
                return v

            lg = rt(0, TT, NG + NE)
            v_gmax, v_gsum, v_ggate = rt(72, TT), rt(74, TT), rt(76, TT)
            v_v1, v_v2, v_ed, v_p1 = rt(78, TT), rt(80, TT), rt(82, TT), rt(84, TT)
            v_m = rt(86, TT)
            g_c, g_oh = rt(88, TT, NG), rt(96, TT, NG)
            e_sel, e_c = rt(104, TT, EPG), rt(120, TT, EPG)
            oh = [rt(136, TT, EPG), rt(152, TT, EPG)]
            tmp32 = rt(168, TT, NG, EPG)
            A1 = [rt(232, TT, NG, EPG), rt(296, TT, NG, EPG)]
            A12 = rt(360, TT, NE)
            v_start, v_incl = rt(424, NE), rt(456, NE)
            v_q, v_full = rt(488, TT, NE), rt(552, NE)
            v_t = rt(616, TT, NE)
            v_pos = [rt(680, TT), rt(682, TT)]
            gates = [rt(688, TT), rt(690, TT)]
            slot_p = rt(692, 1)
            i_8m = rt(724, EPG)
            cmax = rt(732, 1)
            g_e = rt(733, TT, NG)
            v_rank = rt(744, TT, NE)
            v_cnt = rt(808, NE)
            place = rt(840, BLOCKS, NE)

            NXT = [None]

            rel = {}

            def sync_program(sp):
                sp.dma_start(x_tok[:], A["x"][0].rearrange("(t p) d -> p t d", p=P)).then_inc(s_x, 16)
                for n in range(UA):
                    if n >= RING:
                        sp.wait_ge(recA_used, n - RING + 1)
                    if n < 2 * GROUPS:
                        src = rec_w_in[:, :, n * 2 * BW:(n + 1) * 2 * BW]
                        dst = unit(n)[:, 0:KT * 2 * BW].rearrange("p (k n) -> p k n", k=KT)
                    else:
                        g = n - 2 * GROUPS
                        src = rec_w_out[:, 2 * g:2 * g + 2, :]
                        dst = unit_view(n, 2)[0:BW]
                    sp.dma_start(dst, src).then_inc(landed[n % RING], 16)
                if stages >= 2:
                    def expert_loads(e, p, wait):
                        for j in range(6):
                            if wait is not None:
                                wait(j)
                            n = 6 * p + j
                            if j < 4:
                                w = (w1, w3)[j % 2]
                                src = w[bass.ds(e, 1), :, 4 * (j // 2):4 * (j // 2) + 4, :].rearrange("e p k f -> (e p) k f") \
                                    if not isinstance(e, int) else w[e, :, 4 * (j // 2):4 * (j // 2) + 4, :]
                                dst = unit_view(n, 4)
                            else:
                                src = w2[bass.ds(e, 1), :, 2 * (j - 4):2 * (j - 4) + 2, :].rearrange("e p k f -> (e p) k f") \
                                    if not isinstance(e, int) else w2[e, :, 2 * (j - 4):2 * (j - 4) + 2, :]
                                dst = unit_view(n, 2)
                            sp.dma_start(dst, src).then_inc(landed[n], 16)

                    for p in range(2):
                        expert_loads(p, p, lambda j, p=p: sp.wait_ge(recA_used, UA - RING + 6 * p + j + 1) if 6 * p + j + 1 < RING
                                     else sp.wait_ge(G["ln_in"], TT))

                    with sp.Fori(1, NE // 2) as it:
                        for p in range(2):
                            def free(j, p=p):
                                if j < 4:
                                    sp.wait_ge(mo["ha"] if j < 2 else mo["hb"], 2 * it + p - 1)
                                else:
                                    sp.wait_ge(mo["y"], 2 * it + p - 1)
                            expert_loads(2 * it + p, p, free)
                    sp.wait_ge(mo["start"], 1)
                    over = sp.value_load(start_i[0:1, NE:NE + 1])
                    with sp.If(over > C):
                        overflow_loads(sp)
                later_loads(sp)
                if True:
                    sp.wait_ge(DONE[0], DONE[1])
                    sp.dma_start(out[0].rearrange("(t p) d -> p t d", p=P), x_tok[:]).then_inc(s_out, 16)
                    sp.wait_ge(s_out, 16)

            in2 = [A["ffn_w_in_2"][l, i].rearrange("(k p) n -> p k n", p=P) for l in range(2) for i in range(2)]
            out2 = [A["ffn_w_out_2"][l, i].rearrange("(k p) d -> p k d", p=P) for l in range(2) for i in range(2)]
            ml_in = A["ml_w_in_2"][0].rearrange("(k p) n -> p k n", p=P)
            ml_out = A["ml_w_out_2"][0].rearrange("(k p) d -> p k d", p=P)
            at_in = A["at_w_in_2"][0].rearrange("(k p) n -> p k n", p=P)
            at_out = A["at_w_out_2"][0].rearrange("(k p) d -> p k d", p=P)
            f_lo = [sem(f"ffn_lo_{k}") for k in "gud"]
            f_hi = [sem(f"ffn_hi_{k}") for k in "gud"]
            f_mm = [sem(f"ffn_mm_{k}") for k in "gud"]
            f_silu, f_h, f_hhi, f_hlo = sem("ffn_silu"), sem("ffn_h"), sem("ffn_hhi"), sem("ffn_hlo")
            mx_tr, mx_act, mx_dve, mx_used = sem("mix_turned"), sem("mix_act"), sem("mix_dve"), sem("mix_used")
            ml = {n: sem("ml_" + n) for n in ("gp", "af", "l", "logf", "cum", "diag", "q", "k", "v", "o", "qs", "ks", "vs",
                                              "os", "b", "mask", "s", "nm", "exp", "p", "tr", "pt", "h", "h3", "ve", "rs",
                                              "y", "param", "exp0")}
            at = {n: sem("at_" + n) for n in ("k", "v", "q", "ka", "kd", "vd", "qa", "qd", "s", "nm", "p", "tr", "pt", "o",
                                              "ds", "sum", "oe", "iota")}
            FIRST = UA + UM
            units = []
            at_unit = {}

            def add_ffn(f):
                at_unit["f", f] = FIRST + len(units)
                order = [(0, 0), (1, 0)]
                for s_ in range(NSTEP - 1):
                    order += [(0, s_ + 1), (1, s_ + 1), (2, s_)]
                order += [(2, NSTEP - 1)]
                for kind, s_ in order:
                    at_unit["f", f, kind, s_] = FIRST + len(units)
                    if kind < 2:
                        src, k = in2[f][:, :, kind * FF + s_ * FSTEP:kind * FF + (s_ + 1) * FSTEP], KT
                    else:
                        src, k = out2[f][:, 2 * s_:2 * s_ + 2, :], 2
                    units.append((k, src, (f_lo[kind], NSTEP * f + s_ + 1)))

            def add_columns(name, w, c, used, n):
                for j in range(2):
                    at_unit[name, n + j] = FIRST + len(units)
                    units.append((4, w[:, 4 * j:4 * j + 4, c * 512:(c + 1) * 512], used))
                return n + 2

            def add_rows(name, w, m, n, L):
                for j in range(4):
                    at_unit[name, n + j] = FIRST + len(units)
                    units.append((2, w[:, 2 * j:2 * j + 2, :], (mx_used, 3 * m + j + 1) if j < 3 else (G["ln_in"], 2 * L + 2)))

            add_ffn(0)
            n_ = 0
            for c_, used_ in enumerate(((ml["q"], 2), (ml["k"], 2), (ml["v"], 2), (ml["v"], 4), (ml["o"], 2), (ml["o"], 4))):
                n_ = add_columns("ml", ml_in, c_, used_, n_)
            add_rows("ml", ml_out, 0, n_, 3)
            add_ffn(1)
            add_ffn(2)
            n_ = 0
            for c_, used_ in ((2, (at["v"], 1)), (0, (at["q"], 2)), (1, (at["q"], 4))):
                n_ = add_columns("at", at_in, c_, used_, n_)
            add_rows("at", at_out, 1, n_, 6)
            add_ffn(3)

            def unit_used(n):
                if n < FIRST:
                    e, j = (n - UA) // 6, (n - UA) % 6
                    return (mo["ha"] if j < 2 else mo["hb"] if j < 4 else mo["y"]), e + 1
                return units[n - FIRST][2]

            def later_loads(sp):
                last = {3: at_unit["f", 0] + 33, 4: at_unit["f", 1], 5: at_unit["f", 2], 6: at_unit["f", 2] + 33,
                        7: at_unit["f", 3], 99: FIRST + len(units)}.get(stages, FIRST)
                for n in range(FIRST, last):
                    k, src, _ = units[n - FIRST]
                    sp.wait_ge(*unit_used(n - RING))
                    sp.dma_start(unit_view(n, k), src).then_inc(landed[n % RING], 16)

            def here(eng, n):
                eng.wait_ge(landed[n % RING], 16 * (n // RING + 1))

            DONE = [G["ln_tok"], 2 * min(stages, N_LN)]
            ov = {n: sem("ov_" + n) for n in ("load", "xe", "h", "silu", "hm", "tr", "hT", "y", "ysb", "sel", "comb")}

            def each_overflow(eng):
                with eng.Fori(1, BLOCKS) as b:
                    with eng.Fori(0, NE) as e:
                        yield (b - 1) * NE + e, b, e

            def overflow_loads(sp):
                sp.wait_ge(mo["y"], NE)
                for n, b, e in each_overflow(sp):
                    sp.wait_ge(ov["y"], n + 1)
                    for j in range(6):
                        w = (w1, w3)[j % 2] if j < 4 else w2
                        k0, kn = (4 * (j // 2), 4) if j < 4 else (2 * (j - 4), 2)
                        src = w[bass.ds(e, 1), :, k0:k0 + kn, :].rearrange("e p k f -> (e p) k f")
                        sp.dma_start(unit_view(j, kn), src).then_inc(ov["load"], 16)

            def pool_program(pool):
                own = Own(pool, own_pool)
                for m, v in ((ident, 0.0), (upper, 1.0), (lower, 1.0), (strict, 1.0)):
                    own.then(nc.gpsimd.memset(m[:], v))
                pool_last = own.did(nc.gpsimd.memset(neg_half[:], -0.5))
                nc.gpsimd.memset(ones[:], 1.0).then_inc(consts, 1)
                nc.gpsimd.affine_select(out=ident[:], in_=ident[:], compare_op=ALU.not_equal, fill=1.0, base=0,
                                        pattern=[[-1, P]], channel_multiplier=1).then_inc(consts, 1)
                nc.gpsimd.affine_select(out=upper[:], in_=upper[:], compare_op=ALU.is_ge, fill=0.0, base=0,
                                        pattern=[[1, P]], channel_multiplier=-1).then_inc(consts, 1)
                nc.gpsimd.affine_select(out=lower[:], in_=lower[:], compare_op=ALU.is_ge, fill=0.0, base=0,
                                        pattern=[[-1, P]], channel_multiplier=1).then_inc(consts, 1)
                nc.gpsimd.affine_select(out=strict[:], in_=strict[:], compare_op=ALU.is_gt, fill=0.0, base=0,
                                        pattern=[[1, P]], channel_multiplier=-1).then_inc(consts, 1)
                nc.gpsimd.iota(iota_s[:], pattern=[[1, SLOTS]], base=0, channel_multiplier=0,
                               allow_small_or_imprecise_dtypes=True).then_inc(consts, 1)
                for j in range(2):
                    pool.wait_ge(consts, 6 + j)
                    nc.gpsimd.iota(slot_p[64 * j:64 * j + 64, :], pattern=[[0, 1]], base=0, channel_multiplier=1,
                                   allow_small_or_imprecise_dtypes=True).then_inc(consts, 1)
                pool.wait_ge(consts, 8)
                nc.gpsimd.iota(i_8m, pattern=[[1, EPG]], base=-64, channel_multiplier=0,
                               allow_small_or_imprecise_dtypes=True).then_inc(consts, 1)
                pool.dma_start(misc_raw[0:64, :], A["rec_conv_w"][0].rearrange("k (n p) -> (k n) p", p=BW)).then_inc(s_misc, 16)
                for j, name in enumerate(("rec_conv_b", "rec_b_r", "rec_b_i", "rec_lambda")):
                    pool.dma_start(misc_raw[64 + 16 * j:80 + 16 * j, :], A[name][0].rearrange("(n p) -> n p", p=BW)).then_inc(s_misc, 16)
                pool.dma_start(wri[:, 0], A["rec_w_r"][0].rearrange("n k j -> k n j")).then_inc(s_wri, 16)
                pool.dma_start(wri[:, 1], A["rec_w_i"][0].rearrange("n k j -> k n j")).then_inc(s_wri, 16)
                for j, (name, rows) in enumerate((("ln_g", 2), ("ln_g_2", 6), ("ln_b", 2), ("ln_b_2", 6))):
                    at = (0, 16, 64, 80)[j]
                    src = A[name][0] if rows == 2 else A[name].rearrange("l s d -> (l s) d")
                    pool.dma_start(gb_raw[at:at + 8 * rows, :], src.rearrange("s (k p) -> (s k) p", p=P)).then_inc(s_misc, 16)
                pool.dma_start(ng_raw[:], A["ml_norm_g_2"][0].rearrange("(k p) -> k p", p=P)).then_inc(s_misc, 16)
                pool.dma_start(route_w[:, :, 0:NG], A["moe_w_group"][0].rearrange("(k p) n -> p k n", p=P)).then_inc(s_route, 16)
                pool.dma_start(route_w[:, :, NG:], A["moe_w_expert"][0].rearrange("(k p) n -> p k n", p=P)).then_inc(s_route, 16)
                pool.dma_start(route_b[:, 0:NG], A["moe_b_group"][0:1, :].partition_broadcast(P) if False else A["moe_b_group"].broadcast_to((P, NG))).then_inc(s_route, 16)
                pool.dma_start(route_b[:, NG:], A["moe_b_expert"].broadcast_to((P, NE))).then_inc(s_route, 16)
                pool.dma_start(gate_w[:], A["ml_w_in_2"][0].rearrange("(k p) n -> p k n", p=P)[:, :, 3072:3088]).then_inc(ml["param"], 16)
                pool.dma_start(gate_b[:], A["ml_gate_b_2"].broadcast_to((P, 16))).then_inc(ml["param"], 16)
                pool.dma_start(sink[:], A["at_sink_2"].broadcast_to((P, NH))).then_inc(ml["param"], 16)
                norm_pool(pool, own, 0, after=("moe", stages >= 2))
                if stages >= 2:
                    moe_pool(pool, own)
                    norm_pool(pool, own, 1)
                for L in range(2, min(stages, N_LN)):
                    norm_pool(pool, own, L)
                    if L == 2 and stages >= 4:
                        ml_pool(pool, own)
                    if L == 5 and stages >= 7:
                        at_pool(pool, own)

            def norm_pool(pool, own, L, after=None):
                g_src, b_src, s = (A["ln_g"], A["ln_b"], L) if L < 2 else (A["ln_g_2"], A["ln_b_2"], L - 2)
                gs = g_src.rearrange("l s d -> (l s) d")[s:s + 1, :]
                bs = b_src.rearrange("l s d -> (l s) d")[s:s + 1, :]
                pool.dma_start(gb_row[:, 0, :], gs.broadcast_to((P, D))).then_inc(s_gbrow, 16)
                pool.dma_start(gb_row[:, 1, :], bs.broadcast_to((P, D))).then_inc(s_gbrow, 16)
                for t in range(TT):
                    pool.wait_ge(G["ln_var"], 2 * L + t + 1)
                    nc.gpsimd.tensor_tensor(rstd[:, t:t + 1], var_eps[:, t:t + 1], neg_half[:, 0:1], ALU.pow) \
                        .then_inc(G["ln_rstd"], 1)
                pool.wait_ge(s_gbrow, 32 * (L + 1))
                if L < N_LN - 1:
                    pool.wait_ge(G["ln_tr"], 4 * (L + 1))
                else:
                    pool.wait_ge(G["ln_hat"], 2 * (L + 1))
                if after and after[1]:
                    pool.wait_ge(mo["gath"], KT)
                for t in range(TT):
                    own.then(nc.gpsimd.tensor_tensor(x_tok[:, t, :], x_tok[:, t, :], gb_row[:, 0, :], ALU.mult))
                    nc.gpsimd.tensor_tensor(x_tok[:, t, :], x_tok[:, t, :], gb_row[:, 1, :], ALU.add).then_inc(G["ln_tok"], 1)
                pool.wait_ge(G["ln_tok"], 2 * (L + 1))

            def norm_dve(dve, own, L, alpha, from_psum=True):
                for t in range(TT):
                    if from_psum:
                        dve.wait_ge(G["ln_in"], 2 * L + t + 1)
                        if L > 0 and t == 0:
                            dve.wait_ge(G["ln_tok"], 2 * L)
                        for hf in range(2):
                            v = x_tok[:, t, hf * HALF:(hf + 1) * HALF]
                            own.then(nc.vector.scalar_tensor_tensor(out=v, in0=v, scalar=alpha, in1=bank[2 * t + hf][:],
                                                                    op0=ALU.mult, op1=ALU.add))
                    for hf in range(2):
                        own.then(nc.vector.bn_stats(stats[:, t, hf, :], x_tok[:, t, hf * HALF:(hf + 1) * HALF]))
                    own.then(nc.vector.bn_aggr(mean_var[:, t, :], stats[:, t, :, :].rearrange("p a b -> p (a b)")))
                    nc.vector.tensor_scalar(var_eps[:, t:t + 1], mean_var[:, t, 1:2], EPS, None, ALU.add).then_inc(G["ln_var"], 1)
                for t in range(TT):
                    dve.wait_ge(G["ln_rstd"], 2 * L + t + 1)
                    nc.vector.tensor_scalar(x_tok[:, t, :], x_tok[:, t, :], mean_var[:, t, 0:1], rstd[:, t:t + 1],
                                            ALU.subtract, ALU.mult).then_inc(G["ln_hat"], 1)
                if L < N_LN - 1:
                    norm_evac_dve(dve, L)

            def norm_evac_dve(dve, L):
                for b in (1, 3):
                    dve.wait_ge(G["ln_tr"], 4 * L + b + 1)
                    for k in (2 * b, 2 * b + 1):
                        i = nc.vector.tensor_scalar(xT[:, k, :], bank[4 + b][:, (k % 2) * T:(k % 2) * T + T],
                                                    gbT[:, 8 * L + k:8 * L + k + 1],
                                                    gbT[:, 64 + 8 * L + k:64 + 8 * L + k + 1], ALU.mult, ALU.add)
                    i.then_inc(G["ln_evac_dve"], 1)
                if L in SPLIT_NORMS:
                    n = SPLIT_NORMS.index(L)
                    for b in range(4):
                        dve.wait_ge(G["ln_hi"], 4 * n + b + 1)
                        nc.vector.tensor_tensor(x_lo[:, 2 * b:2 * b + 2, :], xT[:, 2 * b:2 * b + 2, :],
                                                x_hi[:, 2 * b:2 * b + 2, :].bitcast(F32), ALU.subtract).then_inc(G["ln_lo"], 1)

            def norm_evac_act(act, L):
                for b in (0, 2):
                    act.wait_ge(G["ln_tr"], 4 * L + b + 1)
                    for k in (2 * b, 2 * b + 1):
                        i = nc.scalar.activation(xT[:, k, :], bank[4 + b][:, (k % 2) * T:(k % 2) * T + T], ACT.Identity,
                                                 scale=gbT[:, 8 * L + k:8 * L + k + 1],
                                                 bias=gbT[:, 64 + 8 * L + k:64 + 8 * L + k + 1])
                    i.then_inc(G["ln_evac_act"], 1)
                if L in SPLIT_NORMS:
                    for b in range(4):
                        s = G["ln_evac_dve"] if b % 2 else G["ln_evac_act"]
                        act.wait_ge(s, 2 * L + b // 2 + 1)
                        nc.scalar.activation(x_hi[:, 2 * b:2 * b + 2, :], xT[:, 2 * b:2 * b + 2, :], ACT.Copy).then_inc(G["ln_hi"], 1)

            def norm_pe(pe, L):
                for t in range(TT):
                    pe.wait_ge(G["ln_hat"], 2 * L + t + 1)
                    for k in range(KT):
                        i = nc.tensor.transpose(bank[4 + k // 2][:, (k % 2) * T + t * P:(k % 2) * T + t * P + P],
                                                x_tok[:, t, k * P:(k + 1) * P], ident[:])
                        if t == TT - 1 and k % 2:
                            i.then_inc(G["ln_tr"], 1)

            def xT_ready(pe, L):
                pe.wait_ge(G["ln_evac_act"], 2 * (L + 1))
                pe.wait_ge(G["ln_evac_dve"], 2 * (L + 1))

            wri = x_parts[0:BW, 0:2 * NB * BW].rearrange("p (g n j) -> p g n j", g=2, n=NB)
            s_wri = sem("s_wri")
            s_par, s_parT, s_xT0, s_xT0b = sem("s_par"), sem("s_parT"), sem("s_xT0"), sem("s_xT0b")
            GCH = ((0, 512), (512, 768))

            def keep_warm(pe, b, n):
                for i in range(n):
                    nc.tensor.matmul(bank[b][:, 0:T], ident[:], xT[:, 0, :], start=True, stop=True)

            def rec_pe(pe):
                pe.wait_ge(s_x, 16)
                pe.wait_ge(consts, 9)
                for k in range(KT):
                    for t in range(TT):
                        i = nc.tensor.transpose(bank[k // 2][:, (k % 2) * T + t * P:(k % 2) * T + t * P + P],
                                                x_tok[:, t, k * P:(k + 1) * P], ident[:])
                    if k % 2:
                        i.then_inc(s_xT0, 1)
                pe.wait_ge(s_xT0b, 4)
                for g in range(GROUPS):
                    pe.wait_ge(landed[g % RING], 16)
                    if g == 4:
                        pe.wait_ge(s_misc, 16 * 10)
                        nc.tensor.transpose(bank[4][0:BW, 0:P], misc_raw[:], ident[:])
                        nc.tensor.transpose(bank[5][:, 0:P], gb_raw[:], ident[:])
                        nc.tensor.transpose(bank[6][:, 0:KT], ng_raw[:], ident[0:KT, 0:KT]).then_inc(s_par, 1)
                    if g >= 2:
                        pe.wait_ge(r["gelu"], g - 1)
                    w = unit(g)[:, 0:KT * 2 * BW].rearrange("p (k n) -> p k n", k=KT)
                    for b in range(2):
                        for k in range(KT):
                            i = nc.tensor.matmul(bank[g % 2][0:BW, b * T:(b + 1) * T], w[:, k, b * BW:(b + 1) * BW],
                                                 xT[:, k, :], start=(k == 0), stop=(k == KT - 1))
                    i.then_inc(recA_used, 1)
                def gates_of(q):
                    if q == 0:
                        pe.wait_ge(s_wri, 32)
                        pe.wait_ge(s_parT, 2)
                    pe.wait_ge(r["conv"], q + 1)
                    if q >= 2:
                        pe.wait_ge(r["tanh"], 2 * (q - 1))
                    for gate in range(2):
                        for b in range(2):
                            i = nc.tensor.matmul(bank[4 + 2 * gate + q % 2][0:BW, b * T:(b + 1) * T],
                                                 wri[:, gate, 2 * q + b, :], xc[q % 2][:, b, :], start=True, stop=True)
                        i.then_inc(r["ri_mm"], 1)

                def project(g):
                    n = 2 * GROUPS + g
                    pe.wait_ge(landed[n % RING], 16 * (n // RING + 1))
                    pe.wait_ge(r["y"], g + 1)
                    w = unit_view(n, 2)[0:BW]
                    for b in range(2):
                        for t in range(TT):
                            for hf in range(2):
                                i = nc.tensor.matmul(bank[2 * t + hf][:], gelu[:, 2 * g + b, t * P:(t + 1) * P],
                                                     w[:, b, hf * HALF:(hf + 1) * HALF],
                                                     start=(g == 0 and b == 0), stop=(g == GROUPS - 1 and b == 1))
                            if g == GROUPS - 1 and b == 1:
                                i.then_inc(G["ln_in"], 1)
                    if g < GROUPS - 1:
                        i.then_inc(recA_used, 1)

                for g in range(GROUPS):
                    if g < GROUPS:
                        n = GROUPS + g
                        pe.wait_ge(landed[n % RING], 16 * (n // RING + 1))
                        if g >= 2:
                            pe.wait_ge(r["x_sb"], g - 1)
                        else:
                            pe.wait_ge(r["gelu"], GROUPS - 1 + g)
                        w = unit(n)[:, 0:KT * 2 * BW].rearrange("p (k n) -> p k n", k=KT)
                        for b in range(2):
                            for k in range(KT):
                                i = nc.tensor.matmul(bank[g % 2][0:BW, b * T:(b + 1) * T], w[:, k, b * BW:(b + 1) * BW],
                                                     xT[:, k, :], start=(k == 0), stop=(k == KT - 1))
                        i.then_inc(recA_used, 1)
                    if 1 <= g < GROUPS:
                        gates_of(g - 1)

                pe.wait_ge(r["x_sb"], GROUPS)
                keep_warm(pe, 7, 12)
                for g in range(GROUPS // 2):
                    project(g)
                gates_of(GROUPS - 1)
                pe.wait_ge(r["tanh"], 2 * GROUPS - 1)
                keep_warm(pe, 4, 12)
                for g in range(GROUPS // 2, GROUPS):
                    project(g)

            def rec_act(act):
                for b in (0, 2):
                    act.wait_ge(s_xT0, b + 1)
                    nc.scalar.activation(xT[:, 2 * b:2 * b + 2, :], bank[b][:].rearrange("p (a t) -> p a t", a=2), ACT.Copy).then_inc(s_xT0b, 1)
                for g in range(GROUPS):
                    act.wait_ge(recA_used, g + 1)
                    nc.scalar.activation(gelu[:, 2 * g:2 * g + 2, :], bank[g % 2][0:BW, :].rearrange("p (b t) -> p b t", b=2),
                                         ACT.Gelu_apprx_tanh).then_inc(r["gelu"], 1)
                act.wait_ge(r["const"], 1)
                nc.scalar.activation(lam_q[:, 1, :], lam_q[:, 0, :], ACT.Exp, scale=-1.0).then_inc(r["q"], 1)
                for g in range(GROUPS + 1):
                    if g < GROUPS:
                        act.wait_ge(recA_used, GROUPS + g + 1)
                        if g >= 2:
                            act.wait_ge(r["conv"], g - 1)
                        if g == 0:
                            act.wait_ge(r["const"], 2)
                        nc.scalar.activation(xp[g % 2][:, :, CONV - 1:], bank[g % 2][0:BW, :].rearrange("p (b t) -> p b t", b=2),
                                             ACT.Copy).then_inc(r["x_sb"], 1)
                    if g >= 1:
                        q = g - 1
                        if q >= 2:
                            act.wait_ge(r["y"], q - 1)
                        if q == 0:
                            act.wait_ge(r["const"], 3)
                        for gate, th in ((0, th_r), (1, th_i)):
                            act.wait_ge(r["ri_mm"], 2 * q + gate + 1)
                            for b in range(2):
                                nb = 2 * q + b
                                i = nc.scalar.activation(th[q % 2][:, b, :], bank[4 + 2 * gate + q % 2][0:BW, b * T:(b + 1) * T],
                                                         ACT.Tanh, scale=0.5, bias=lam_q[:, 10 + gate, nb:nb + 1])
                            i.then_inc(r["tanh"], 1)
                        act.wait_ge(r["tanh"], 2 * q + 1)
                        for b in range(2):
                            nb = 2 * q + b
                            i = nc.scalar.activation(th_r[q % 2][:, b, :], th_r[q % 2][:, b, :], ACT.Tanh,
                                                     scale=lam_q[:, 9, nb:nb + 1], bias=lam_q[:, 9, nb:nb + 1])
                        i.then_inc(r["t"], 1)
                        act.wait_ge(r["t"], q + 1)
                        nc.scalar.activation(root[q % 2], th_r[q % 2], ACT.Sqrt).then_inc(r["sqrt"], 1)

            def rec_dve(dve, own):
                for b in (1, 3):
                    dve.wait_ge(s_xT0, b + 1)
                    nc.vector.tensor_copy(xT[:, 2 * b:2 * b + 2, :], bank[b][:].rearrange("p (a t) -> p a t", a=2)).then_inc(s_xT0b, 1)
                dve.wait_ge(s_par, 1)
                own.then(nc.vector.tensor_copy(misc[:], bank[4][0:BW, 0:P]))
                nc.vector.tensor_copy(gbT[:], bank[5][:, 0:P]).then_inc(s_parT, 1)
                nc.vector.tensor_copy(ngT[:], bank[6][:, 0:KT]).then_inc(s_parT, 1)
                lam = misc[:, 112:128]
                own.then(nc.vector.tensor_scalar(lam_q[:, 2, :], lam, -1.0, 0.0, ALU.mult, ALU.max))
                own.then(nc.vector.tensor_scalar(lam_q[:, 3, :], lam, 0.0, None, ALU.max))
                nc.vector.tensor_tensor(lam_q[:, 0, :], lam_q[:, 2, :], lam_q[:, 3, :], ALU.add).then_inc(r["const"], 1)
                for g in range(2):
                    i = nc.vector.memset(xp[g][:, :, 0:CONV - 1], 0.0)
                i.then_inc(r["const"], 1)
                own.then(nc.vector.tensor_scalar(lam_q[:, 10, :], misc[:, 80:96], 0.5, None, ALU.mult))
                own.then(nc.vector.tensor_scalar(lam_q[:, 11, :], misc[:, 96:112], 0.5, None, ALU.mult))
                dve.wait_ge(r["q"], 1)
                e = lam_q[:, 1, :]
                own.then(nc.vector.tensor_scalar(lam_q[:, 4, :], e, 2.0, None, ALU.add))
                own.then(nc.vector.reciprocal(lam_q[:, 5, :], lam_q[:, 4, :]))
                own.then(nc.vector.tensor_tensor(lam_q[:, 6, :], e, lam_q[:, 5, :], ALU.mult))
                own.then(nc.vector.tensor_tensor(lam_q[:, 7, :], lam_q[:, 6, :], lam_q[:, 6, :], ALU.mult))
                own.then(nc.vector.tensor_scalar(lam_q[:, 8, :], lam_q[:, 7, :], 1.0 / 17, 1.0 / 15, ALU.mult, ALU.add))
                for c in (13, 11, 9, 7, 5, 3, 1):
                    own.then(nc.vector.tensor_tensor(lam_q[:, 8, :], lam_q[:, 8, :], lam_q[:, 7, :], ALU.mult))
                    own.then(nc.vector.tensor_scalar(lam_q[:, 8, :], lam_q[:, 8, :], 1.0 / c, None, ALU.add))
                own.then(nc.vector.tensor_tensor(lam_q[:, 8, :], lam_q[:, 8, :], lam_q[:, 6, :], ALU.mult))
                own.then(nc.vector.scalar_tensor_tensor(out=lam_q[:, 9, :], in0=lam_q[:, 8, :], scalar=2.0, in1=lam_q[:, 2, :],
                                                        op0=ALU.mult, op1=ALU.add))
                nc.vector.tensor_scalar(lam_q[:, 9, :], lam_q[:, 9, :], 2.0, None, ALU.mult).then_inc(r["const"], 1)
                for g in range(GROUPS + 1):
                    if g < GROUPS:
                        dve.wait_ge(r["x_sb"], g + 1)
                        if g >= 2:
                            dve.wait_ge(r["ri_mm"], 2 * (g - 1))
                        for tap in range(CONV):
                            for b in range(2):
                                nb = 2 * g + b
                                o, src = xc[g % 2][:, b, :], xp[g % 2][:, b, tap:tap + T]
                                w = misc[:, tap * NB + nb:tap * NB + nb + 1]
                                if tap == 0:
                                    i = nc.vector.tensor_scalar(o, src, w, misc[:, 64 + nb:65 + nb], ALU.mult, ALU.add)
                                else:
                                    i = nc.vector.scalar_tensor_tensor(out=o, in0=src, scalar=w, in1=o, op0=ALU.mult, op1=ALU.add)
                            if tap < CONV - 1:
                                own.then(i)
                        i.then_inc(r["conv"], 1)
                    if g >= 1:
                        q = g - 1
                        s = q % 2
                        dve.wait_ge(r["t"], q + 1)
                        own.then(nc.vector.tensor_scalar(rec_b[s], th_r[s], 1.0, None, ALU.add))
                        own.then(nc.vector.reciprocal(rec_b[s], rec_b[s]))
                        v1 = own.did(nc.vector.scalar_tensor_tensor(out=th_i[s], in0=th_i[s], scalar=1.0, in1=xc[s],
                                                                    op0=ALU.add, op1=ALU.mult))
                        dve.wait_ge(r["sqrt"], q + 1)
                        own.then(nc.vector.tensor_tensor(root[s], root[s], rec_b[s], ALU.mult))
                        own.then(nc.vector.tensor_scalar(rec_b[s], rec_b[s], 2.0, -1.0, ALU.mult, ALU.add))
                        own.then(nc.vector.tensor_tensor(root[s], root[s], th_i[s], ALU.mult))
                        for b in range(2):
                            i = nc.vector.tensor_tensor_scan(h_b[s][:, b, :], rec_b[s][:, b, :], root[s][:, b, :], 0.0,
                                                             ALU.mult, ALU.add)
                            own.did(i)
                        dve.wait_ge(own_dve, own.n)
                        nc.vector.tensor_tensor(gelu[:, 2 * q:2 * q + 2, :], h_b[s], gelu[:, 2 * q:2 * q + 2, :],
                                                ALU.mult).then_inc(r["y"], 1)

            def moe_pe(pe):
                xT_ready(pe, 0)
                pe.wait_ge(s_route, 64)
                lgp = bank[0][:, 0:128].rearrange("p (t n) -> p t n", t=TT)[:, :, 0:NG + NE]
                for t in range(TT):
                    for k in range(KT):
                        i = nc.tensor.matmul(lgp[:, t, :], xT[:, k, t * P:(t + 1) * P], route_w[:, k, :],
                                             start=(k == 0), stop=(k == KT - 1))
                i.then_inc(mo["logit"], 1)
                pe.wait_ge(mo["assign"], 1)
                rk = bank[1][:, 0:64].rearrange("p (t n) -> p t n", t=TT)
                nc.tensor.matmul(rk[:, 0, :], strict[:], A12[:, 0, :], start=True, stop=True)
                nc.tensor.matmul(rk[:, 1, :], strict[:], A12[:, 1, :], start=True, stop=False)
                nc.tensor.matmul(rk[:, 1, :], ones[:], A12[:, 0, :], start=False, stop=True)
                nc.tensor.matmul(bank[2][:, 0:NE], ones[:], A12[:, 0, :], start=True, stop=False)
                nc.tensor.matmul(bank[2][:, 0:NE], ones[:], A12[:, 1, :], start=False, stop=True).then_inc(mo["rank"], 1)
                pe.wait_ge(mo["pos"], 1)
                for k in range(KT):
                    for t in range(TT):
                        i = nc.tensor.matmul(bank[k][:], x_tok[:, t, k * P:(k + 1) * P], onehot[:, t, :],
                                             start=(t == 0), stop=(t == TT - 1))
                    i.then_inc(mo["gath"], 1)
                pe.wait_ge(mo["gath_ev"], KT)
                pe.wait_ge(mo["diag"], 1)
                for j in range(2):
                    i = nc.tensor.matmul(bank[j][:], ones[:], rows_diag[:, 2 * j:2 * j + 2].rearrange("p v t j -> p (v t j)"),
                                         start=True, stop=True)
                i.then_inc(mo["rows"], 1)
                pe.wait_ge(mo["rows_sb"], 2)
                pe.wait_ge(mo["h0"], 1)

                def hidden(e, p, count):
                    pe.wait_ge(mo["xe"], e + 1)
                    for k in range(KT):
                        for j in range(2):
                            n = 6 * p + 2 * (k // 4) + j
                            if k % 4 == 0:
                                pe.wait_ge(landed[n], count)
                            i = nc.tensor.matmul(bank[4 + p][64 * j:64 * j + 64, :], xe[p][:, k, :], unit_view(n, 4)[:, k % 4, :],
                                                 start=(k == 0), stop=(k == KT - 1))
                        if k % 4 == 3:
                            i.then_inc(mo["ha"] if k < 4 else mo["hb"], 1)

                def down(e, p, count):
                    pe.wait_ge(mo["hT"], e + 1)
                    for k in range(4):
                        n = 6 * p + 4 + k // 2
                        if k % 2 == 0:
                            pe.wait_ge(landed[n], count)
                        for j in range(2):
                            i = nc.tensor.matmul(bank[6][64 * j:64 * j + 64, :], hT_e[p][:, k, :],
                                                 unit_view(n, 2)[:, k % 2, j * HALF:(j + 1) * HALF], start=(k == 0), stop=(k == 3))
                    i.then_inc(mo["y"], 1)

                def turn(e, p):
                    pe.wait_ge(mo["h"], e + 1)
                    for k in range(4):
                        i = nc.tensor.transpose(bank[7][:, k * P:(k + 1) * P], h_e[:, k * P:(k + 1) * P], ident[:])
                    i.then_inc(mo["tr"], 1)

                def combine(e, p, first=False, last=False):
                    pe.wait_ge(mo["ysb"], e + 1)
                    pe.wait_ge(mo["sel"], e + 1)
                    for t in range(TT):
                        for j in range(2):
                            i = nc.tensor.matmul(bank[2 * t + j][:], pick_e[p][64 * j:64 * j + 64, t * P:(t + 1) * P],
                                                 y_e[p][64 * j:64 * j + 64, :], start=first, stop=last, skip_group_check=True)
                        if last:
                            i.then_inc(G["ln_in"], 1)
                    if not last:
                        i.then_inc(mo["comb"], 1)

                base = UA // RING
                for e in range(4):
                    hidden(e, e % 2, 16 * (base + 1 + e // 2))
                    if e >= 2:
                        combine(e - 2, e % 2, first=(e == 2))
                    if e:
                        down(e - 1, 1 - e % 2, 16 * (base + 1 + (e - 1) // 2))
                    turn(e, e % 2)
                with pe.Fori(2, NE // 2) as it:
                    for p in range(2):
                        hidden(2 * it + p, p, 16 * (it + base + 1))
                        combine(2 * it + p - 2, p)
                        down(2 * it + p - 1, 1 - p, 16 * (it + base + p))
                        turn(2 * it + p, p)
                combine(NE - 2, 0)
                down(NE - 1, 1, 16 * (base + NE // 2))
                over = pe.value_load(start_i[0:1, NE:NE + 1])
                with pe.If(over > C):
                    pe.sem_inc(ov["y"], 1)
                    pe.sem_inc(ov["h"], 1)
                    pe.sem_inc(ov["comb"], 1)
                    for n, b, e in each_overflow(pe):
                        pe.wait_ge(ov["xe"], n + 1)
                        pe.wait_ge(ov["load"], 96 * (n + 1))
                        for k in range(KT):
                            for j in range(2):
                                i = nc.tensor.matmul(bank[4][64 * j:64 * j + 64, :], xe[0][:, k, :],
                                                     unit_view(2 * (k // 4) + j, 4)[:, k % 4, :], start=(k == 0), stop=(k == KT - 1))
                        i.then_inc(ov["h"], 1)
                        pe.wait_ge(ov["hm"], n + 1)
                        for k in range(4):
                            i = nc.tensor.transpose(bank[7][:, k * P:(k + 1) * P], h_e[:, k * P:(k + 1) * P], ident[:])
                        i.then_inc(ov["tr"], 1)
                        pe.wait_ge(ov["hT"], n + 1)
                        for k in range(4):
                            for j in range(2):
                                i = nc.tensor.matmul(bank[6][64 * j:64 * j + 64, :], hT_e[0][:, k, :],
                                                     unit_view(4 + k // 2, 2)[:, k % 2, j * HALF:(j + 1) * HALF],
                                                     start=(k == 0), stop=(k == 3))
                        i.then_inc(ov["y"], 1)
                        pe.wait_ge(ov["ysb"], n + 1)
                        pe.wait_ge(ov["sel"], n + 1)
                        for t in range(TT):
                            for j in range(2):
                                i = nc.tensor.matmul(bank[2 * t + j][:], pick_e[0][64 * j:64 * j + 64, t * P:(t + 1) * P],
                                                     y_e[0][64 * j:64 * j + 64, :], start=False, stop=False, skip_group_check=True)
                        i.then_inc(ov["comb"], 1)
                combine(NE - 1, 1, last=True)

            def moe_dve(dve, own):
                th = own.then
                dve.wait_ge(mo["logit"], 1)
                lgp = bank[0][:, 0:128].rearrange("p (t n) -> p t n", t=TT)[:, :, 0:NG + NE]
                bc = lambda v, n: v.unsqueeze(2).broadcast_to((P, TT, n))
                for t in range(TT):
                    own.did(nc.vector.tensor_tensor(lg[:, t, :], lgp[:, t, :], route_b[:], ALU.add))
                dve.wait_ge(own_dve, own.n)
                gl = lg[:, :, 0:NG]
                el = [lg[:, t, NG:].rearrange("p (g i) -> p g i", g=NG) for t in range(TT)]
                th(nc.vector.tensor_reduce(v_gmax, gl, AX_X, ALU.max))
                for t in range(TT):
                    i = nc.vector.tensor_scalar(g_e[:, t, :], gl[:, t, :], v_gmax[:, t:t + 1], None, ALU.subtract)
                i.then_inc(mo["e1"], 1)

                def first_max(dst, values, vmax, n):
                    for t in range(TT):
                        own.did(nc.vector.scalar_tensor_tensor(out=dst[:, t, :], in0=values[:, t, :], scalar=vmax[:, t:t + 1],
                                                               in1=i_8m[:, 0:n], op0=ALU.is_ge, op1=ALU.mult))
                    dve.wait_ge(own_dve, own.n)
                    th(nc.vector.tensor_reduce(v_m, dst, AX_X, ALU.min))
                    for t in range(TT):
                        own.did(nc.vector.tensor_scalar(dst[:, t, :], dst[:, t, :], v_m[:, t:t + 1], None, ALU.is_equal))
                    dve.wait_ge(own_dve, own.n)

                first_max(g_oh, gl, v_gmax, NG)
                for t in range(TT):
                    own.did(nc.vector.tensor_tensor(tmp32[:, t], el[t], g_oh[:, t, :].unsqueeze(2).broadcast_to((P, NG, EPG)), ALU.mult))
                dve.wait_ge(own_dve, own.n)
                for t in range(TT):
                    own.did(nc.vector.tensor_reduce(e_sel[:, t, :], tmp32[:, t].rearrange("p g i -> p i g"), AX_X, ALU.add))
                dve.wait_ge(own_dve, own.n)
                th(nc.vector.tensor_reduce(v_v1, e_sel, AX_X, ALU.max))
                first_max(oh[0], e_sel, v_v1, EPG)
                th(nc.vector.scalar_tensor_tensor(out=e_c, in0=oh[0], scalar=NEG, in1=e_sel, op0=ALU.mult, op1=ALU.add))
                th(nc.vector.tensor_reduce(v_v2, e_c, AX_X, ALU.max))
                first_max(oh[1], e_c, v_v2, EPG)
                nc.vector.tensor_tensor(v_ed, v_v2, v_v1, ALU.subtract).then_inc(mo["e2"], 1)
                for kk in range(2):
                    for t in range(TT):
                        own.did(nc.vector.tensor_tensor(A1[kk][:, t], g_oh[:, t, :].unsqueeze(2).broadcast_to((P, NG, EPG)),
                                                        oh[kk][:, t, :].unsqueeze(1).broadcast_to((P, NG, EPG)), ALU.mult))
                dve.wait_ge(own_dve, own.n)
                flat = lambda v: v.rearrange("p t g i -> p (t g i)")
                a12 = A12.rearrange("p t n -> p (t n)")
                nc.vector.tensor_tensor(a12, flat(A1[0]), flat(A1[1]), ALU.add).then_inc(mo["assign"], 1)
                dve.wait_ge(mo["exp1"], 1)
                th(nc.vector.tensor_reduce(v_gsum, g_e, AX_X, ALU.add))
                th(nc.vector.reciprocal(v_ggate, v_gsum))
                dve.wait_ge(mo["exp2"], 1)
                th(nc.vector.tensor_scalar(v_p1, v_ed, 1.0, None, ALU.add))
                th(nc.vector.reciprocal(v_p1, v_p1))
                th(nc.vector.tensor_tensor(gates[0], v_p1, v_ggate, ALU.mult))
                th(nc.vector.tensor_tensor(gates[1], v_ed, gates[0], ALU.mult))
                dve.wait_ge(mo["rank"], 1)
                rk = v_rank
                own.did(nc.vector.tensor_copy(rk, bank[1][:, 0:64].rearrange("p (t n) -> p t n", t=TT)))
                th(nc.vector.tensor_tensor_scan(v_incl, ones[:, 0:NE], bank[2][:, 0:NE], 0.0, ALU.mult, ALU.add))
                th(nc.vector.tensor_tensor(v_start, v_incl, bank[2][:, 0:NE], ALU.subtract))
                own.did(nc.vector.tensor_copy(v_cnt, bank[2][:, 0:NE]))
                th(nc.vector.tensor_reduce(cmax, bank[2][:, 0:NE], AX_X, ALU.max))
                own.did(nc.vector.tensor_copy(start_i[0:1, 0:NE], v_start[0:1, :]))
                nc.vector.tensor_copy(start_i[0:1, NE:NE + 1], cmax[0:1, :]).then_inc(mo["start"], 1)
                for t in range(TT):
                    own.did(nc.vector.tensor_tensor(v_q[:, t, :], rk[:, t, :], v_start, ALU.add))
                dve.wait_ge(own_dve, own.n)
                for kk in range(2):
                    th(nc.vector.tensor_tensor(v_t, v_q, A1[kk].rearrange("p t g i -> p t (g i)"), ALU.mult))
                    th(nc.vector.tensor_reduce(v_pos[kk], v_t, AX_X, ALU.add))
                for t in range(TT):
                    th(nc.vector.tensor_scalar(onehot[:, t, :], iota_s[:], v_pos[0][:, t:t + 1], None, ALU.is_equal))
                    i = nc.vector.scalar_tensor_tensor(out=onehot[:, t, :], in0=iota_s[:], scalar=v_pos[1][:, t:t + 1],
                                                       in1=onehot[:, t, :], op0=ALU.is_equal, op1=ALU.add)
                i.then_inc(mo["pos"], 1)
                own.did(nc.vector.memset(xs[:, :, SLOTS:], 0.0))
                for k in range(1, KT, 2):
                    dve.wait_ge(mo["gath"], k + 1)
                    nc.vector.tensor_scalar(xs[:, k, 0:SLOTS], bank[k][:], gbT[:, k:k + 1], gbT[:, 64 + k:65 + k],
                                            ALU.mult, ALU.add).then_inc(mo["gath_ev"], 1)

                for v, val in enumerate((v_pos[0], v_pos[1], gates[0], gates[1])):
                    i = nc.vector.tensor_tensor(rows_diag[:, v], ident[:].unsqueeze(1).broadcast_to((P, TT, P)),
                                                val.unsqueeze(2).broadcast_to((P, TT, P)), ALU.mult)
                i.then_inc(mo["diag"], 1)
                for b in range(BLOCKS):
                    own.did(nc.vector.tensor_scalar(place[:, b, :], v_start, slot_p, float(C * b), ALU.add, ALU.add))
                    own.did(nc.vector.tensor_scalar(v_full, v_cnt, float(-C * b), slot_p, ALU.add, ALU.is_gt))
                    dve.wait_ge(own_dve, own.n)
                    th(nc.vector.scalar_tensor_tensor(out=place[:, b, :], in0=place[:, b, :], scalar=1.0, in1=v_full,
                                                      op0=ALU.add, op1=ALU.mult))
                    th(nc.vector.tensor_scalar(place[:, b, :], place[:, b, :], -1.0, None, ALU.add))
                dve.wait_ge(mo["rows"], 1)
                for j in range(2):
                    nc.vector.tensor_copy(rows_b[:, 2 * j:2 * j + 2, :], bank[j][:].rearrange("p (v t) -> p v t", v=2)) \
                        .then_inc(mo["rows_sb"], 1)
                nc.vector.memset(h_e[0:64, :], 0.0).then_inc(mo["h0"], 1)
                dve.wait_ge(mo["rows_sb"], 2)

                def select(e, p, b, s1, s):
                    at_e = place[:, b, e:e + 1] if isinstance(e, int) else place[:, b, bass.ds(e, 1)]
                    nc.vector.scalar_tensor_tensor(out=pick_e[p], in0=rows_b[:, 0, :], scalar=at_e, in1=rows_b[:, 2, :],
                                                   op0=ALU.is_equal, op1=ALU.mult).then_inc(s1, 1)
                    nc.vector.scalar_tensor_tensor(out=sel_tmp, in0=rows_b[:, 1, :], scalar=at_e, in1=rows_b[:, 3, :],
                                                   op0=ALU.is_equal, op1=ALU.mult).then_inc(s1, 1)

                def select_sum(p, s):
                    nc.vector.tensor_tensor(pick_e[p], pick_e[p], sel_tmp, ALU.add).then_inc(s, 1)

                def expert(e, p, first=False):
                    if not first:
                        dve.wait_ge(mo["comb"], e - 1)
                    select(e, p, 0, own_sel, None)
                    dve.wait_ge(own_sel, 2 * e + 2)
                    select_sum(p, mo["sel"])
                    dve.wait_ge(mo["silu"], e + 1)
                    nc.vector.tensor_tensor(h_e[64:128, :], sil_e[64:128, :], bank[4 + p][64:128, :], ALU.mult).then_inc(mo["h"], 1)
                    dve.wait_ge(mo["tr"], e + 1)
                    nc.vector.tensor_copy(hT_e[p], bank[7][:].rearrange("p (k c) -> p k c", k=4)[:, :, C:]).then_inc(mo["hT"], 1)

                expert(0, 0, True)
                expert(1, 1, True)
                with dve.Fori(1, NE // 2) as it:
                    for p in range(2):
                        expert(2 * it + p, p)
                over = dve.value_load(start_i[0:1, NE:NE + 1])
                with dve.If(over > C):
                    dve.wait_ge(mo["comb"], NE - 1)
                    for n, b, e in each_overflow(dve):
                        dve.wait_ge(ov["comb"], n + 1)
                        at_b = place.rearrange("p b e -> p (b e)")[:, bass.ds(n + NE, 1)]
                        nc.vector.scalar_tensor_tensor(out=pick_e[0], in0=rows_b[:, 0, :], scalar=at_b, in1=rows_b[:, 2, :],
                                                       op0=ALU.is_equal, op1=ALU.mult).then_inc(own_sel, 1)
                        nc.vector.scalar_tensor_tensor(out=sel_tmp, in0=rows_b[:, 1, :], scalar=at_b, in1=rows_b[:, 3, :],
                                                       op0=ALU.is_equal, op1=ALU.mult).then_inc(own_sel, 1)
                        dve.wait_ge(own_sel, 2 * NE + 2 * n + 2)
                        select_sum(0, ov["sel"])
                        dve.wait_ge(ov["silu"], n + 1)
                        nc.vector.tensor_tensor(h_e[64:128, :], sil_e[64:128, :], bank[4][64:128, :], ALU.mult).then_inc(ov["hm"], 1)
                        dve.wait_ge(ov["tr"], n + 1)
                        nc.vector.tensor_copy(hT_e[0], bank[7][:].rearrange("p (k c) -> p k c", k=4)[:, :, C:]).then_inc(ov["hT"], 1)
                if stages >= 3:
                    ffn_first_dve(dve, 0)

            def moe_act(act):
                act.wait_ge(mo["e1"], 1)
                nc.scalar.activation(g_e, g_e, ACT.Exp).then_inc(mo["exp1"], 1)
                act.wait_ge(mo["e2"], 1)
                nc.scalar.activation(v_ed, v_ed, ACT.Exp).then_inc(mo["exp2"], 1)
                for k in range(0, KT, 2):
                    act.wait_ge(mo["gath"], k + 1)
                    nc.scalar.activation(xs[:, k, 0:SLOTS], bank[k][:], ACT.Identity, scale=gbT[:, k:k + 1],
                                         bias=gbT[:, 64 + k:65 + k]).then_inc(mo["gath_ev"], 1)

                def gate(e, p):
                    act.wait_ge(mo["hb"], e + 1)
                    nc.scalar.activation(sil_e[64:128, :], bank[4 + p][0:64, :], ACT.Silu).then_inc(mo["silu"], 1)

                def keep(e, p, first=False):
                    act.wait_ge(mo["y"], e + 1)
                    if not first:
                        act.wait_ge(mo["comb"], e - 1)
                    nc.scalar.activation(y_e[p], bank[6][:], ACT.Copy).then_inc(mo["ysb"], 1)

                gate(0, 0)
                gate(1, 1)
                keep(0, 0, True)
                gate(2, 0)
                keep(1, 1, True)
                gate(3, 1)
                keep(2, 0)
                with act.Fori(2, NE // 2) as it:
                    for p in range(2):
                        gate(2 * it + p, p)
                        keep(2 * it + p - 1, 1 - p)
                keep(NE - 1, 1)
                over = act.value_load(start_i[0:1, NE:NE + 1])
                with act.If(over > C):
                    act.wait_ge(mo["comb"], NE - 1)
                    for n, b, e in each_overflow(act):
                        act.wait_ge(ov["h"], n + 2)
                        nc.scalar.activation(sil_e[64:128, :], bank[4][0:64, :], ACT.Silu).then_inc(ov["silu"], 1)
                        act.wait_ge(ov["y"], n + 2)
                        act.wait_ge(ov["comb"], n + 1)
                        nc.scalar.activation(y_e[0], bank[6][:], ACT.Copy).then_inc(ov["ysb"], 1)

            def moe_pool(pool, own):
                pool.wait_ge(mo["start"], 1)
                pool.wait_ge(mo["gath_ev"], KT)

                def pick(e, p):
                    at = pool.value_load(start_i[0:1, bass.ds(e, 1)] if not isinstance(e, int) else start_i[0:1, e:e + 1],
                                         min_val=0, max_val=SLOTS)
                    nc.gpsimd.tensor_copy(xe[p], xs[:, :, bass.ds(at, C)]).then_inc(mo["xe"], 1)

                pick(0, 0)
                pick(1, 1)
                with pool.Fori(1, NE // 2) as it:
                    for p in range(2):
                        pool.wait_ge(mo["hb"], 2 * it + p - 1)
                        pick(2 * it + p, p)
                over = pool.value_load(start_i[0:1, NE:NE + 1])
                with pool.If(over > C):
                    pool.wait_ge(mo["hb"], NE)
                    for n, b, e in each_overflow(pool):
                        pool.wait_ge(ov["h"], n + 1)
                        at = pool.value_load(start_i[0:1, bass.ds(e, 1)], min_val=0, max_val=SLOTS)
                        nc.gpsimd.tensor_copy(xe[0], xs[:, :, bass.ds(at + C * b, C)]).then_inc(ov["xe"], 1)

            pairs = ((0, 0), (0, 1), (1, 0))
            xp_ = (x_hi, x_lo)
            hp_ = (h_hi, h_lo)

            def split_act(act, f, kind, s_):
                n = at_unit["f", f, kind, s_]
                here(act, n)
                if NSTEP * f + s_ > 0:
                    act.wait_ge(f_mm[kind], NSTEP * f + s_)
                nc.scalar.activation(split[kind][0][:], unit(n), ACT.Copy).then_inc(f_hi[kind], 1)

            def split_dve(dve, f, kind, s_):
                n = at_unit["f", f, kind, s_]
                dve.wait_ge(f_hi[kind], NSTEP * f + s_ + 1)
                nc.vector.tensor_tensor(split[kind][1][:], unit(n), split[kind][0][:].bitcast(F32), ALU.subtract) \
                    .then_inc(f_lo[kind], 1)

            def ffn_first_act(act, f):
                split_act(act, f, 0, 0)
                split_act(act, f, 1, 0)

            def ffn_first_dve(dve, f):
                split_dve(dve, f, 0, 0)
                split_dve(dve, f, 1, 0)

            def ffn_act(act, f):
                for s_ in range(NSTEP):
                    c = NSTEP * f + s_
                    act.wait_ge(f_mm[0], c + 1)
                    if c:
                        act.wait_ge(f_h, c)
                    nc.scalar.activation(silu, bank[4 + 2 * (s_ % 2)][:].rearrange("p (a t) -> p a t", a=2),
                                         ACT.Silu).then_inc(f_silu, 1)
                    if s_ < NSTEP - 1:
                        split_act(act, f, 0, s_ + 1)
                    act.wait_ge(f_h, c + 1)
                    nc.scalar.activation(h_hi[:, s_ % 2], h_raw, ACT.Copy).then_inc(f_hhi, 1)
                    if s_ < NSTEP - 1:
                        split_act(act, f, 1, s_ + 1)
                    split_act(act, f, 2, s_)

            def ffn_dve(dve, f):
                for s_ in range(NSTEP):
                    c = NSTEP * f + s_
                    if s_ < NSTEP - 1:
                        split_dve(dve, f, 0, s_ + 1)
                    dve.wait_ge(f_silu, c + 1)
                    dve.wait_ge(f_mm[1], c + 1)
                    if c:
                        dve.wait_ge(f_hhi, c)
                        dve.wait_ge(f_hlo, c)
                    nc.vector.scalar_tensor_tensor(out=h_raw, in0=silu, scalar=0.5,
                                                   in1=bank[5 + 2 * (s_ % 2)][:].rearrange("p (a t) -> p a t", a=2),
                                                   op0=ALU.mult, op1=ALU.mult).then_inc(f_h, 1)
                    dve.wait_ge(f_hhi, c + 1)
                    nc.vector.tensor_tensor(h_lo[:, s_ % 2], h_raw, h_hi[:, s_ % 2].bitcast(F32), ALU.subtract).then_inc(f_hlo, 1)
                    if s_ < NSTEP - 1:
                        split_dve(dve, f, 1, s_ + 1)
                    split_dve(dve, f, 2, s_)

            def ffn_pe(pe, f, L):
                n_split = SPLIT_NORMS.index(L)

                def up(kind, s_, c):
                    pe.wait_ge(f_lo[kind], c + 1)
                    for m in range(2):
                        for k in range(KT):
                            if s_ == 0 and kind == 0 and m == 0 and k % 2 == 0:
                                pe.wait_ge(G["ln_lo"], 4 * n_split + k // 2 + 1)
                            for j, (a, b) in enumerate(pairs):
                                w = split[kind][a][:, k * FSTEP + m * P:k * FSTEP + (m + 1) * P]
                                i = nc.tensor.matmul(bank[4 + 2 * (s_ % 2) + kind][:, m * T:(m + 1) * T], w, xp_[b][:, k, :],
                                                     start=(k == 0 and j == 0), stop=(k == KT - 1 and j == 2))
                    i.then_inc(f_mm[kind], 1)

                def down(s_, c, first=False, last=False):
                    pe.wait_ge(f_hlo, c + 1)
                    pe.wait_ge(f_lo[2], c + 1)
                    for k in range(2):
                        for t in range(TT):
                            for j, (a, b) in enumerate(pairs):
                                for hf in range(2):
                                    w = split[2][b][:, k * D + hf * HALF:k * D + (hf + 1) * HALF]
                                    i = nc.tensor.matmul(bank[2 * t + hf][:], hp_[a][:, s_ % 2, k, t * P:(t + 1) * P], w,
                                                         start=(first and k == 0 and j == 0), stop=(last and k == 1 and j == 2))
                            if last and k == 1:
                                i.then_inc(G["ln_in"], 1)
                    if not last:
                        i.then_inc(f_mm[2], 1)

                base = NSTEP * f
                for s_ in range(3):
                    up(0, s_, base + s_)
                    up(1, s_, base + s_)
                    if s_:
                        down(s_ - 1, base + s_ - 1, first=(s_ == 1))
                with pe.Fori(0, (NSTEP - 3) // 2) as it:
                    for q in range(2):
                        c = base + 3 + 2 * it + q
                        up(0, 3 + q, c)
                        up(1, 3 + q, c)
                        down(2 + q, c - 1)
                down(NSTEP - 1, base + NSTEP - 1, last=True)
                pe.sem_inc(f_mm[2], 1)

            gate_w = sb("ml_gate_w", [P, KT, 16])
            gate_b = sb("ml_gate_b", [P, 16])
            sink = sb("at_sink", [P, NH])
            MS = sb("ml_small", [P, 192])
            mask = x_parts[:, 0:768].rearrange("p (d c) -> p d c", d=2)
            q_T = arena[:, 0:1024].rearrange("p (h t) -> p h t", h=MLH)
            k_T = arena[:, 1024:2048].rearrange("p (h t) -> p h t", h=MLH)
            v_tok = arena[:, 2048:4096].rearrange("p (t d) -> p t d", t=TT)
            o_t = arena[:, 4096:6144].rearrange("p (t d) -> p t d", t=TT)
            Wb = [arena[:, 6144 + i * 1024:7168 + i * 1024].rearrange("p (t d s) -> p t d s", t=TT, d=2) for i in range(2)]
            diag = arena[:, 6144:8192].rearrange("p (t c j) -> p t c j", t=TT, c=8)
            p_tot = [arena[:, 8192 + i * 512:8704 + i * 512].rearrange("p (t s) -> p t s", t=TT) for i in range(2)]
            p_T = [arena[:, 9216 + i * 512:9728 + i * 512].rearrange("p (s j) -> p s j", s=TT) for i in range(2)]
            y_T = arena[:, 10240:12288].rearrange("p (k t) -> p k t", k=KT)
            h_tok = xT[:].rearrange("p k t -> p (k t)").rearrange("p (t d) -> p t d", t=TT)
            B_bank = (6, 7, 0, 1)

            def ms(a, *shape):
                n = int(np.prod(shape))
                v = MS[:, a:a + n]
                return v.rearrange("p (a b) -> p a b", b=shape[1]) if len(shape) == 2 else \
                    v.rearrange("p (a b c) -> p a b c", b=shape[1], c=shape[2]) if len(shape) == 3 else v

            gp = MS[:, 0:32].rearrange("p (t d w h) -> p t d w h", t=TT, d=2, w=2)
            gp_t = ms(0, TT, 16)
            af, lg1, logf = ms(32, TT, 2, MLH), ms(48, TT, 2, MLH), ms(64, TT, 2, MLH)
            gcum, b_t = ms(80, TT, 2, MLH), ms(96, TT, 2, MLH)
            mx = [ms(112 + 4 * i, TT, 2) for i in range(2)]
            n_m = [ms(120 + 4 * i, TT, 2) for i in range(2)]
            floor = [ms(128 + 4 * i, TT, 2) for i in range(2)]
            den = [ms(136 + 4 * i, TT, 2) for i in range(2)]
            ng_half = MS[:, 144:152]
            mv4 = ms(152, TT, 2)
            ve4, rs4 = ms(156, TT), ms(158, TT)
            AS = sb("at_small", [P, 192])
            a_mx = AS[:, 0:4].rearrange("p (q t) -> p q t", q=2)
            a_nm = AS[:, 8:40].rearrange("p (t h) -> p t h", t=TT)
            a_sum = AS[:, 40:72].rearrange("p (t h) -> p t h", t=TT)
            a_ds = AS[:, 72:104].rearrange("p (t h) -> p t h", t=TT)
            a_rec = AS[:, 104:136].rearrange("p (t h) -> p t h", t=TT)
            a_nsink = AS[:, 136:152]

            ML_U = lambda n: at_unit["ml", n]

            def ml_pe(pe):
                xT_ready(pe, 2)
                pe.wait_ge(ml["param"], 48)
                for t in range(TT):
                    for k in range(KT):
                        i = nc.tensor.matmul(bank[0][:, t * 16:(t + 1) * 16], xT[:, k, t * P:(t + 1) * P], gate_w[:, k, :],
                                             start=(k == 0), stop=(k == KT - 1))
                i.then_inc(ml["gp"], 1)

                def heads(u0, banks, s):
                    for j in range(2):
                        here(pe, ML_U(u0 + j))
                    for h in range(MLH):
                        for k in range(KT):
                            w = unit_view(ML_U(u0 + k // 4), 4)[:, k % 4, h * P:(h + 1) * P]
                            i = nc.tensor.matmul(bank[banks[h // 2]][:, (h % 2) * T:(h % 2) * T + T], w, xT[:, k, :],
                                                 start=(k == 0), stop=(k == KT - 1))
                        if h % 2:
                            i.then_inc(s, 1)

                def rows(u0, banks, s, free):
                    for hf in range(2):
                        for j in range(2):
                            here(pe, ML_U(u0 + 2 * hf + j))
                        for t in range(TT):
                            if free and free[2 * hf + t]:
                                pe.wait_ge(*free[2 * hf + t])
                            for k in range(KT):
                                w = unit_view(ML_U(u0 + 2 * hf + k // 4), 4)[:, k % 4, :]
                                i = nc.tensor.matmul(bank[banks[2 * hf + t]][:], xT[:, k, t * P:(t + 1) * P], w,
                                                     start=(k == 0), stop=(k == KT - 1))
                            i.then_inc(s, 1)

                heads(0, (1, 2), ml["q"])
                pe.wait_ge(ml["logf"], 1)
                for d in range(2):
                    for t in range(TT):
                        o = bank[0][:, 64 + t * 8 + d * 4:68 + t * 8 + d * 4]
                        m = upper if d == 0 else lower
                        other = t != d
                        i = nc.tensor.matmul(o, m[:], logf[:, t, d, :], start=True, stop=not other)
                        if other:
                            i = nc.tensor.matmul(o, ones[:], logf[:, 1 - t, d, :], start=False, stop=True)
                i.then_inc(ml["cum"], 1)
                heads(2, (3, 4), ml["k"])
                rows(4, (5, 6, 7, 1), ml["v"], (None, None, None, (ml["qs"], 1)))
                rows(8, (2, 3, 4, 5), ml["o"], ((ml["qs"], 2), (ml["ks"], 1), (ml["ks"], 2), (ml["vs"], 1)))
                pe.wait_ge(ml["diag"], 2)
                pe.wait_ge(ml["vs"], 4)
                for h in range(MLH):
                    for d in range(2):
                        for t in range(TT):
                            i = nc.tensor.matmul(bank[B_bank[h]][:, d * T + t * P:d * T + t * P + P], ones[:],
                                                 diag[:, t, 4 * d + h, :], start=True, stop=True)
                    i.then_inc(ml["b"], 1)
                pe.wait_ge(ml["os"], 4)

                def scores(h):
                    for t in range(TT):
                        i = nc.tensor.matmul(bank[2 + h % 2][:, t * T:(t + 1) * T], q_T[:, h, t * P:(t + 1) * P], k_T[:, h, :],
                                             start=True, stop=True)
                    i.then_inc(ml["s"], 1)

                scores(0)
                for h in range(MLH):
                    if h + 1 < MLH:
                        scores(h + 1)
                    pe.wait_ge(ml["p"], h + 1)
                    for s_ in range(TT):
                        for t in range(TT):
                            i = nc.tensor.transpose(bank[4][:, s_ * T + t * P:s_ * T + t * P + P],
                                                    p_tot[h % 2][:, t, s_ * P:(s_ + 1) * P], ident[:])
                    i.then_inc(ml["tr"], 1)
                    pe.wait_ge(ml["pt"], h + 1)
                    if h:
                        pe.wait_ge(ml["h3"], h)
                    for t in range(TT):
                        for s_ in range(TT):
                            i = nc.tensor.matmul(bank[5][:, t * T:(t + 1) * T], p_T[h % 2][:, s_, t * P:(t + 1) * P],
                                                 v_tok[:, s_, h * DV:(h + 1) * DV], start=(s_ == 0), stop=(s_ == 1))
                    i.then_inc(ml["h"], 1)
                pe.wait_ge(ml["y"], MLH)
                branch_out(pe, h_tok, "ml", 12, 0)

            def branch_out(pe, rows, name, u0, m):
                for k in range(KT):
                    for t in range(TT):
                        i = nc.tensor.transpose(bank[4 + k // 2][:, (k % 2) * T + t * P:(k % 2) * T + t * P + P],
                                                rows[:, t, k * P:(k + 1) * P], ident[:])
                    if k % 2:
                        i.then_inc(mx_tr, 1)
                yT_ = y_T if name == "ml" else y_Ta
                for u in range(4):
                    here(pe, at_unit[name, u0 + u])
                    pe.wait_ge(mx_dve if u % 2 else mx_act, 2 * m + u // 2 + 1)
                    w = unit_view(at_unit[name, u0 + u], 2)
                    for k in range(2):
                        for t in range(TT):
                            for hf in range(2):
                                i = nc.tensor.matmul(bank[2 * t + hf][:], yT_[:, 2 * u + k, t * P:(t + 1) * P],
                                                     w[:, k, hf * HALF:(hf + 1) * HALF], start=(u == 0 and k == 0),
                                                     stop=(u == 3 and k == 1))
                            if u == 3 and k == 1:
                                i.then_inc(G["ln_in"], 1)
                    if u < 3:
                        i.then_inc(mx_used, 1)

            def ml_act(act):
                act.wait_ge(ml["af"], 1)
                own_l = nc.scalar.activation(lg1, af, ACT.Exp, scale=-1.0).then_inc(ml["exp0"], 1)
                act.wait_ge(ml["exp0"], 1)
                nc.scalar.activation(lg1, lg1, ACT.Ln, bias=1.0).then_inc(ml["l"], 1)
                for j in range(2):
                    act.wait_ge(ml["q"], j + 1)
                    nc.scalar.activation(q_T[:, 2 * j:2 * j + 2, :], bank[1 + j][:].rearrange("p (a t) -> p a t", a=2),
                                         ACT.Copy).then_inc(ml["qs"], 1)
                for j in range(4):
                    hf, t = j // 2, j % 2
                    act.wait_ge(ml["o"], j + 1)
                    nc.scalar.activation(o_t[:, t, hf * HALF:(hf + 1) * HALF], bank[2 + j][:], ACT.Tanh, scale=0.5).then_inc(ml["os"], 1)

                def exps(h):
                    act.wait_ge(ml["nm"], h + 1)
                    for t in range(TT):
                        for d in range(2):
                            nc.scalar.activation(Wb[h % 2][:, t, d, :], Wb[h % 2][:, t, d, :], ACT.Exp,
                                                 bias=n_m[h % 2][:, t, d:d + 1])
                    nc.scalar.activation(floor[h % 2], floor[h % 2], ACT.Exp).then_inc(ml["exp"], 1)

                exps(0)
                for h in range(MLH):
                    if h + 1 < MLH:
                        exps(h + 1)
                    act.wait_ge(ml["tr"], h + 1)
                    nc.scalar.activation(p_T[h % 2], bank[4][:].rearrange("p (s j) -> p s j", s=TT), ACT.Copy).then_inc(ml["pt"], 1)
                for b in (0, 2):
                    act.wait_ge(mx_tr, b + 1)
                    for k in (2 * b, 2 * b + 1):
                        i = nc.scalar.activation(y_T[:, k, :], bank[4 + b][:, (k % 2) * T:(k % 2) * T + T], ACT.Copy,
                                                 scale=ng_half[:, k:k + 1])
                    i.then_inc(mx_act, 1)

            def ml_dve(dve, own):
                th = own.then
                own.did(nc.vector.tensor_scalar(ng_half, ngT[:], 0.5, None, ALU.mult))
                dve.wait_ge(ml["gp"], 1)
                for t in range(TT):
                    own.did(nc.vector.tensor_tensor(gp_t[:, t, :], bank[0][:, t * 16:(t + 1) * 16], gate_b[:], ALU.add))
                dve.wait_ge(own_dve, own.n)
                for t in range(TT):
                    i = nc.vector.scalar_tensor_tensor(out=af[:, t], in0=gp[:, t, :, 1, :], scalar=-1.0, in1=gp[:, t, :, 1, :],
                                                       op0=ALU.mult, op1=ALU.max)
                i.then_inc(ml["af"], 1)
                dve.wait_ge(ml["l"], 1)
                for t in range(TT):
                    i = nc.vector.scalar_tensor_tensor(out=logf[:, t], in0=gp[:, t, :, 1, :], scalar=0.0, in1=lg1[:, t],
                                                       op0=ALU.min, op1=ALU.subtract)
                i.then_inc(ml["logf"], 1)
                dve.wait_ge(ml["cum"], 1)
                th(nc.vector.tensor_copy(gcum, bank[0][:, 64:80].rearrange("p (t d h) -> p t d h", t=TT, d=2)))
                for t in range(TT):
                    own.did(nc.vector.tensor_tensor(b_t[:, t], gp[:, t, :, 0, :], gcum[:, t], ALU.subtract))
                dve.wait_ge(own_dve, own.n)
                for t in range(TT):
                    bt = b_t[:, t].rearrange("p d h -> p (d h)")
                    nc.vector.tensor_tensor(diag[:, t], ident[:].unsqueeze(1).broadcast_to((P, 8, P)),
                                            bt.unsqueeze(2).broadcast_to((P, 8, P)), ALU.mult).then_inc(ml["diag"], 1)
                for j in range(2):
                    dve.wait_ge(ml["k"], j + 1)
                    nc.vector.tensor_copy(k_T[:, 2 * j:2 * j + 2, :], bank[3 + j][:].rearrange("p (a t) -> p a t", a=2)).then_inc(ml["ks"], 1)
                for j in range(4):
                    hf, t = j // 2, j % 2
                    dve.wait_ge(ml["v"], j + 1)
                    nc.vector.tensor_copy(v_tok[:, t, hf * HALF:(hf + 1) * HALF], bank[(5, 6, 7, 1)[j]][:]).then_inc(ml["vs"], 1)

                def weights(h):
                    q = h % 2
                    if h == 0:
                        dve.wait_ge(ml["mask"], 2)
                        dve.wait_ge(ml["b"], MLH)
                    for t in range(TT):
                        off = P * (1 - t)
                        own.did(nc.vector.tensor_tensor(Wb[q][:, t], bank[B_bank[h]][:].rearrange("p (d s) -> p d s", d=2),
                                                        mask[:, :, off:off + T], ALU.add))
                    dve.wait_ge(own_dve, own.n)
                    th(nc.vector.tensor_reduce(mx[q], Wb[q], AX_X, ALU.max))
                    own.did(nc.vector.tensor_scalar(n_m[q], mx[q], 0.0, -1.0, ALU.max, ALU.mult))
                    dve.wait_ge(own_dve, own.n)
                    nc.vector.tensor_tensor(floor[q], n_m[q], gcum[:, :, :, h], ALU.subtract).then_inc(ml["nm"], 1)

                def probs(h):
                    q = h % 2
                    dve.wait_ge(ml["exp"], h + 1)
                    dve.wait_ge(ml["s"], h + 1)
                    for t in range(TT):
                        for d in range(2):
                            w = Wb[q][:, t, d, :]
                            own.did(nc.vector.scalar_tensor_tensor(out=w, in0=bank[2 + q][:, t * T:(t + 1) * T], scalar=DQK ** -0.5,
                                                                   in1=w, op0=ALU.mult, op1=ALU.mult,
                                                                   accum_out=den[q][:, t, d:d + 1]))
                    dve.wait_ge(own_dve, own.n)
                    own.did(nc.vector.tensor_tensor(floor[q], floor[q], den[q], ALU.max))
                    dve.wait_ge(own_dve, own.n)
                    th(nc.vector.scalar_tensor_tensor(out=den[q], in0=den[q], scalar=-1.0, in1=floor[q], op0=ALU.mult, op1=ALU.max))
                    th(nc.vector.reciprocal(den[q], den[q]))
                    for t in range(TT):
                        own.did(nc.vector.tensor_scalar(p_tot[q][:, t, :], Wb[q][:, t, 0, :], den[q][:, t, 0:1], None, ALU.mult))
                    dve.wait_ge(own_dve, own.n)
                    for t in range(TT):
                        i = nc.vector.scalar_tensor_tensor(out=p_tot[q][:, t, :], in0=Wb[q][:, t, 1, :], scalar=den[q][:, t, 1:2],
                                                           in1=p_tot[q][:, t, :], op0=ALU.mult, op1=ALU.add)
                    i.then_inc(ml["p"], 1)

                def head_norm(h):
                    dve.wait_ge(ml["h"], h + 1)
                    for t in range(TT):
                        own.did(nc.vector.bn_stats(stats[:, t, 0, :], bank[5][:, t * T:(t + 1) * T]))
                    dve.wait_ge(own_dve, own.n)
                    for t in range(TT):
                        own.did(nc.vector.bn_aggr(mv4[:, t, :], stats[:, t, 0, :]))
                    dve.wait_ge(own_dve, own.n)
                    nc.vector.tensor_scalar(ve4, mv4[:, :, 1], EPS, None, ALU.add).then_inc(ml["ve"], 1)
                    dve.wait_ge(ml["rs"], h + 1)
                    for t in range(TT):
                        i = nc.vector.tensor_scalar(h_tok[:, t, h * DV:(h + 1) * DV], bank[5][:, t * T:(t + 1) * T], mv4[:, t, 0:1],
                                                    rs4[:, t:t + 1], ALU.subtract, ALU.mult)
                    i.then_inc(ml["h3"], 1)
                    dve.wait_ge(ml["h3"], h + 1)
                    for t in range(TT):
                        v = h_tok[:, t, h * DV:(h + 1) * DV]
                        i = nc.vector.scalar_tensor_tensor(out=v, in0=o_t[:, t, h * DV:(h + 1) * DV], scalar=1.0, in1=v,
                                                           op0=ALU.add, op1=ALU.mult)
                    i.then_inc(ml["y"], 1)

                weights(0)
                for h in range(MLH):
                    probs(h)
                    if h + 1 < MLH:
                        weights(h + 1)
                    head_norm(h)
                for b in (1, 3):
                    dve.wait_ge(mx_tr, b + 1)
                    for k in (2 * b, 2 * b + 1):
                        i = nc.vector.tensor_scalar(y_T[:, k, :], bank[4 + b][:, (k % 2) * T:(k % 2) * T + T], ng_half[:, k:k + 1],
                                                    None, ALU.mult)
                    i.then_inc(mx_dve, 1)

            def ml_pool(pool, own):
                own.did(nc.gpsimd.memset(mask, 0.0))
                pool.wait_ge(own_pool, own.n)
                nc.gpsimd.affine_select(out=mask[:, 0, :], in_=mask[:, 0, :], compare_op=ALU.is_ge, fill=NEG, base=P,
                                        pattern=[[-1, 3 * P]], channel_multiplier=1).then_inc(ml["mask"], 1)
                nc.gpsimd.affine_select(out=mask[:, 1, :], in_=mask[:, 1, :], compare_op=ALU.is_ge, fill=NEG, base=-P,
                                        pattern=[[1, 3 * P]], channel_multiplier=-1).then_inc(ml["mask"], 1)
                for h in range(MLH):
                    pool.wait_ge(ml["ve"], h + 1)
                    nc.gpsimd.tensor_tensor(rs4, ve4, neg_half[:, 0:TT], ALU.pow).then_inc(ml["rs"], 1)

            qa_T = arena[:, 0:2048].rearrange("p (c t) -> p c t", c=8)
            ka_T = arena[:, 2048:3072].rearrange("p (g t) -> p g t", g=NKV)
            va_t = arena[:, 3072:3584].rearrange("p (t d) -> p t d", t=TT)
            NSB = 3
            pr = [arena[:, 3584 + i * 512:4096 + i * 512].rearrange("p (t s) -> p t s", t=TT) for i in range(NSB)]
            pa_T = [arena[:, 5120 + i * 512:5632 + i * 512].rearrange("p (s j) -> p s j", s=TT) for i in range(2)]
            o_tok = arena[:, 6144:8192].rearrange("p (t d) -> p t d", t=TT)
            y_Ta = arena[:, 8192:10240].rearrange("p (k t) -> p k t", k=KT)
            dist = x_parts[:, 0:384]
            dist_far = x_parts[:, 384:768]
            AT_U = lambda n: at_unit["at", n]

            def at_pe(pe):
                xT_ready(pe, 5)
                for j in range(2):
                    here(pe, AT_U(j))
                kv = lambda k: unit_view(AT_U(k // 4), 4)[:, k % 4, :]
                for g in range(NKV):
                    for k in range(KT):
                        for j in range(2):
                            i = nc.tensor.matmul(bank[g // 2][64 * j:64 * j + 64, (g % 2) * T:(g % 2) * T + T],
                                                 kv(k)[:, g * HD:(g + 1) * HD], xT[:, k, :], start=(k == 0), stop=(k == KT - 1))
                    if g % 2:
                        i.then_inc(at["k"], 1)
                for t in range(TT):
                    for k in range(KT):
                        i = nc.tensor.matmul(bank[2][:, t * T:(t + 1) * T], xT[:, k, t * P:(t + 1) * P], kv(k)[:, 256:512],
                                             start=(k == 0), stop=(k == KT - 1))
                i.then_inc(at["v"], 1)
                for c in range(8):
                    if c % 4 == 0:
                        for j in range(2):
                            here(pe, AT_U(2 + 2 * (c // 4) + j))
                    for k in range(KT):
                        w = unit_view(AT_U(2 + 2 * (c // 4) + k // 4), 4)[:, k % 4, (c % 4) * P:(c % 4) * P + P]
                        i = nc.tensor.matmul(bank[3 + c // 2][:, (c % 2) * T:(c % 2) * T + T], w, xT[:, k, :],
                                             start=(k == 0), stop=(k == KT - 1))
                    if c % 2:
                        i.then_inc(at["q"], 1)

                def scores(h):
                    if h == 0:
                        pe.wait_ge(at["ka"], 1)
                        pe.wait_ge(at["kd"], 1)
                    c, r0, g = h // 2, (h % 2) * HD, h // 4
                    pe.wait_ge(at["qa"] if c // 2 % 2 == 0 else at["qd"], c // 4 + 1)
                    for t in range(TT):
                        i = nc.tensor.matmul(bank[h % 2][:, t * T:(t + 1) * T], qa_T[r0:r0 + HD, c, t * P:(t + 1) * P],
                                             ka_T[r0:r0 + HD, g, :], start=True, stop=True)
                    i.then_inc(at["s"], 1)

                def turn(h):
                    if h == 0:
                        pe.wait_ge(at["vd"], 1)
                        pe.wait_ge(at["qa"], 2)
                        pe.wait_ge(at["qd"], 2)
                    pe.wait_ge(at["p"], h + 1)
                    if h >= 2:
                        pe.wait_ge(at["pt"], h - 1)
                    for s_ in range(TT):
                        for t in range(TT):
                            i = nc.tensor.transpose(bank[2 + h % 2][:, s_ * T + t * P:s_ * T + t * P + P],
                                                    pr[h % NSB][:, t, s_ * P:(s_ + 1) * P], ident[:])
                    i.then_inc(at["tr"], 1)

                def mix(h):
                    g = h // 4
                    pe.wait_ge(at["pt"], h + 1)
                    if h % 4 == 0 and g >= 2:
                        pe.wait_ge(at["oe"], g - 1)
                    ob = bank[4 + g % 2][:].rearrange("p (t h d) -> p t h d", t=TT, h=4)
                    for t in range(TT):
                        for s_ in range(TT):
                            i = nc.tensor.matmul(ob[:, t, h % 4, :], pa_T[h % 2][:, s_, t * P:(t + 1) * P],
                                                 va_t[:, s_, g * HD:(g + 1) * HD], start=(s_ == 0), stop=(s_ == 1))
                    i.then_inc(at["o"], 1)

                scores(0)
                for h in range(NH):
                    if h + 1 < NH:
                        scores(h + 1)
                    turn(h)
                    if h:
                        mix(h - 1)
                mix(NH - 1)
                pe.wait_ge(at["oe"], NKV)
                branch_out(pe, o_tok, "at", 6, 1)

            def at_act(act):
                act.wait_ge(at["k"], 1)
                nc.scalar.activation(ka_T[:, 0:2, :], bank[0][:].rearrange("p (a t) -> p a t", a=2), ACT.Copy).then_inc(at["ka"], 1)
                for j in (0, 2):
                    act.wait_ge(at["q"], j + 1)
                    nc.scalar.activation(qa_T[:, 2 * j:2 * j + 2, :], bank[3 + j][:].rearrange("p (a t) -> p a t", a=2), ACT.Copy) \
                        .then_inc(at["qa"], 1)

                def evac(h):
                    act.wait_ge(at["tr"], h + 1)
                    if h >= 2:
                        act.wait_ge(at["o"], h - 1)
                    nc.scalar.activation(pa_T[h % 2], bank[2 + h % 2][:].rearrange("p (s j) -> p s j", s=TT), ACT.Copy).then_inc(at["pt"], 1)

                for h in range(NH):
                    act.wait_ge(at["nm"], h + 1)
                    for t in range(TT):
                        i = nc.scalar.activation(pr[h % NSB][:, t, :], pr[h % NSB][:, t, :], ACT.Exp, scale=HD ** -0.5,
                                                 bias=a_nm[:, t, h:h + 1], accum_out=a_sum[:, t, h:h + 1])
                    i.then_inc(at["p"], 1)
                    if h % 4 == 3:
                        act.wait_ge(at["ds"], h // 4 + 1)
                        v = a_ds[:, :, h - 3:h + 1]
                        nc.scalar.activation(v, v, ACT.Exp).then_inc(at["sum"], 1)
                    if h:
                        evac(h - 1)
                evac(NH - 1)
                for b in (0, 2):
                    act.wait_ge(mx_tr, 4 + b + 1)
                    nc.scalar.activation(y_Ta[:, 2 * b:2 * b + 2, :], bank[4 + b][:].rearrange("p (a t) -> p a t", a=2), ACT.Copy) \
                        .then_inc(mx_act, 1)

            def at_dve(dve, own):
                th = own.then
                dve.wait_ge(at["iota"], 1)
                th(nc.vector.scalar_tensor_tensor(out=dist, in0=dist, scalar=-1.0, in1=dist, op0=ALU.mult, op1=ALU.max))
                th(nc.vector.tensor_scalar(dist_far, dist, float(WINDOW), 1e30, ALU.is_gt, ALU.mult))
                own.did(nc.vector.tensor_tensor(dist, dist, dist_far, ALU.add))
                own.did(nc.vector.tensor_scalar(a_nsink, sink[:], -1.0, None, ALU.mult))
                dve.wait_ge(own_dve, own.n)
                dve.wait_ge(at["k"], 2)
                nc.vector.tensor_copy(ka_T[:, 2:4, :], bank[1][:].rearrange("p (a t) -> p a t", a=2)).then_inc(at["kd"], 1)
                dve.wait_ge(at["v"], 1)
                nc.vector.tensor_copy(va_t, bank[2][:].rearrange("p (t d) -> p t d", t=TT)).then_inc(at["vd"], 1)
                for j in (1, 3):
                    dve.wait_ge(at["q"], j + 1)
                    nc.vector.tensor_copy(qa_T[:, 2 * j:2 * j + 2, :], bank[3 + j][:].rearrange("p (a t) -> p a t", a=2)).then_inc(at["qd"], 1)

                def finish(g):
                    dve.wait_ge(at["sum"], g + 1)
                    h4 = slice(4 * g, 4 * g + 4)
                    th(nc.vector.tensor_tensor(a_rec[:, :, h4], a_sum[:, :, h4], a_ds[:, :, h4], ALU.add))
                    th(nc.vector.reciprocal(a_rec[:, :, h4], a_rec[:, :, h4]))
                    dve.wait_ge(at["o"], 4 * g + 4)
                    for t in range(TT):
                        i = nc.vector.tensor_tensor(o_tok[:, t, g * 256:(g + 1) * 256].rearrange("p (h d) -> p h d", h=4),
                                                    bank[4 + g % 2][:, t * T:(t + 1) * T].rearrange("p (h d) -> p h d", h=4),
                                                    a_rec[:, t, h4].unsqueeze(2).broadcast_to((P, 4, HD)), ALU.mult)
                    i.then_inc(at["oe"], 1)

                for h in range(NH):
                    q = h % NSB
                    slope = 2.0 ** (-8.0 * (h + 1) / NH)
                    dve.wait_ge(at["s"], h + 1)
                    if h >= NSB:
                        dve.wait_ge(at["tr"], h - NSB + 1)
                    for t in range(TT):
                        off = P * (1 - t)
                        own.did(nc.vector.scalar_tensor_tensor(out=pr[q][:, t, :], in0=dist[:, off:off + T],
                                                               scalar=-slope * HD ** 0.5, in1=bank[h % 2][:, t * T:(t + 1) * T],
                                                               op0=ALU.mult, op1=ALU.add))
                    dve.wait_ge(own_dve, own.n)
                    th(nc.vector.tensor_reduce(a_mx[:, h % 2, :], pr[q], AX_X, ALU.max))
                    nc.vector.tensor_scalar(a_nm[:, :, h], a_mx[:, h % 2, :], -HD ** -0.5, a_nsink[:, h:h + 1], ALU.mult, ALU.min) \
                        .then_inc(at["nm"], 1)
                    if h % 4 == 3:
                        h4 = slice(h - 3, h + 1)
                        dve.wait_ge(at["nm"], h + 1)
                        nc.vector.tensor_tensor(a_ds[:, :, h4], a_nm[:, :, h4], sink[:, h4].unsqueeze(1).broadcast_to((P, TT, 4)),
                                                ALU.add).then_inc(at["ds"], 1)
                    if h % 4 == 1 and h > 4:
                        finish(h // 4 - 1)
                finish(NKV - 1)
                for b in (1, 3):
                    dve.wait_ge(mx_tr, 4 + b + 1)
                    nc.vector.tensor_copy(y_Ta[:, 2 * b:2 * b + 2, :], bank[4 + b][:].rearrange("p (a t) -> p a t", a=2)).then_inc(mx_dve, 1)

            def at_pool(pool, own):
                nc.gpsimd.iota(dist, pattern=[[-1, 3 * P]], base=P, channel_multiplier=1,
                               allow_small_or_imprecise_dtypes=True).then_inc(at["iota"], 1)

            S = stages

            @block.tensor
            def _(pe):
                rec_pe(pe)
                norm_pe(pe, 0)
                if S >= 2:
                    moe_pe(pe)
                    norm_pe(pe, 1)
                if S >= 3:
                    ffn_pe(pe, 0, 1)
                    norm_pe(pe, 2)
                if S >= 4:
                    ml_pe(pe)
                    norm_pe(pe, 3)
                if S >= 5:
                    ffn_pe(pe, 1, 3)
                    norm_pe(pe, 4)
                if S >= 6:
                    ffn_pe(pe, 2, 4)
                    norm_pe(pe, 5)
                if S >= 7:
                    at_pe(pe)
                    norm_pe(pe, 6)
                if S >= 8:
                    ffn_pe(pe, 3, 6)

            @block.scalar
            def _(act):
                rec_act(act)
                norm_evac_act(act, 0)
                if S >= 2:
                    moe_act(act)
                    if S >= 3:
                        ffn_first_act(act, 0)
                    norm_evac_act(act, 1)
                if S >= 3:
                    ffn_act(act, 0)
                    norm_evac_act(act, 2)
                if S >= 4:
                    ml_act(act)
                    if S >= 5:
                        ffn_first_act(act, 1)
                    norm_evac_act(act, 3)
                if S >= 5:
                    ffn_act(act, 1)
                    if S >= 6:
                        ffn_first_act(act, 2)
                    norm_evac_act(act, 4)
                if S >= 6:
                    ffn_act(act, 2)
                    norm_evac_act(act, 5)
                if S >= 7:
                    at_act(act)
                    if S >= 8:
                        ffn_first_act(act, 3)
                    norm_evac_act(act, 6)
                if S >= 8:
                    ffn_act(act, 3)

            @block.vector
            def _(dve):
                own = Own(dve, own_dve)
                rec_dve(dve, own)
                norm_dve(dve, own, 0, ALPHA)
                if S >= 2:
                    moe_dve(dve, own)
                    norm_dve(dve, own, 1, ALPHA)
                if S >= 3:
                    ffn_dve(dve, 0)
                    norm_dve(dve, own, 2, ALPHA_2)
                if S >= 4:
                    ml_dve(dve, own)
                    if S >= 5:
                        ffn_first_dve(dve, 1)
                    norm_dve(dve, own, 3, ALPHA_2)
                if S >= 5:
                    ffn_dve(dve, 1)
                    if S >= 6:
                        ffn_first_dve(dve, 2)
                    norm_dve(dve, own, 4, ALPHA_2)
                if S >= 6:
                    ffn_dve(dve, 2)
                    norm_dve(dve, own, 5, ALPHA_2)
                if S >= 7:
                    at_dve(dve, own)
                    if S >= 8:
                        ffn_first_dve(dve, 3)
                    norm_dve(dve, own, 6, ALPHA_2)
                if S >= 8:
                    ffn_dve(dve, 3)
                    norm_dve(dve, own, 7, ALPHA_2)

            @block.sync
            def _(sp):
                sync_program(sp)

            @block.gpsimd
            def _(pool):
                pool_program(pool)


_INS = ['x', 'rec_w_in', 'rec_conv_w', 'rec_conv_b', 'rec_w_r', 'rec_b_r', 'rec_w_i', 'rec_b_i', 'rec_lambda',
        'rec_w_out', 'moe_w_group', 'moe_b_group', 'moe_w_expert', 'moe_b_expert', 'moe_w1', 'moe_w3', 'moe_w2',
        'ln_g', 'ln_b', 'ffn_w_in_2', 'ffn_w_out_2', 'ln_g_2', 'ln_b_2', 'ml_w_in_2', 'ml_gate_b_2', 'ml_norm_g_2',
        'ml_w_out_2', 'at_w_in_2', 'at_sink_2', 'at_w_out_2']


def kernel(**inputs):
    import numpy as _np
    import concourse.bacc as _bacc
    from concourse import mybir as _mybir
    from concourse.bass_utils import run_bass_kernel_spmd as _run

    nc = _bacc.Bacc("TRN2", target_bir_lowering=False, num_devices=1)
    arrays, args = {}, {}
    for name in _INS:
        a = _np.ascontiguousarray(inputs[name])
        arrays[f"in_{name}_dram"] = a
        args[name] = nc.dram_tensor(f"in_{name}_dram", a.shape, _mybir.dt.from_np(a.dtype), kind="ExternalInput").ap()
    out = nc.dram_tensor("out_0_dram", (1, T, D), F32, kind="ExternalOutput").ap()
    build(nc, args, out)
    r = _run(nc, [arrays], core_ids=[0])
    return r.results[0]["out_0_dram"]
```

```python
from contextlib import ExitStack

import numpy as np

import concourse.bass as bass
from concourse import mybir

F32 = mybir.dt.float32
F32R = mybir.dt.float32r
I32 = mybir.dt.int32
ALU = mybir.AluOpType
ACT = mybir.ActivationFunctionType
AX_X = mybir.AxisListType.X

P = 128
T = 256
TT = T // P
D = 1024
KT = D // P
HALF = 512

D_RNN, BW, CONV = 1280, 80, 4
CH = D_RNN // P
GROUPS = CH // 2
PERIOD = int(np.lcm(BW, P)) // P


def gate_tiles():
    tiles, col = [], 0
    for c in range(PERIOD):
        lo, hi, row = c * P, c * P + P, [(c, 0, P)]
        if lo % BW:
            row.append((c - 1, 0, -(-(BW - lo % BW) // 32) * 32))
        if hi % BW:
            first = (P - hi % BW) // 32 * 32
            row.append((c + 1, first, P - first))
        tiles.append([])
        for a, first, rows in row:
            tiles[c].append((a, first, rows, col))
            col += rows
    return tiles, col


GATE_TILES, GATE_COLS = gate_tiles()
ALPHA = 2.0 ** 0.25
EPS = 1e-5

NG, EPG, NE = 4, 8, 32
C = 64
SLOTS = 2 * T
BLOCKS = T // C

ALPHA_2 = 4.0 ** 0.25
FF, FSTEP = 2816, 256
NSTEP = FF // FSTEP
MLH, DQK, DV = 4, 128, 256
NH, HD, NKV = 16, 64, 4
WINDOW = 128
NEG = -1e30

UNIT = 2048
RING = 12
N_LN = 8
WARM = (12, 6)
SPLIT_NORMS = (1, 3, 4, 6)


class Own:

    def __init__(self, eng, sem):
        self.eng, self.sem, self.n = eng, sem, 0

    def did(self, ins):
        ins.then_inc(self.sem, 1)
        self.n += 1
        return self.n

    def then(self, ins):
        self.eng.wait_ge(self.sem, self.did(ins))


def build(nc, A, out):
    ctx = ExitStack()
    with ctx:
        def sb(name, shape, dt=F32):
            return ctx.enter_context(nc.sbuf_tensor(name, shape, dt))

        def sem(name):
            return ctx.enter_context(nc.semaphore(name))

        ring = sb("ring", [P, RING, UNIT])
        arena_at = nc.sbuf_base
        arena = sb("arena", [P, 6 * UNIT])
        split = [[nc.alloc_sbuf_tensor_at(f"split_{kind}_{part}", [P, UNIT], F32R,
                                          offset=arena_at + (2 * j + i) * UNIT * 4)
                  for i, part in enumerate(("hi", "lo"))] for j, kind in enumerate("gud")]
        x_tok = sb("x_tok", [P, TT, D])
        xT = sb("xT", [P, KT, T])
        parts_at = nc.sbuf_base
        x_parts = sb("x_parts", [P, 2 * KT * T])
        x_hi, x_lo = [nc.alloc_sbuf_tensor_at(f"x_{part}", [P, KT, T], F32R, offset=parts_at + i * KT * T * 4)
                      for i, part in enumerate(("hi", "lo"))]
        h_hi = sb("h_hi", [P, 2, 2, T], F32R)
        h_lo = sb("h_lo", [P, 2, 2, T], F32R)
        work = sb("work", [P, 4 * T])
        silu = work[:, 0:2 * T].rearrange("p (a t) -> p a t", a=2)
        h_raw = work[:, 2 * T:].rearrange("p (a t) -> p a t", a=2)
        gb_row = sb("gb_row", [P, 2, D])
        ident = sb("ident", [P, P])
        upper = sb("upper", [P, P])
        lower = sb("lower", [P, P])
        strict = sb("strict", [P, P])
        ones = sb("ones", [P, P])
        gb_raw = sb("gb_raw", [P, P])
        gbT = sb("gbT", [P, P])
        misc_raw = sb("misc_raw", [8 * CH, P])
        misc = sb("misc", [P, 8 * CH])
        ng_raw = sb("ng_raw", [KT, P])
        ngT = sb("ngT", [P, KT])
        stats = sb("stats", [P, 2, 2, 6])
        mean_var = sb("mean_var", [P, 2, 2])
        rstd = sb("rstd", [P, 2])
        neg_mean = sb("neg_mean", [P, 2])
        shift = sb("shift", [P, 2])
        var_eps = sb("var_eps", [P, 2])
        neg_half = sb("neg_half", [P, 8])
        bank = [ctx.enter_context(nc.psum_tensor(f"bank{i}", [P, HALF], F32)) for i in range(8)]

        landed = [sem(f"landed{i}") for i in range(RING)]
        s_x, s_misc, s_gbrow, s_out = sem("s_x"), sem("s_misc"), sem("s_gbrow"), sem("s_out")
        consts, own_dve, own_pool = sem("consts"), sem("own_dve"), sem("own_pool")

        unit = lambda n: ring[:, n % RING, :]

        rec_w_in = A["rec_w_in"][0].rearrange("(k p) n -> p k n", p=P)
        rec_w_out = A["rec_w_out"][0].rearrange("(n p) d -> p n d", p=P)
        w1 = A["moe_w1"][0].rearrange("e (k p) f -> e p k f", p=P)
        w3 = A["moe_w3"][0].rearrange("e (k p) f -> e p k f", p=P)
        w2 = A["moe_w2"][0].rearrange("e (k p) d -> e p k d", p=P)

        UR = 3 * GROUPS
        UA = 2 * RING
        UM = 6 * NE

        def unit_view(n, k):
            return unit(n).rearrange("p (k n) -> p k n", k=k)

        recA_used = sem("recA_used")

        block = ctx.enter_context(nc.Block())

        G = {}
        for name in ("ln_in", "ln_var", "ln_rstd", "ln_shift", "ln_hat_act", "ln_hat_dve", "ln_tr", "ln_evac_act", "ln_evac_dve",
                     "ln_hi", "ln_lo", "ln_tok"):
            G[name] = sem(name)


        r = {n: sem("rec_" + n) for n in ("gelu", "x_sb", "conv", "ri_mm", "tanh", "sqrt",
                                          "t", "y", "const", "q")}
        buf = lambda a: [arena[:, a + g * 512:a + g * 512 + 512].rearrange("p (b t) -> p b t", b=2)
                         for g in range(2)]
        xp = [arena[:, g * 518:g * 518 + 518].rearrange("p (b t) -> p b t", b=2) for g in range(2)]
        xc = arena[:, 1040:1040 + CH * T].rearrange("p (n t) -> p n t", n=CH)
        th_r, th_i, root, rec_b, h_b = buf(3600), buf(4624), buf(5648), buf(6672), buf(7696)
        gelu = arena[:, 8720:8720 + CH * T].rearrange("p (n t) -> p n t", n=CH)
        lam_q = sb("lam_q", [P, 12, CH])

        mo = {n: sem("moe_" + n) for n in (
            "logit", "e1", "e2", "exp1", "exp2", "assign", "rank", "pos", "gath", "gath_ev", "start", "xe",
            "ha", "hb", "silu", "h", "tr", "hT", "y", "ysb", "h0", "diag", "rows", "rows_sb", "sel", "comb")}
        xs = arena[:, 0:KT * 768].rearrange("p (k s) -> p k s", k=KT)
        onehot = arena[:, 6144:7168].rearrange("p (t s) -> p t s", t=TT)
        xe = [arena[:, 7168 + i * 512:7680 + i * 512].rearrange("p (k c) -> p k c", k=KT) for i in range(2)]
        sil_e, h_e = arena[:, 8192:8704], arena[:, 8704:9216]
        hT_e = [arena[:, 9216 + i * 256:9472 + i * 256].rearrange("p (k c) -> p k c", k=4) for i in range(2)]
        y_e = [arena[:, 9728 + i * 512:10240 + i * 512] for i in range(2)]
        rows_b = arena[:, 10752:11776].rearrange("p (v t) -> p v t", v=4)
        rows_diag = arena[:, 8192:9216].rearrange("p (v t j) -> p v t j", v=4, t=TT)
        pick_e = [arena[:, 11776 + i * 256:12032 + i * 256] for i in range(2)]
        route_w = sb("route_w", [P, KT, NG + NE])
        route_b = sb("route_b", [P, NG + NE])
        RT = work
        iota_s = sb("iota_s", [P, SLOTS])
        start_i = sb("start_i", [1, NE + 1], I32)
        s_route, own_sel = sem("s_route"), sem("own_sel")
        sel_tmp = work[:, 0:T]

        def rt(a, *shape):
            n = int(np.prod(shape))
            v = RT[:, a:a + n]
            if len(shape) == 2:
                return v.rearrange("p (a b) -> p a b", b=shape[1])
            if len(shape) == 3:
                return v.rearrange("p (a b c) -> p a b c", b=shape[1], c=shape[2])
            return v

        lg = rt(0, TT, NG + NE)
        v_gmax, v_gsum, v_ggate = rt(72, TT), rt(74, TT), rt(76, TT)
        v_v1, v_v2, v_ed, v_p1 = rt(78, TT), rt(80, TT), rt(82, TT), rt(84, TT)
        v_m = rt(86, TT)
        g_oh = rt(96, TT, NG)
        e_sel, e_c = rt(104, TT, EPG), rt(120, TT, EPG)
        oh = [rt(136, TT, EPG), rt(152, TT, EPG)]
        tmp32 = rt(168, TT, NG, EPG)
        A1 = [rt(232, TT, NG, EPG), rt(296, TT, NG, EPG)]
        A12 = rt(360, TT, NE)
        v_start, v_incl = rt(424, NE), rt(456, NE)
        v_q, v_full = rt(488, TT, NE), rt(552, NE)
        v_t = rt(616, TT, NE)
        v_pos = [rt(680, TT), rt(682, TT)]
        gates = [rt(688, TT), rt(690, TT)]
        slot_p = rt(692, 1)
        i_8m = rt(724, EPG)
        cmax = rt(732, 1)
        g_e = rt(733, TT, NG)
        v_rank = rt(744, TT, NE)
        v_cnt = rt(808, NE)
        place = rt(840, BLOCKS, NE)


        def sync_program(sp):
            sp.dma_start(x_tok[:], A["x"][0].rearrange("(t p) d -> p t d", p=P)).then_inc(s_x, 16)
            for n in range(UR):
                if n == GROUPS:
                    sp.wait_ge(s_wzero, 1)
                    for gate, name in enumerate(("rec_w_r", "rec_w_i")):
                        blocks = A[name][0].rearrange("(q n) k j -> n k q j", q=2)
                        for m, row, k0, k1, j0, j1, col in pieces:
                            sp.dma_start(wri[k0 - row:k1 - row, gate, :, col:col + j1 - j0],
                                          blocks[m, k0 - m * BW:k1 - m * BW, :, j0 - m * BW:j1 - m * BW]).then_inc(s_wri, 16)
                if n >= RING:
                    sp.wait_ge(recA_used, n - RING + 1)
                if n < 2 * GROUPS:
                    src, dst = rec_w_in[:, :, n * 2 * P:(n + 1) * 2 * P], unit_view(n, KT)
                else:
                    g = n - 2 * GROUPS
                    src, dst = rec_w_out[:, 2 * g:2 * g + 2, :], unit_view(n, 2)
                sp.dma_start(dst, src).then_inc(landed[n % RING], 16)
            def expert_loads(e, p, wait):
                for j in range(6):
                    if wait is not None:
                        wait(j)
                    n = 6 * p + j
                    if j < 4:
                        w = (w1, w3)[j % 2]
                        src = w[bass.ds(e, 1), :, 4 * (j // 2):4 * (j // 2) + 4, :].rearrange("e p k f -> (e p) k f") \
                            if not isinstance(e, int) else w[e, :, 4 * (j // 2):4 * (j // 2) + 4, :]
                        dst = unit_view(n, 4)
                    else:
                        src = w2[bass.ds(e, 1), :, 2 * (j - 4):2 * (j - 4) + 2, :].rearrange("e p k f -> (e p) k f") \
                            if not isinstance(e, int) else w2[e, :, 2 * (j - 4):2 * (j - 4) + 2, :]
                        dst = unit_view(n, 2)
                    sp.dma_start(dst, src).then_inc(landed[n], 16)

            def first_free(slot):
                if slot >= UR - RING:
                    sp.wait_ge(recA_used, slot + 1)
                    sp.sem_inc(landed[slot], 16)
                elif slot < UR - RING - 1:
                    sp.wait_ge(recA_used, RING + slot + 1)
                else:
                    sp.wait_ge(G["ln_in"], TT)

            for p in range(2):
                expert_loads(p, p, lambda j, p=p: first_free(6 * p + j))

            with sp.Fori(1, NE // 2) as it:
                for p in range(2):
                    def free(j, p=p):
                        if j < 4:
                            sp.wait_ge(mo["ha"] if j < 2 else mo["hb"], 2 * it + p - 1)
                        else:
                            sp.wait_ge(mo["y"], 2 * it + p - 1)
                    expert_loads(2 * it + p, p, free)
            sp.wait_ge(mo["start"], 1)
            over = sp.value_load(start_i[0:1, NE:NE + 1])
            with sp.If(over > C):
                overflow_loads(sp)
            later_loads(sp)
            rows = out[0].rearrange("(t p) d -> t p d", p=P)
            for t, (s, count) in enumerate(((G["ln_tok"], 2 * N_LN - 1), (G["ln_hat_dve"], N_LN + 1))):
                sp.wait_ge(s, count)
                sp.dma_start(rows[t], x_tok[:, t, :]).then_inc(s_out, 16)
            sp.wait_ge(s_out, 32)

        in2 = [A["ffn_w_in_2"][l, i].rearrange("(k p) n -> p k n", p=P) for l in range(2) for i in range(2)]
        out2 = [A["ffn_w_out_2"][l, i].rearrange("(k p) d -> p k d", p=P) for l in range(2) for i in range(2)]
        ml_in = A["ml_w_in_2"][0].rearrange("(k p) n -> p k n", p=P)
        ml_out = A["ml_w_out_2"][0].rearrange("(k p) d -> p k d", p=P)
        at_in = A["at_w_in_2"][0].rearrange("(k p) n -> p k n", p=P)
        at_out = A["at_w_out_2"][0].rearrange("(k p) d -> p k d", p=P)
        f_lo = [sem(f"ffn_lo_{k}") for k in "gud"]
        f_hi = [sem(f"ffn_hi_{k}") for k in "gud"]
        f_mm = [sem(f"ffn_mm_{k}") for k in "gud"]
        f_silu, f_h, f_hhi, f_hlo = sem("ffn_silu"), sem("ffn_h"), sem("ffn_hhi"), sem("ffn_hlo")
        mx_tr, mx_act, mx_dve, mx_used = sem("mix_turned"), sem("mix_act"), sem("mix_dve"), sem("mix_used")
        ml = {n: sem("ml_" + n) for n in ("gp", "af", "l", "logf", "cum", "diag", "q", "k", "v", "o", "qs", "ks", "vs",
                                          "os", "b", "mask", "s", "nm", "exp", "p", "tr", "pt", "h", "h3", "ve", "rs",
                                          "y", "param", "exp0")}
        at = {n: sem("at_" + n) for n in ("k", "v", "q", "ka", "kd", "vd", "qa", "qd", "s", "nm", "p", "tr", "pt", "o",
                                          "ds", "sum", "oe", "iota")}
        FIRST = UA + UM
        units = []
        at_unit = {}

        def add_ffn(f):
            at_unit["f", f] = FIRST + len(units)
            order = [(0, 0), (1, 0)]
            for s_ in range(NSTEP - 1):
                order += [(0, s_ + 1), (1, s_ + 1), (2, s_)]
            order += [(2, NSTEP - 1)]
            for kind, s_ in order:
                at_unit["f", f, kind, s_] = FIRST + len(units)
                if kind < 2:
                    src, k = in2[f][:, :, kind * FF + s_ * FSTEP:kind * FF + (s_ + 1) * FSTEP], KT
                else:
                    src, k = out2[f][:, 2 * s_:2 * s_ + 2, :], 2
                units.append((k, src, (f_lo[kind], NSTEP * f + s_ + 1)))

        def add_columns(name, w, c, used, n):
            for j in range(2):
                at_unit[name, n + j] = FIRST + len(units)
                units.append((4, w[:, 4 * j:4 * j + 4, c * 512:(c + 1) * 512], used))
            return n + 2

        def add_rows(name, w, m, n, L):
            for j in range(4):
                at_unit[name, n + j] = FIRST + len(units)
                units.append((2, w[:, 2 * j:2 * j + 2, :], (mx_used, 3 * m + j + 1) if j < 3 else (G["ln_in"], 2 * L + 2)))

        add_ffn(0)
        n_ = 0
        for c_, used_ in enumerate(((ml["q"], 2), (ml["k"], 2), (ml["v"], 2), (ml["v"], 4), (ml["o"], 2), (ml["o"], 4))):
            n_ = add_columns("ml", ml_in, c_, used_, n_)
        add_rows("ml", ml_out, 0, n_, 3)
        add_ffn(1)
        add_ffn(2)
        n_ = 0
        for c_, used_ in ((2, (at["v"], 1)), (0, (at["q"], 2)), (1, (at["q"], 4))):
            n_ = add_columns("at", at_in, c_, used_, n_)
        add_rows("at", at_out, 1, n_, 6)
        add_ffn(3)

        def unit_used(n):
            if n < FIRST:
                e, j = (n - UA) // 6, (n - UA) % 6
                return (mo["ha"] if j < 2 else mo["hb"] if j < 4 else mo["y"]), e + 1
            return units[n - FIRST][2]

        def later_loads(sp):
            for n in range(FIRST, FIRST + len(units)):
                k, src, _ = units[n - FIRST]
                sp.wait_ge(*unit_used(n - RING))
                sp.dma_start(unit_view(n, k), src).then_inc(landed[n % RING], 16)

        def here(eng, n):
            eng.wait_ge(landed[n % RING], 16 * (n // RING + 1))

        ov = {n: sem("ov_" + n) for n in ("load", "xe", "h", "silu", "hm", "tr", "hT", "y", "ysb", "sel", "comb")}

        def each_overflow(eng):
            with eng.Fori(1, BLOCKS) as b:
                with eng.Fori(0, NE) as e:
                    yield (b - 1) * NE + e, b, e

        def overflow_loads(sp):
            sp.wait_ge(mo["y"], NE)
            for n, b, e in each_overflow(sp):
                sp.wait_ge(ov["y"], n + 1)
                for j in range(6):
                    w = (w1, w3)[j % 2] if j < 4 else w2
                    k0, kn = (4 * (j // 2), 4) if j < 4 else (2 * (j - 4), 2)
                    src = w[bass.ds(e, 1), :, k0:k0 + kn, :].rearrange("e p k f -> (e p) k f")
                    sp.dma_start(unit_view(j, kn), src).then_inc(ov["load"], 16)

        def pool_program(pool):
            own = Own(pool, own_pool)
            for m, v in ((ident, 0.0), (upper, 1.0), (lower, 1.0), (strict, 1.0)):
                own.then(nc.gpsimd.memset(m[:], v))
            own.did(nc.gpsimd.memset(neg_half[:], -0.5))
            nc.gpsimd.memset(ones[:], 1.0).then_inc(consts, 1)
            nc.gpsimd.affine_select(out=ident[:], in_=ident[:], compare_op=ALU.not_equal, fill=1.0, base=0,
                                    pattern=[[-1, P]], channel_multiplier=1).then_inc(consts, 1)
            nc.gpsimd.affine_select(out=upper[:], in_=upper[:], compare_op=ALU.is_ge, fill=0.0, base=0,
                                    pattern=[[1, P]], channel_multiplier=-1).then_inc(consts, 1)
            nc.gpsimd.affine_select(out=lower[:], in_=lower[:], compare_op=ALU.is_ge, fill=0.0, base=0,
                                    pattern=[[-1, P]], channel_multiplier=1).then_inc(consts, 1)
            nc.gpsimd.affine_select(out=strict[:], in_=strict[:], compare_op=ALU.is_gt, fill=0.0, base=0,
                                    pattern=[[1, P]], channel_multiplier=-1).then_inc(consts, 1)
            nc.gpsimd.iota(iota_s[:], pattern=[[1, SLOTS]], base=0, channel_multiplier=0,
                           allow_small_or_imprecise_dtypes=True).then_inc(consts, 1)
            for j in range(2):
                pool.wait_ge(consts, 6 + j)
                nc.gpsimd.iota(slot_p[64 * j:64 * j + 64, :], pattern=[[0, 1]], base=0, channel_multiplier=1,
                               allow_small_or_imprecise_dtypes=True).then_inc(consts, 1)
            pool.wait_ge(consts, 8)
            nc.gpsimd.iota(i_8m, pattern=[[1, EPG]], base=-64, channel_multiplier=0,
                           allow_small_or_imprecise_dtypes=True).then_inc(consts, 1)
            pool.dma_start(misc_raw[0:CONV * CH, :], A["rec_conv_w"][0].rearrange("k (n p) -> (k n) p", p=P)).then_inc(s_misc, 16)
            for j, name in enumerate(("rec_conv_b", "rec_b_r", "rec_b_i", "rec_lambda")):
                at = (CONV + j) * CH
                pool.dma_start(misc_raw[at:at + CH, :], A[name][0].rearrange("(n p) -> n p", p=P)).then_inc(s_misc, 16)
            for j, (name, rows) in enumerate((("ln_g", 2), ("ln_g_2", 6), ("ln_b", 2), ("ln_b_2", 6))):
                at = (0, 16, 64, 80)[j]
                src = A[name][0] if rows == 2 else A[name].rearrange("l s d -> (l s) d")
                pool.dma_start(gb_raw[at:at + 8 * rows, :], src.rearrange("s (k p) -> (s k) p", p=P)).then_inc(s_misc, 16)
            pool.dma_start(ng_raw[:], A["ml_norm_g_2"][0].rearrange("(k p) -> k p", p=P)).then_inc(s_misc, 16)
            pool.dma_start(route_w[:, :, 0:NG], A["moe_w_group"][0].rearrange("(k p) n -> p k n", p=P)).then_inc(s_route, 16)
            pool.dma_start(route_w[:, :, NG:], A["moe_w_expert"][0].rearrange("(k p) n -> p k n", p=P)).then_inc(s_route, 16)
            pool.dma_start(route_b[:, 0:NG], A["moe_b_group"].broadcast_to((P, NG))).then_inc(s_route, 16)
            pool.dma_start(route_b[:, NG:], A["moe_b_expert"].broadcast_to((P, NE))).then_inc(s_route, 16)
            pool.dma_start(gate_w[:], A["ml_w_in_2"][0].rearrange("(k p) n -> p k n", p=P)[:, :, 3072:3088]).then_inc(ml["param"], 16)
            pool.dma_start(gate_b[:], A["ml_gate_b_2"].broadcast_to((P, 16))).then_inc(ml["param"], 16)
            pool.dma_start(sink[:], A["at_sink_2"].broadcast_to((P, NH))).then_inc(ml["param"], 16)
            norm_pool(pool, own, 0, after_gather=True)
            moe_pool(pool, own)
            norm_pool(pool, own, 1)
            for L in range(2, N_LN):
                norm_pool(pool, own, L)
                if L == 2:
                    ml_pool(pool, own)
                if L == 5:
                    at_pool(pool, own)

        def norm_pool(pool, own, L, after_gather=False):
            g_src, b_src, s = (A["ln_g"], A["ln_b"], L) if L < 2 else (A["ln_g_2"], A["ln_b_2"], L - 2)
            gs = g_src.rearrange("l s d -> (l s) d")[s:s + 1, :]
            bs = b_src.rearrange("l s d -> (l s) d")[s:s + 1, :]
            pool.dma_start(gb_row[:, 0, :], gs.broadcast_to((P, D))).then_inc(s_gbrow, 16)
            pool.dma_start(gb_row[:, 1, :], bs.broadcast_to((P, D))).then_inc(s_gbrow, 16)
            for t in range(TT):
                pool.wait_ge(G["ln_var"], 2 * (2 * L + t + 1))
                nc.gpsimd.tensor_tensor(rstd[:, t:t + 1], var_eps[:, t:t + 1], neg_half[:, 0:1], ALU.pow) \
                    .then_inc(G["ln_rstd"], 1)
                pool.wait_ge(G["ln_rstd"], 2 * L + t + 1)
                nc.gpsimd.tensor_tensor(shift[:, t:t + 1], neg_mean[:, t:t + 1], rstd[:, t:t + 1], ALU.mult) \
                    .then_inc(G["ln_shift"], 1)
            pool.wait_ge(s_gbrow, 32 * (L + 1))
            if L < N_LN - 1:
                pool.wait_ge(G["ln_tr"], 4 * (L + 1))
            else:
                pool.wait_ge(G["ln_hat_act"], 2 * L + 1)
            if after_gather:
                pool.wait_ge(mo["gath"], KT)
            tiles = TT if L < N_LN - 1 else 1
            for t in range(tiles):
                own.then(nc.gpsimd.tensor_tensor(x_tok[:, t, :], x_tok[:, t, :], gb_row[:, 0, :], ALU.mult))
                nc.gpsimd.tensor_tensor(x_tok[:, t, :], x_tok[:, t, :], gb_row[:, 1, :], ALU.add).then_inc(G["ln_tok"], 1)
            pool.wait_ge(G["ln_tok"], 2 * L + tiles)

        def norm_dve(dve, own, L, alpha):
            for t in range(TT):
                dve.wait_ge(G["ln_in"], 2 * L + t + 1)
                if L > 0 and t == 0:
                    dve.wait_ge(G["ln_tok"], 2 * L)
                for hf in range(2):
                    v = x_tok[:, t, hf * HALF:(hf + 1) * HALF]
                    own.did(nc.vector.scalar_tensor_tensor(out=v, in0=v, scalar=alpha, in1=bank[2 * t + hf][:],
                                                           op0=ALU.mult, op1=ALU.add))
                    dve.wait_ge(own_dve, own.n)
                    own.did(nc.vector.bn_stats(stats[:, t, hf, :], v))
                dve.wait_ge(own_dve, own.n)
                own.then(nc.vector.bn_aggr(mean_var[:, t, :], stats[:, t, :, :].rearrange("p a b -> p (a b)")))
                nc.vector.tensor_scalar(var_eps[:, t:t + 1], mean_var[:, t, 1:2], EPS, None, ALU.add).then_inc(G["ln_var"], 1)
                nc.vector.tensor_scalar(neg_mean[:, t:t + 1], mean_var[:, t, 0:1], -1.0, None, ALU.mult).then_inc(G["ln_var"], 1)
            dve.wait_ge(G["ln_rstd"], 2 * L + 2)
            nc.vector.tensor_scalar(x_tok[:, 1, 0:HALF], x_tok[:, 1, 0:HALF], mean_var[:, 1, 0:1], rstd[:, 1:2],
                                    ALU.subtract, ALU.mult).then_inc(G["ln_hat_dve"], 1)
            if L < N_LN - 1:
                norm_evac_dve(dve, L)
            else:
                dve.wait_ge(G["ln_hat_dve"], L + 1)
                dve.wait_ge(G["ln_hat_act"], 2 * (L + 1))
                dve.wait_ge(s_gbrow, 32 * (L + 1))
                own.then(nc.vector.tensor_tensor(x_tok[:, 1, :], x_tok[:, 1, :], gb_row[:, 0, :], ALU.mult))
                nc.vector.tensor_tensor(x_tok[:, 1, :], x_tok[:, 1, :], gb_row[:, 1, :], ALU.add).then_inc(G["ln_hat_dve"], 1)

        def norm_evac_dve(dve, L):
            for b in (1, 3):
                dve.wait_ge(G["ln_tr"], 4 * L + b + 1)
                for k in (2 * b, 2 * b + 1):
                    i = nc.vector.tensor_scalar(xT[:, k, :], bank[4 + b][:, (k % 2) * T:(k % 2) * T + T],
                                                gbT[:, 8 * L + k:8 * L + k + 1],
                                                gbT[:, 64 + 8 * L + k:64 + 8 * L + k + 1], ALU.mult, ALU.add)
                i.then_inc(G["ln_evac_dve"], 1)
            if L in SPLIT_NORMS:
                n = SPLIT_NORMS.index(L)
                for b in range(4):
                    dve.wait_ge(G["ln_hi"], 4 * n + b + 1)
                    nc.vector.tensor_tensor(x_lo[:, 2 * b:2 * b + 2, :], xT[:, 2 * b:2 * b + 2, :],
                                            x_hi[:, 2 * b:2 * b + 2, :].bitcast(F32), ALU.subtract).then_inc(G["ln_lo"], 1)

        def norm_act(act, L):
            for t in range(TT):
                act.wait_ge(G["ln_shift"], 2 * L + t + 1)
                v = x_tok[:, t, t * HALF:]
                nc.scalar.activation(v, v, ACT.Identity, scale=rstd[:, t:t + 1], bias=shift[:, t:t + 1]) \
                    .then_inc(G["ln_hat_act"], 1)

        def norm_evac_act(act, L):
            norm_act(act, L)
            for b in (0, 2):
                act.wait_ge(G["ln_tr"], 4 * L + b + 1)
                for k in (2 * b, 2 * b + 1):
                    i = nc.scalar.activation(xT[:, k, :], bank[4 + b][:, (k % 2) * T:(k % 2) * T + T], ACT.Identity,
                                             scale=gbT[:, 8 * L + k:8 * L + k + 1],
                                             bias=gbT[:, 64 + 8 * L + k:64 + 8 * L + k + 1])
                i.then_inc(G["ln_evac_act"], 1)
            if L in SPLIT_NORMS:
                for b in range(4):
                    s = G["ln_evac_dve"] if b % 2 else G["ln_evac_act"]
                    act.wait_ge(s, 2 * L + b // 2 + 1)
                    nc.scalar.activation(x_hi[:, 2 * b:2 * b + 2, :], xT[:, 2 * b:2 * b + 2, :], ACT.Copy).then_inc(G["ln_hi"], 1)

        def keep_warm(pe, n):
            for i in range(n):
                nc.tensor.matmul(bank[6][:, P:2 * P], ident[:], xT[:, 0, 0:P], start=True, stop=True)

        def norm_pe(pe, L):
            for t in range(TT):
                keep_warm(pe, WARM[t])
                for k in range(KT):
                    if k == 0 and t == 1:
                        pe.wait_ge(G["ln_hat_dve"], L + 1)
                    elif k == t * KT // 2:
                        pe.wait_ge(G["ln_hat_act"], 2 * L + t + 1)
                    i = nc.tensor.transpose(bank[4 + k // 2][:, (k % 2) * T + t * P:(k % 2) * T + t * P + P],
                                            x_tok[:, t, k * P:(k + 1) * P], ident[:])
                    if t == TT - 1 and k % 2:
                        i.then_inc(G["ln_tr"], 1)

        def xT_ready(pe, L):
            pe.wait_ge(G["ln_evac_act"], 2 * (L + 1))
            pe.wait_ge(G["ln_evac_dve"], 2 * (L + 1))

        wri = x_parts[:, 0:4 * GATE_COLS].rearrange("p (g q j) -> p g q j", g=2, q=2)
        s_wri, s_wzero = sem("s_wri"), sem("s_wzero")
        s_par, s_parT, s_xT0, s_xT0b = sem("s_par"), sem("s_parT"), sem("s_xT0"), sem("s_xT0b")

        pieces = []
        for n in range(PERIOD * P // BW):
            lo, hi = n * BW, (n + 1) * BW
            for c in range(lo // P, (hi - 1) // P + 1):
                for a, first, rows, col in GATE_TILES[c]:
                    k0, k1 = max(lo, a * P), min(hi, (a + 1) * P)
                    j0, j1 = max(lo, c * P), min(hi, (c + 1) * P)
                    if k0 < k1:
                        pieces.append((n, a * P, k0, k1, j0, j1, col + j0 - c * P - first))
        GATE_PIECES = 2 * len(pieces)

        def columns(n, o):
            for b in range(2):
                for k in range(KT):
                    i = nc.tensor.matmul(o[:, b * T:(b + 1) * T], unit_view(n, KT)[:, k, b * P:(b + 1) * P],
                                         xT[:, k, :], start=(k == 0), stop=(k == KT - 1))
            i.then_inc(recA_used, 1)

        def rec_pe(pe):
            pe.wait_ge(s_x, 16)
            pe.wait_ge(consts, 9)
            for k in range(KT):
                for t in range(TT):
                    i = nc.tensor.transpose(bank[k // 2][:, (k % 2) * T + t * P:(k % 2) * T + t * P + P],
                                            x_tok[:, t, k * P:(k + 1) * P], ident[:])
                if k % 2:
                    i.then_inc(s_xT0, 1)
            pe.wait_ge(s_xT0b, 4)
            for g in range(GROUPS):
                pe.wait_ge(landed[g % RING], 16)
                if g == 3:
                    pe.wait_ge(s_misc, 16 * 10)
                    nc.tensor.transpose(bank[4][:, 0:8 * CH], misc_raw[:], ident[0:8 * CH, 0:8 * CH])
                    nc.tensor.transpose(bank[5][:, 0:P], gb_raw[:], ident[:])
                    nc.tensor.transpose(bank[6][:, 0:KT], ng_raw[:], ident[0:KT, 0:KT]).then_inc(s_par, 1)
                if g >= 2:
                    pe.wait_ge(r["gelu"], g - 1)
                columns(g, bank[g % 2])

            def gates_of(q):
                if q == 0:
                    pe.wait_ge(s_wri, 16 * GATE_PIECES)
                    pe.wait_ge(s_parT, 2)
                pe.wait_ge(r["conv"], min(q + 2, GROUPS))
                if q >= 2:
                    pe.wait_ge(r["tanh"], 2 * (q - 1))
                for gate in range(2):
                    for b in range(2):
                        per, c = divmod(2 * q + b, PERIOD)
                        tiles = GATE_TILES[c]
                        for j, (a, first, rows, col) in enumerate(tiles):
                            i = nc.tensor.matmul(bank[4 + 2 * gate + q % 2][first:first + rows, b * T:(b + 1) * T],
                                                 wri[:, gate, per, col:col + rows], xc[:, per * PERIOD + a, :],
                                                 start=(j == 0), stop=(j == len(tiles) - 1), skip_group_check=True)
                    i.then_inc(r["ri_mm"], 1)

            def project(g):
                n = 2 * GROUPS + g
                pe.wait_ge(landed[n % RING], 16 * (n // RING + 1))
                pe.wait_ge(r["y"], g + 1)
                w = unit_view(n, 2)
                for b in range(2):
                    for t in range(TT):
                        for hf in range(2):
                            i = nc.tensor.matmul(bank[2 * t + hf][:], gelu[:, 2 * g + b, t * P:(t + 1) * P],
                                                 w[:, b, hf * HALF:(hf + 1) * HALF],
                                                 start=(g == 0 and b == 0), stop=(g == GROUPS - 1 and b == 1))
                        if g == GROUPS - 1 and b == 1:
                            i.then_inc(G["ln_in"], 1)
                if g < GROUPS - 1:
                    i.then_inc(recA_used, 1)

            for g in range(GROUPS):
                n = GROUPS + g
                pe.wait_ge(landed[n % RING], 16 * (n // RING + 1))
                if g >= 2:
                    pe.wait_ge(r["x_sb"], g - 1)
                else:
                    pe.wait_ge(r["gelu"], GROUPS - 1 + g)
                columns(n, bank[n % 2])
                if g >= 2:
                    gates_of(g - 2)
            gates_of(GROUPS - 2)
            pe.wait_ge(r["x_sb"], GROUPS)
            project(0)
            gates_of(GROUPS - 1)
            for g in range(1, GROUPS):
                project(g)

        def rec_act(act):
            for b in (0, 2):
                act.wait_ge(s_xT0, b + 1)
                nc.scalar.activation(xT[:, 2 * b:2 * b + 2, :], bank[b][:].rearrange("p (a t) -> p a t", a=2), ACT.Copy).then_inc(s_xT0b, 1)
            for g in range(GROUPS):
                act.wait_ge(recA_used, g + 1)
                nc.scalar.activation(gelu[:, 2 * g:2 * g + 2, :], bank[g % 2][:].rearrange("p (b t) -> p b t", b=2),
                                     ACT.Gelu_apprx_tanh).then_inc(r["gelu"], 1)
            act.wait_ge(r["const"], 1)
            nc.scalar.activation(lam_q[:, 1, :], lam_q[:, 0, :], ACT.Exp, scale=-1.0).then_inc(r["q"], 1)
            for g in range(GROUPS + 2):
                if g < GROUPS:
                    act.wait_ge(recA_used, GROUPS + g + 1)
                    if g >= 2:
                        act.wait_ge(r["conv"], g - 1)
                    if g == 0:
                        act.wait_ge(r["const"], 2)
                    nc.scalar.activation(xp[g % 2][:, :, CONV - 1:], bank[(GROUPS + g) % 2][:].rearrange("p (b t) -> p b t", b=2),
                                         ACT.Copy).then_inc(r["x_sb"], 1)
                if g >= 2:
                    q = g - 2
                    if q >= 2:
                        act.wait_ge(r["y"], q - 1)
                    if q == 0:
                        act.wait_ge(r["const"], 3)
                    for gate, th in ((0, th_r), (1, th_i)):
                        act.wait_ge(r["ri_mm"], 2 * q + gate + 1)
                        for b in range(2):
                            nb = 2 * q + b
                            i = nc.scalar.activation(th[q % 2][:, b, :], bank[4 + 2 * gate + q % 2][:, b * T:(b + 1) * T],
                                                     ACT.Tanh, scale=0.5, bias=lam_q[:, 10 + gate, nb:nb + 1])
                        i.then_inc(r["tanh"], 1)
                    act.wait_ge(r["tanh"], 2 * q + 1)
                    for b in range(2):
                        nb = 2 * q + b
                        i = nc.scalar.activation(th_r[q % 2][:, b, :], th_r[q % 2][:, b, :], ACT.Tanh,
                                                 scale=lam_q[:, 9, nb:nb + 1], bias=lam_q[:, 9, nb:nb + 1])
                    i.then_inc(r["t"], 1)
                    act.wait_ge(r["t"], q + 1)
                    nc.scalar.activation(root[q % 2], th_r[q % 2], ACT.Sqrt).then_inc(r["sqrt"], 1)

        def rec_dve(dve, own):
            nc.vector.memset(x_parts[:], 0.0).then_inc(s_wzero, 1)
            for b in (1, 3):
                dve.wait_ge(s_xT0, b + 1)
                nc.vector.tensor_copy(xT[:, 2 * b:2 * b + 2, :], bank[b][:].rearrange("p (a t) -> p a t", a=2)).then_inc(s_xT0b, 1)
            dve.wait_ge(s_par, 1)
            own.then(nc.vector.tensor_copy(misc[:], bank[4][:, 0:8 * CH]))
            nc.vector.tensor_copy(gbT[:], bank[5][:, 0:P]).then_inc(s_parT, 1)
            nc.vector.tensor_copy(ngT[:], bank[6][:, 0:KT]).then_inc(s_parT, 1)
            lam = misc[:, 7 * CH:8 * CH]
            own.then(nc.vector.tensor_scalar(lam_q[:, 2, :], lam, -1.0, 0.0, ALU.mult, ALU.max))
            own.then(nc.vector.tensor_scalar(lam_q[:, 3, :], lam, 0.0, None, ALU.max))
            nc.vector.tensor_tensor(lam_q[:, 0, :], lam_q[:, 2, :], lam_q[:, 3, :], ALU.add).then_inc(r["const"], 1)
            for g in range(2):
                i = nc.vector.memset(xp[g][:, :, 0:CONV - 1], 0.0)
            i.then_inc(r["const"], 1)
            own.then(nc.vector.tensor_scalar(lam_q[:, 10, :], misc[:, 5 * CH:6 * CH], 0.5, None, ALU.mult))
            own.then(nc.vector.tensor_scalar(lam_q[:, 11, :], misc[:, 6 * CH:7 * CH], 0.5, None, ALU.mult))
            dve.wait_ge(r["q"], 1)
            e = lam_q[:, 1, :]
            own.then(nc.vector.tensor_scalar(lam_q[:, 4, :], e, 2.0, None, ALU.add))
            own.then(nc.vector.reciprocal(lam_q[:, 5, :], lam_q[:, 4, :]))
            own.then(nc.vector.tensor_tensor(lam_q[:, 6, :], e, lam_q[:, 5, :], ALU.mult))
            own.then(nc.vector.tensor_tensor(lam_q[:, 7, :], lam_q[:, 6, :], lam_q[:, 6, :], ALU.mult))
            own.then(nc.vector.tensor_scalar(lam_q[:, 8, :], lam_q[:, 7, :], 1.0 / 17, 1.0 / 15, ALU.mult, ALU.add))
            for c in (13, 11, 9, 7, 5, 3, 1):
                own.then(nc.vector.tensor_tensor(lam_q[:, 8, :], lam_q[:, 8, :], lam_q[:, 7, :], ALU.mult))
                own.then(nc.vector.tensor_scalar(lam_q[:, 8, :], lam_q[:, 8, :], 1.0 / c, None, ALU.add))
            own.then(nc.vector.tensor_tensor(lam_q[:, 8, :], lam_q[:, 8, :], lam_q[:, 6, :], ALU.mult))
            own.then(nc.vector.scalar_tensor_tensor(out=lam_q[:, 9, :], in0=lam_q[:, 8, :], scalar=2.0, in1=lam_q[:, 2, :],
                                                    op0=ALU.mult, op1=ALU.add))
            nc.vector.tensor_scalar(lam_q[:, 9, :], lam_q[:, 9, :], 2.0, None, ALU.mult).then_inc(r["const"], 1)
            for g in range(GROUPS + 2):
                if g < GROUPS:
                    dve.wait_ge(r["x_sb"], g + 1)
                    for tap in range(CONV):
                        for b in range(2):
                            nb = 2 * g + b
                            o, src = xc[:, nb, :], xp[g % 2][:, b, tap:tap + T]
                            w = misc[:, tap * CH + nb:tap * CH + nb + 1]
                            if tap == 0:
                                i = nc.vector.tensor_scalar(o, src, w, misc[:, CONV * CH + nb:CONV * CH + nb + 1], ALU.mult, ALU.add)
                            else:
                                i = nc.vector.scalar_tensor_tensor(out=o, in0=src, scalar=w, in1=o, op0=ALU.mult, op1=ALU.add)
                        if tap < CONV - 1:
                            own.then(i)
                    i.then_inc(r["conv"], 1)
                if g >= 2:
                    q = g - 2
                    s = q % 2
                    dve.wait_ge(r["t"], q + 1)
                    own.then(nc.vector.tensor_scalar(rec_b[s], th_r[s], 1.0, None, ALU.add))
                    own.then(nc.vector.reciprocal(rec_b[s], rec_b[s]))
                    own.did(nc.vector.scalar_tensor_tensor(out=th_i[s], in0=th_i[s], scalar=1.0, in1=xc[:, 2 * q:2 * q + 2, :],
                                                                op0=ALU.add, op1=ALU.mult))
                    dve.wait_ge(r["sqrt"], q + 1)
                    own.then(nc.vector.tensor_tensor(root[s], root[s], rec_b[s], ALU.mult))
                    own.then(nc.vector.tensor_scalar(rec_b[s], rec_b[s], 2.0, -1.0, ALU.mult, ALU.add))
                    own.then(nc.vector.tensor_tensor(root[s], root[s], th_i[s], ALU.mult))
                    for b in range(2):
                        i = nc.vector.tensor_tensor_scan(h_b[s][:, b, :], rec_b[s][:, b, :], root[s][:, b, :], 0.0,
                                                         ALU.mult, ALU.add)
                        own.did(i)
                    dve.wait_ge(own_dve, own.n)
                    nc.vector.tensor_tensor(gelu[:, 2 * q:2 * q + 2, :], h_b[s], gelu[:, 2 * q:2 * q + 2, :],
                                            ALU.mult).then_inc(r["y"], 1)

        def moe_pe(pe):
            xT_ready(pe, 0)
            pe.wait_ge(s_route, 64)
            lgp = bank[0][:, 0:128].rearrange("p (t n) -> p t n", t=TT)[:, :, 0:NG + NE]
            for t in range(TT):
                for k in range(KT):
                    i = nc.tensor.matmul(lgp[:, t, :], xT[:, k, t * P:(t + 1) * P], route_w[:, k, :],
                                         start=(k == 0), stop=(k == KT - 1))
            i.then_inc(mo["logit"], 1)
            pe.wait_ge(mo["assign"], 1)
            rk = bank[1][:, 0:64].rearrange("p (t n) -> p t n", t=TT)
            nc.tensor.matmul(rk[:, 0, :], strict[:], A12[:, 0, :], start=True, stop=True)
            nc.tensor.matmul(rk[:, 1, :], strict[:], A12[:, 1, :], start=True, stop=False)
            nc.tensor.matmul(rk[:, 1, :], ones[:], A12[:, 0, :], start=False, stop=True)
            nc.tensor.matmul(bank[2][:, 0:NE], ones[:], A12[:, 0, :], start=True, stop=False)
            nc.tensor.matmul(bank[2][:, 0:NE], ones[:], A12[:, 1, :], start=False, stop=True).then_inc(mo["rank"], 1)
            pe.wait_ge(mo["pos"], 1)
            for k in range(KT):
                for t in range(TT):
                    i = nc.tensor.matmul(bank[k][:], x_tok[:, t, k * P:(k + 1) * P], onehot[:, t, :],
                                         start=(t == 0), stop=(t == TT - 1))
                i.then_inc(mo["gath"], 1)
            pe.wait_ge(mo["gath_ev"], KT)
            pe.wait_ge(mo["diag"], 1)
            for j in range(2):
                i = nc.tensor.matmul(bank[j][:], ones[:], rows_diag[:, 2 * j:2 * j + 2].rearrange("p v t j -> p (v t j)"),
                                     start=True, stop=True)
            i.then_inc(mo["rows"], 1)
            pe.wait_ge(mo["rows_sb"], 2)
            pe.wait_ge(mo["h0"], 1)

            def hidden(e, p, count):
                pe.wait_ge(mo["xe"], e + 1)
                for k in range(KT):
                    for j in range(2):
                        n = 6 * p + 2 * (k // 4) + j
                        if k % 4 == 0:
                            pe.wait_ge(landed[n], count)
                        i = nc.tensor.matmul(bank[4 + p][64 * j:64 * j + 64, :], xe[p][:, k, :], unit_view(n, 4)[:, k % 4, :],
                                             start=(k == 0), stop=(k == KT - 1))
                    if k % 4 == 3:
                        i.then_inc(mo["ha"] if k < 4 else mo["hb"], 1)

            def down(e, p, count):
                pe.wait_ge(mo["hT"], e + 1)
                for k in range(4):
                    n = 6 * p + 4 + k // 2
                    if k % 2 == 0:
                        pe.wait_ge(landed[n], count)
                    for j in range(2):
                        i = nc.tensor.matmul(bank[6][64 * j:64 * j + 64, :], hT_e[p][:, k, :],
                                             unit_view(n, 2)[:, k % 2, j * HALF:(j + 1) * HALF], start=(k == 0), stop=(k == 3))
                i.then_inc(mo["y"], 1)

            def turn(e, p):
                pe.wait_ge(mo["h"], e + 1)
                for k in range(4):
                    i = nc.tensor.transpose(bank[7][:, k * P:(k + 1) * P], h_e[:, k * P:(k + 1) * P], ident[:])
                i.then_inc(mo["tr"], 1)

            def combine(e, p, first=False, last=False):
                pe.wait_ge(mo["ysb"], e + 1)
                pe.wait_ge(mo["sel"], e + 1)
                for t in range(TT):
                    for j in range(2):
                        i = nc.tensor.matmul(bank[2 * t + j][:], pick_e[p][64 * j:64 * j + 64, t * P:(t + 1) * P],
                                             y_e[p][64 * j:64 * j + 64, :], start=first, stop=last, skip_group_check=True)
                    if last:
                        i.then_inc(G["ln_in"], 1)
                if not last:
                    i.then_inc(mo["comb"], 1)

            base = UA // RING
            for e in range(4):
                hidden(e, e % 2, 16 * (base + 1 + e // 2))
                if e >= 2:
                    combine(e - 2, e % 2, first=(e == 2))
                if e:
                    down(e - 1, 1 - e % 2, 16 * (base + 1 + (e - 1) // 2))
                turn(e, e % 2)
            with pe.Fori(2, NE // 2) as it:
                for p in range(2):
                    hidden(2 * it + p, p, 16 * (it + base + 1))
                    combine(2 * it + p - 2, p)
                    down(2 * it + p - 1, 1 - p, 16 * (it + base + p))
                    turn(2 * it + p, p)
            combine(NE - 2, 0)
            down(NE - 1, 1, 16 * (base + NE // 2))
            over = pe.value_load(start_i[0:1, NE:NE + 1])
            with pe.If(over > C):
                pe.sem_inc(ov["y"], 1)
                pe.sem_inc(ov["h"], 1)
                pe.sem_inc(ov["comb"], 1)
                for n, b, e in each_overflow(pe):
                    pe.wait_ge(ov["xe"], n + 1)
                    pe.wait_ge(ov["load"], 96 * (n + 1))
                    for k in range(KT):
                        for j in range(2):
                            i = nc.tensor.matmul(bank[4][64 * j:64 * j + 64, :], xe[0][:, k, :],
                                                 unit_view(2 * (k // 4) + j, 4)[:, k % 4, :], start=(k == 0), stop=(k == KT - 1))
                    i.then_inc(ov["h"], 1)
                    pe.wait_ge(ov["hm"], n + 1)
                    for k in range(4):
                        i = nc.tensor.transpose(bank[7][:, k * P:(k + 1) * P], h_e[:, k * P:(k + 1) * P], ident[:])
                    i.then_inc(ov["tr"], 1)
                    pe.wait_ge(ov["hT"], n + 1)
                    for k in range(4):
                        for j in range(2):
                            i = nc.tensor.matmul(bank[6][64 * j:64 * j + 64, :], hT_e[0][:, k, :],
                                                 unit_view(4 + k // 2, 2)[:, k % 2, j * HALF:(j + 1) * HALF],
                                                 start=(k == 0), stop=(k == 3))
                    i.then_inc(ov["y"], 1)
                    pe.wait_ge(ov["ysb"], n + 1)
                    pe.wait_ge(ov["sel"], n + 1)
                    for t in range(TT):
                        for j in range(2):
                            i = nc.tensor.matmul(bank[2 * t + j][:], pick_e[0][64 * j:64 * j + 64, t * P:(t + 1) * P],
                                                 y_e[0][64 * j:64 * j + 64, :], start=False, stop=False, skip_group_check=True)
                    i.then_inc(ov["comb"], 1)
            combine(NE - 1, 1, last=True)

        def moe_dve(dve, own):
            th = own.then
            dve.wait_ge(mo["logit"], 1)
            lgp = bank[0][:, 0:128].rearrange("p (t n) -> p t n", t=TT)[:, :, 0:NG + NE]
            for t in range(TT):
                own.did(nc.vector.tensor_tensor(lg[:, t, :], lgp[:, t, :], route_b[:], ALU.add))
            dve.wait_ge(own_dve, own.n)
            gl = lg[:, :, 0:NG]
            el = [lg[:, t, NG:].rearrange("p (g i) -> p g i", g=NG) for t in range(TT)]
            th(nc.vector.tensor_reduce(v_gmax, gl, AX_X, ALU.max))
            for t in range(TT):
                i = nc.vector.tensor_scalar(g_e[:, t, :], gl[:, t, :], v_gmax[:, t:t + 1], None, ALU.subtract)
            i.then_inc(mo["e1"], 1)

            def first_max(dst, values, vmax, n):
                for t in range(TT):
                    own.did(nc.vector.scalar_tensor_tensor(out=dst[:, t, :], in0=values[:, t, :], scalar=vmax[:, t:t + 1],
                                                           in1=i_8m[:, 0:n], op0=ALU.is_ge, op1=ALU.mult))
                dve.wait_ge(own_dve, own.n)
                th(nc.vector.tensor_reduce(v_m, dst, AX_X, ALU.min))
                for t in range(TT):
                    own.did(nc.vector.tensor_scalar(dst[:, t, :], dst[:, t, :], v_m[:, t:t + 1], None, ALU.is_equal))
                dve.wait_ge(own_dve, own.n)

            first_max(g_oh, gl, v_gmax, NG)
            for t in range(TT):
                own.did(nc.vector.tensor_tensor(tmp32[:, t], el[t], g_oh[:, t, :].unsqueeze(2).broadcast_to((P, NG, EPG)), ALU.mult))
            dve.wait_ge(own_dve, own.n)
            for t in range(TT):
                own.did(nc.vector.tensor_reduce(e_sel[:, t, :], tmp32[:, t].rearrange("p g i -> p i g"), AX_X, ALU.add))
            dve.wait_ge(own_dve, own.n)
            th(nc.vector.tensor_reduce(v_v1, e_sel, AX_X, ALU.max))
            first_max(oh[0], e_sel, v_v1, EPG)
            th(nc.vector.scalar_tensor_tensor(out=e_c, in0=oh[0], scalar=NEG, in1=e_sel, op0=ALU.mult, op1=ALU.add))
            th(nc.vector.tensor_reduce(v_v2, e_c, AX_X, ALU.max))
            first_max(oh[1], e_c, v_v2, EPG)
            nc.vector.tensor_tensor(v_ed, v_v2, v_v1, ALU.subtract).then_inc(mo["e2"], 1)
            for kk in range(2):
                for t in range(TT):
                    own.did(nc.vector.tensor_tensor(A1[kk][:, t], g_oh[:, t, :].unsqueeze(2).broadcast_to((P, NG, EPG)),
                                                    oh[kk][:, t, :].unsqueeze(1).broadcast_to((P, NG, EPG)), ALU.mult))
            dve.wait_ge(own_dve, own.n)
            flat = lambda v: v.rearrange("p t g i -> p (t g i)")
            a12 = A12.rearrange("p t n -> p (t n)")
            nc.vector.tensor_tensor(a12, flat(A1[0]), flat(A1[1]), ALU.add).then_inc(mo["assign"], 1)
            dve.wait_ge(mo["exp1"], 1)
            th(nc.vector.tensor_reduce(v_gsum, g_e, AX_X, ALU.add))
            th(nc.vector.reciprocal(v_ggate, v_gsum))
            dve.wait_ge(mo["exp2"], 1)
            th(nc.vector.tensor_scalar(v_p1, v_ed, 1.0, None, ALU.add))
            th(nc.vector.reciprocal(v_p1, v_p1))
            th(nc.vector.tensor_tensor(gates[0], v_p1, v_ggate, ALU.mult))
            th(nc.vector.tensor_tensor(gates[1], v_ed, gates[0], ALU.mult))
            dve.wait_ge(mo["rank"], 1)
            rk = v_rank
            own.did(nc.vector.tensor_copy(rk, bank[1][:, 0:64].rearrange("p (t n) -> p t n", t=TT)))
            th(nc.vector.tensor_tensor_scan(v_incl, ones[:, 0:NE], bank[2][:, 0:NE], 0.0, ALU.mult, ALU.add))
            th(nc.vector.tensor_tensor(v_start, v_incl, bank[2][:, 0:NE], ALU.subtract))
            own.did(nc.vector.tensor_copy(v_cnt, bank[2][:, 0:NE]))
            th(nc.vector.tensor_reduce(cmax, bank[2][:, 0:NE], AX_X, ALU.max))
            own.did(nc.vector.tensor_copy(start_i[0:1, 0:NE], v_start[0:1, :]))
            nc.vector.tensor_copy(start_i[0:1, NE:NE + 1], cmax[0:1, :]).then_inc(mo["start"], 1)
            for t in range(TT):
                own.did(nc.vector.tensor_tensor(v_q[:, t, :], rk[:, t, :], v_start, ALU.add))
            dve.wait_ge(own_dve, own.n)
            for kk in range(2):
                th(nc.vector.tensor_tensor(v_t, v_q, A1[kk].rearrange("p t g i -> p t (g i)"), ALU.mult))
                th(nc.vector.tensor_reduce(v_pos[kk], v_t, AX_X, ALU.add))
            for t in range(TT):
                th(nc.vector.tensor_scalar(onehot[:, t, :], iota_s[:], v_pos[0][:, t:t + 1], None, ALU.is_equal))
                i = nc.vector.scalar_tensor_tensor(out=onehot[:, t, :], in0=iota_s[:], scalar=v_pos[1][:, t:t + 1],
                                                   in1=onehot[:, t, :], op0=ALU.is_equal, op1=ALU.add)
            i.then_inc(mo["pos"], 1)
            own.did(nc.vector.memset(xs[:, :, SLOTS:], 0.0))
            for k in range(1, KT, 2):
                dve.wait_ge(mo["gath"], k + 1)
                nc.vector.tensor_scalar(xs[:, k, 0:SLOTS], bank[k][:], gbT[:, k:k + 1], gbT[:, 64 + k:65 + k],
                                        ALU.mult, ALU.add).then_inc(mo["gath_ev"], 1)

            for v, val in enumerate((v_pos[0], v_pos[1], gates[0], gates[1])):
                i = nc.vector.tensor_tensor(rows_diag[:, v], ident[:].unsqueeze(1).broadcast_to((P, TT, P)),
                                            val.unsqueeze(2).broadcast_to((P, TT, P)), ALU.mult)
            i.then_inc(mo["diag"], 1)
            for b in range(BLOCKS):
                own.did(nc.vector.tensor_scalar(place[:, b, :], v_start, slot_p, float(C * b), ALU.add, ALU.add))
                own.did(nc.vector.tensor_scalar(v_full, v_cnt, float(-C * b), slot_p, ALU.add, ALU.is_gt))
                dve.wait_ge(own_dve, own.n)
                th(nc.vector.scalar_tensor_tensor(out=place[:, b, :], in0=place[:, b, :], scalar=1.0, in1=v_full,
                                                  op0=ALU.add, op1=ALU.mult))
                th(nc.vector.tensor_scalar(place[:, b, :], place[:, b, :], -1.0, None, ALU.add))
            dve.wait_ge(mo["rows"], 1)
            for j in range(2):
                nc.vector.tensor_copy(rows_b[:, 2 * j:2 * j + 2, :], bank[j][:].rearrange("p (v t) -> p v t", v=2)) \
                    .then_inc(mo["rows_sb"], 1)
            nc.vector.memset(h_e[0:64, :], 0.0).then_inc(mo["h0"], 1)
            dve.wait_ge(mo["rows_sb"], 2)

            def select(e, p):
                at_e = place[:, 0, e:e + 1] if isinstance(e, int) else place[:, 0, bass.ds(e, 1)]
                nc.vector.scalar_tensor_tensor(out=pick_e[p], in0=rows_b[:, 0, :], scalar=at_e, in1=rows_b[:, 2, :],
                                               op0=ALU.is_equal, op1=ALU.mult).then_inc(own_sel, 1)
                nc.vector.scalar_tensor_tensor(out=sel_tmp, in0=rows_b[:, 1, :], scalar=at_e, in1=rows_b[:, 3, :],
                                               op0=ALU.is_equal, op1=ALU.mult).then_inc(own_sel, 1)

            def select_sum(p, s):
                nc.vector.tensor_tensor(pick_e[p], pick_e[p], sel_tmp, ALU.add).then_inc(s, 1)

            def expert(e, p, first=False):
                if not first:
                    dve.wait_ge(mo["comb"], e - 1)
                select(e, p)
                dve.wait_ge(own_sel, 2 * e + 2)
                select_sum(p, mo["sel"])
                dve.wait_ge(mo["silu"], e + 1)
                nc.vector.tensor_tensor(h_e[64:128, :], sil_e[64:128, :], bank[4 + p][64:128, :], ALU.mult).then_inc(mo["h"], 1)
                dve.wait_ge(mo["tr"], e + 1)
                nc.vector.tensor_copy(hT_e[p], bank[7][:].rearrange("p (k c) -> p k c", k=4)[:, :, C:]).then_inc(mo["hT"], 1)

            expert(0, 0, True)
            expert(1, 1, True)
            with dve.Fori(1, NE // 2) as it:
                for p in range(2):
                    expert(2 * it + p, p)
            over = dve.value_load(start_i[0:1, NE:NE + 1])
            with dve.If(over > C):
                dve.wait_ge(mo["comb"], NE - 1)
                for n, b, e in each_overflow(dve):
                    dve.wait_ge(ov["comb"], n + 1)
                    at_b = place.rearrange("p b e -> p (b e)")[:, bass.ds(n + NE, 1)]
                    nc.vector.scalar_tensor_tensor(out=pick_e[0], in0=rows_b[:, 0, :], scalar=at_b, in1=rows_b[:, 2, :],
                                                   op0=ALU.is_equal, op1=ALU.mult).then_inc(own_sel, 1)
                    nc.vector.scalar_tensor_tensor(out=sel_tmp, in0=rows_b[:, 1, :], scalar=at_b, in1=rows_b[:, 3, :],
                                                   op0=ALU.is_equal, op1=ALU.mult).then_inc(own_sel, 1)
                    dve.wait_ge(own_sel, 2 * NE + 2 * n + 2)
                    select_sum(0, ov["sel"])
                    dve.wait_ge(ov["silu"], n + 1)
                    nc.vector.tensor_tensor(h_e[64:128, :], sil_e[64:128, :], bank[4][64:128, :], ALU.mult).then_inc(ov["hm"], 1)
                    dve.wait_ge(ov["tr"], n + 1)
                    nc.vector.tensor_copy(hT_e[0], bank[7][:].rearrange("p (k c) -> p k c", k=4)[:, :, C:]).then_inc(ov["hT"], 1)
            ffn_first_dve(dve, 0)

        def moe_act(act):
            act.wait_ge(mo["e1"], 1)
            nc.scalar.activation(g_e, g_e, ACT.Exp).then_inc(mo["exp1"], 1)
            act.wait_ge(mo["e2"], 1)
            nc.scalar.activation(v_ed, v_ed, ACT.Exp).then_inc(mo["exp2"], 1)
            for k in range(0, KT, 2):
                act.wait_ge(mo["gath"], k + 1)
                nc.scalar.activation(xs[:, k, 0:SLOTS], bank[k][:], ACT.Identity, scale=gbT[:, k:k + 1],
                                     bias=gbT[:, 64 + k:65 + k]).then_inc(mo["gath_ev"], 1)

            def gate(e, p):
                act.wait_ge(mo["hb"], e + 1)
                nc.scalar.activation(sil_e[64:128, :], bank[4 + p][0:64, :], ACT.Silu).then_inc(mo["silu"], 1)

            def keep(e, p, first=False):
                act.wait_ge(mo["y"], e + 1)
                if not first:
                    act.wait_ge(mo["comb"], e - 1)
                nc.scalar.activation(y_e[p], bank[6][:], ACT.Copy).then_inc(mo["ysb"], 1)

            gate(0, 0)
            gate(1, 1)
            keep(0, 0, True)
            gate(2, 0)
            keep(1, 1, True)
            gate(3, 1)
            keep(2, 0)
            with act.Fori(2, NE // 2) as it:
                for p in range(2):
                    gate(2 * it + p, p)
                    keep(2 * it + p - 1, 1 - p)
            keep(NE - 1, 1)
            over = act.value_load(start_i[0:1, NE:NE + 1])
            with act.If(over > C):
                act.wait_ge(mo["comb"], NE - 1)
                for n, b, e in each_overflow(act):
                    act.wait_ge(ov["h"], n + 2)
                    nc.scalar.activation(sil_e[64:128, :], bank[4][0:64, :], ACT.Silu).then_inc(ov["silu"], 1)
                    act.wait_ge(ov["y"], n + 2)
                    act.wait_ge(ov["comb"], n + 1)
                    nc.scalar.activation(y_e[0], bank[6][:], ACT.Copy).then_inc(ov["ysb"], 1)

        def moe_pool(pool, own):
            pool.wait_ge(mo["start"], 1)
            pool.wait_ge(mo["gath_ev"], KT)

            def pick(e, p):
                at = pool.value_load(start_i[0:1, bass.ds(e, 1)] if not isinstance(e, int) else start_i[0:1, e:e + 1],
                                     min_val=0, max_val=SLOTS)
                nc.gpsimd.tensor_copy(xe[p], xs[:, :, bass.ds(at, C)]).then_inc(mo["xe"], 1)

            pick(0, 0)
            pick(1, 1)
            with pool.Fori(1, NE // 2) as it:
                for p in range(2):
                    pool.wait_ge(mo["hb"], 2 * it + p - 1)
                    pick(2 * it + p, p)
            over = pool.value_load(start_i[0:1, NE:NE + 1])
            with pool.If(over > C):
                pool.wait_ge(mo["hb"], NE)
                for n, b, e in each_overflow(pool):
                    pool.wait_ge(ov["h"], n + 1)
                    at = pool.value_load(start_i[0:1, bass.ds(e, 1)], min_val=0, max_val=SLOTS)
                    nc.gpsimd.tensor_copy(xe[0], xs[:, :, bass.ds(at + C * b, C)]).then_inc(ov["xe"], 1)

        pairs = ((0, 0), (0, 1), (1, 0))
        xp_ = (x_hi, x_lo)
        hp_ = (h_hi, h_lo)

        def place_of(kind, s_):
            return split[1] if kind == 2 and s_ == NSTEP - 1 else split[kind]

        def split_act(act, f, kind, s_):
            n = at_unit["f", f, kind, s_]
            here(act, n)
            if kind == 2 and s_ == NSTEP - 1:
                act.wait_ge(f_mm[1], NSTEP * (f + 1))
            elif NSTEP * f + s_ > 0:
                act.wait_ge(f_mm[kind], NSTEP * f + s_)
            if kind == 1 and s_ == 0 and f > 0:
                act.wait_ge(f_mm[2], NSTEP * f)
            nc.scalar.activation(place_of(kind, s_)[0][:], unit(n), ACT.Copy).then_inc(f_hi[kind], 1)

        def split_dve(dve, f, kind, s_):
            n = at_unit["f", f, kind, s_]
            dve.wait_ge(f_hi[kind], NSTEP * f + s_ + 1)
            hi, lo = place_of(kind, s_)
            nc.vector.tensor_tensor(lo[:], unit(n), hi[:].bitcast(F32), ALU.subtract) \
                .then_inc(f_lo[kind], 1)

        def ffn_first_act(act, f):
            split_act(act, f, 0, 0)

        def ffn_first_dve(dve, f):
            split_dve(dve, f, 0, 0)

        def ffn_act(act, f):
            split_act(act, f, 1, 0)
            for s_ in range(NSTEP):
                c = NSTEP * f + s_
                act.wait_ge(f_mm[0], c + 1)
                if c:
                    act.wait_ge(f_h, c)
                nc.scalar.activation(silu, bank[4 + 2 * (s_ % 2)][:].rearrange("p (a t) -> p a t", a=2),
                                     ACT.Silu).then_inc(f_silu, 1)
                if s_ < NSTEP - 1:
                    split_act(act, f, 0, s_ + 1)
                act.wait_ge(f_h, c + 1)
                nc.scalar.activation(h_hi[:, s_ % 2], h_raw, ACT.Copy).then_inc(f_hhi, 1)
                if s_ < NSTEP - 1:
                    split_act(act, f, 1, s_ + 1)
                split_act(act, f, 2, s_)

        def ffn_dve(dve, f):
            split_dve(dve, f, 1, 0)
            for s_ in range(NSTEP):
                c = NSTEP * f + s_
                if s_ < NSTEP - 1:
                    split_dve(dve, f, 0, s_ + 1)
                dve.wait_ge(f_silu, c + 1)
                dve.wait_ge(f_mm[1], c + 1)
                if c:
                    dve.wait_ge(f_hhi, c)
                    dve.wait_ge(f_hlo, c)
                nc.vector.scalar_tensor_tensor(out=h_raw, in0=silu, scalar=0.5,
                                               in1=bank[5 + 2 * (s_ % 2)][:].rearrange("p (a t) -> p a t", a=2),
                                               op0=ALU.mult, op1=ALU.mult).then_inc(f_h, 1)
                dve.wait_ge(f_hhi, c + 1)
                nc.vector.tensor_tensor(h_lo[:, s_ % 2], h_raw, h_hi[:, s_ % 2].bitcast(F32), ALU.subtract).then_inc(f_hlo, 1)
                if s_ < NSTEP - 1:
                    split_dve(dve, f, 1, s_ + 1)
                split_dve(dve, f, 2, s_)

        def ffn_pe(pe, f, L):
            n_split = SPLIT_NORMS.index(L)

            def up(kind, s_, c):
                pe.wait_ge(f_lo[kind], c + 1)
                for m in range(2):
                    for k in range(KT):
                        if s_ == 0 and kind == 0 and m == 0 and k % 2 == 0:
                            pe.wait_ge(G["ln_lo"], 4 * n_split + k // 2 + 1)
                        for j, (a, b) in enumerate(pairs):
                            w = split[kind][a][:, k * FSTEP + m * P:k * FSTEP + (m + 1) * P]
                            i = nc.tensor.matmul(bank[4 + 2 * (s_ % 2) + kind][:, m * T:(m + 1) * T], w, xp_[b][:, k, :],
                                                 start=(k == 0 and j == 0), stop=(k == KT - 1 and j == 2))
                i.then_inc(f_mm[kind], 1)

            def down(s_, c, first=False, last=False):
                weights = split[1] if last else split[2]
                pe.wait_ge(f_hlo, c + 1)
                pe.wait_ge(f_lo[2], c + 1)
                for t in range(TT):
                    for k in range(2):
                        for j, (a, b) in enumerate(pairs):
                            for hf in range(2):
                                w = weights[b][:, k * D + hf * HALF:k * D + (hf + 1) * HALF]
                                i = nc.tensor.matmul(bank[2 * t + hf][:], hp_[a][:, s_ % 2, k, t * P:(t + 1) * P], w,
                                                     start=(first and k == 0 and j == 0), stop=(last and k == 1 and j == 2))
                    if last:
                        i.then_inc(G["ln_in"], 1)
                if not last:
                    i.then_inc(f_mm[2], 1)

            base = NSTEP * f
            for s_ in range(3):
                up(0, s_, base + s_)
                up(1, s_, base + s_)
                if s_:
                    down(s_ - 1, base + s_ - 1, first=(s_ == 1))
            with pe.Fori(0, (NSTEP - 3) // 2) as it:
                for q in range(2):
                    c = base + 3 + 2 * it + q
                    up(0, 3 + q, c)
                    up(1, 3 + q, c)
                    down(2 + q, c - 1)
            down(NSTEP - 1, base + NSTEP - 1, last=True)
            pe.sem_inc(f_mm[2], 1)

        gate_w = sb("ml_gate_w", [P, KT, 16])
        gate_b = sb("ml_gate_b", [P, 16])
        sink = sb("at_sink", [P, NH])
        MS = sb("ml_small", [P, 192])
        mask = x_parts[:, 0:768].rearrange("p (d c) -> p d c", d=2)
        q_T = arena[:, 0:1024].rearrange("p (h t) -> p h t", h=MLH)
        k_T = arena[:, 1024:2048].rearrange("p (h t) -> p h t", h=MLH)
        v_tok = arena[:, 2048:4096].rearrange("p (t d) -> p t d", t=TT)
        o_t = arena[:, 4096:6144].rearrange("p (t d) -> p t d", t=TT)
        Wb = [arena[:, 6144 + i * 1024:7168 + i * 1024].rearrange("p (t d s) -> p t d s", t=TT, d=2) for i in range(2)]
        diag = arena[:, 6144:8192].rearrange("p (t c j) -> p t c j", t=TT, c=8)
        p_tot = [arena[:, 8192 + i * 512:8704 + i * 512].rearrange("p (t s) -> p t s", t=TT) for i in range(2)]
        p_T = [arena[:, 9216 + i * 512:9728 + i * 512].rearrange("p (s j) -> p s j", s=TT) for i in range(2)]
        y_T = arena[:, 10240:12288].rearrange("p (k t) -> p k t", k=KT)
        h_tok = xT[:].rearrange("p k t -> p (k t)").rearrange("p (t d) -> p t d", t=TT)
        B_bank = (6, 7, 0, 1)

        def ms(a, *shape):
            n = int(np.prod(shape))
            v = MS[:, a:a + n]
            return v.rearrange("p (a b) -> p a b", b=shape[1]) if len(shape) == 2 else \
                v.rearrange("p (a b c) -> p a b c", b=shape[1], c=shape[2]) if len(shape) == 3 else v

        gp = MS[:, 0:32].rearrange("p (t d w h) -> p t d w h", t=TT, d=2, w=2)
        gp_t = ms(0, TT, 16)
        af, lg1, logf = ms(32, TT, 2, MLH), ms(48, TT, 2, MLH), ms(64, TT, 2, MLH)
        gcum, b_t = ms(80, TT, 2, MLH), ms(96, TT, 2, MLH)
        mx = [ms(112 + 4 * i, TT, 2) for i in range(2)]
        n_m = [ms(120 + 4 * i, TT, 2) for i in range(2)]
        floor = [ms(128 + 4 * i, TT, 2) for i in range(2)]
        den = [ms(136 + 4 * i, TT, 2) for i in range(2)]
        ng_half = MS[:, 144:152]
        mv4 = ms(152, TT, 2)
        ve4, rs4 = ms(156, TT), ms(158, TT)
        AS = sb("at_small", [P, 192])
        a_mx = AS[:, 0:4].rearrange("p (q t) -> p q t", q=2)
        a_nm = AS[:, 8:40].rearrange("p (t h) -> p t h", t=TT)
        a_sum = AS[:, 40:72].rearrange("p (t h) -> p t h", t=TT)
        a_ds = AS[:, 72:104].rearrange("p (t h) -> p t h", t=TT)
        a_rec = AS[:, 104:136].rearrange("p (t h) -> p t h", t=TT)
        a_nsink = AS[:, 136:152]

        ML_U = lambda n: at_unit["ml", n]

        def ml_pe(pe):
            xT_ready(pe, 2)
            pe.wait_ge(ml["param"], 48)
            for t in range(TT):
                for k in range(KT):
                    i = nc.tensor.matmul(bank[0][:, t * 16:(t + 1) * 16], xT[:, k, t * P:(t + 1) * P], gate_w[:, k, :],
                                         start=(k == 0), stop=(k == KT - 1))
            i.then_inc(ml["gp"], 1)

            def heads(u0, banks, s):
                for j in range(2):
                    here(pe, ML_U(u0 + j))
                for h in range(MLH):
                    for k in range(KT):
                        w = unit_view(ML_U(u0 + k // 4), 4)[:, k % 4, h * P:(h + 1) * P]
                        i = nc.tensor.matmul(bank[banks[h // 2]][:, (h % 2) * T:(h % 2) * T + T], w, xT[:, k, :],
                                             start=(k == 0), stop=(k == KT - 1))
                    if h % 2:
                        i.then_inc(s, 1)

            def rows(u0, banks, s, free):
                for hf in range(2):
                    for j in range(2):
                        here(pe, ML_U(u0 + 2 * hf + j))
                    for t in range(TT):
                        if free and free[2 * hf + t]:
                            pe.wait_ge(*free[2 * hf + t])
                        for k in range(KT):
                            w = unit_view(ML_U(u0 + 2 * hf + k // 4), 4)[:, k % 4, :]
                            i = nc.tensor.matmul(bank[banks[2 * hf + t]][:], xT[:, k, t * P:(t + 1) * P], w,
                                                 start=(k == 0), stop=(k == KT - 1))
                        i.then_inc(s, 1)

            heads(0, (1, 2), ml["q"])
            pe.wait_ge(ml["logf"], 1)
            for d in range(2):
                for t in range(TT):
                    o = bank[0][:, 64 + t * 8 + d * 4:68 + t * 8 + d * 4]
                    m = upper if d == 0 else lower
                    other = t != d
                    i = nc.tensor.matmul(o, m[:], logf[:, t, d, :], start=True, stop=not other)
                    if other:
                        i = nc.tensor.matmul(o, ones[:], logf[:, 1 - t, d, :], start=False, stop=True)
            i.then_inc(ml["cum"], 1)
            heads(2, (3, 4), ml["k"])
            rows(4, (5, 6, 7, 1), ml["v"], (None, None, None, (ml["qs"], 1)))
            rows(8, (2, 3, 4, 5), ml["o"], ((ml["qs"], 2), (ml["ks"], 1), (ml["ks"], 2), (ml["vs"], 1)))
            pe.wait_ge(ml["diag"], 2)
            pe.wait_ge(ml["vs"], 4)
            for h in range(MLH):
                for d in range(2):
                    for t in range(TT):
                        i = nc.tensor.matmul(bank[B_bank[h]][:, d * T + t * P:d * T + t * P + P], ones[:],
                                             diag[:, t, 4 * d + h, :], start=True, stop=True)
                i.then_inc(ml["b"], 1)
            pe.wait_ge(ml["os"], 4)

            def scores(h):
                for t in range(TT):
                    i = nc.tensor.matmul(bank[2 + h % 2][:, t * T:(t + 1) * T], q_T[:, h, t * P:(t + 1) * P], k_T[:, h, :],
                                         start=True, stop=True)
                i.then_inc(ml["s"], 1)

            scores(0)
            for h in range(MLH):
                if h + 1 < MLH:
                    scores(h + 1)
                pe.wait_ge(ml["p"], h + 1)
                for s_ in range(TT):
                    for t in range(TT):
                        i = nc.tensor.transpose(bank[4][:, s_ * T + t * P:s_ * T + t * P + P],
                                                p_tot[h % 2][:, t, s_ * P:(s_ + 1) * P], ident[:])
                i.then_inc(ml["tr"], 1)
                pe.wait_ge(ml["pt"], h + 1)
                if h >= 2:
                    pe.wait_ge(ml["h3"], h - 1)
                for t in range(TT):
                    for s_ in range(TT):
                        i = nc.tensor.matmul(bank[(5, 6)[h % 2]][:, t * T:(t + 1) * T], p_T[h % 2][:, s_, t * P:(t + 1) * P],
                                             v_tok[:, s_, h * DV:(h + 1) * DV], start=(s_ == 0), stop=(s_ == 1))
                i.then_inc(ml["h"], 1)
            pe.wait_ge(ml["y"], MLH)
            branch_out(pe, h_tok, "ml", 12, 0)

        def branch_out(pe, rows, name, u0, m):
            for k in range(KT):
                for t in range(TT):
                    i = nc.tensor.transpose(bank[4 + k // 2][:, (k % 2) * T + t * P:(k % 2) * T + t * P + P],
                                            rows[:, t, k * P:(k + 1) * P], ident[:])
                if k % 2:
                    i.then_inc(mx_tr, 1)
            yT_ = y_T if name == "ml" else y_Ta
            for u in range(4):
                here(pe, at_unit[name, u0 + u])
                pe.wait_ge(mx_dve if u % 2 else mx_act, 2 * m + u // 2 + 1)
                w = unit_view(at_unit[name, u0 + u], 2)
                for k in range(2):
                    for t in range(TT):
                        for hf in range(2):
                            i = nc.tensor.matmul(bank[2 * t + hf][:], yT_[:, 2 * u + k, t * P:(t + 1) * P],
                                                 w[:, k, hf * HALF:(hf + 1) * HALF], start=(u == 0 and k == 0),
                                                 stop=(u == 3 and k == 1))
                        if u == 3 and k == 1:
                            i.then_inc(G["ln_in"], 1)
                if u < 3:
                    i.then_inc(mx_used, 1)

        def ml_act(act):
            act.wait_ge(ml["af"], 1)
            nc.scalar.activation(lg1, af, ACT.Exp, scale=-1.0).then_inc(ml["exp0"], 1)
            act.wait_ge(ml["exp0"], 1)
            nc.scalar.activation(lg1, lg1, ACT.Ln, bias=1.0).then_inc(ml["l"], 1)
            for j in range(2):
                act.wait_ge(ml["q"], j + 1)
                nc.scalar.activation(q_T[:, 2 * j:2 * j + 2, :], bank[1 + j][:].rearrange("p (a t) -> p a t", a=2),
                                     ACT.Copy).then_inc(ml["qs"], 1)
            for j in range(4):
                hf, t = j // 2, j % 2
                act.wait_ge(ml["o"], j + 1)
                nc.scalar.activation(o_t[:, t, hf * HALF:(hf + 1) * HALF], bank[2 + j][:], ACT.Tanh, scale=0.5).then_inc(ml["os"], 1)

            def exps(h):
                act.wait_ge(ml["nm"], h + 1)
                for t in range(TT):
                    for d in range(2):
                        nc.scalar.activation(Wb[h % 2][:, t, d, :], Wb[h % 2][:, t, d, :], ACT.Exp,
                                             bias=n_m[h % 2][:, t, d:d + 1])
                nc.scalar.activation(floor[h % 2], floor[h % 2], ACT.Exp).then_inc(ml["exp"], 1)

            exps(0)
            exps(1)
            for h in range(MLH):
                act.wait_ge(ml["tr"], h + 1)
                nc.scalar.activation(p_T[h % 2], bank[4][:].rearrange("p (s j) -> p s j", s=TT), ACT.Copy).then_inc(ml["pt"], 1)
                if h + 2 < MLH:
                    exps(h + 2)
            for b in (0, 2):
                act.wait_ge(mx_tr, b + 1)
                for k in (2 * b, 2 * b + 1):
                    i = nc.scalar.activation(y_T[:, k, :], bank[4 + b][:, (k % 2) * T:(k % 2) * T + T], ACT.Copy,
                                             scale=ng_half[:, k:k + 1])
                i.then_inc(mx_act, 1)

        def ml_dve(dve, own):
            th = own.then
            own.did(nc.vector.tensor_scalar(ng_half, ngT[:], 0.5, None, ALU.mult))
            dve.wait_ge(ml["gp"], 1)
            for t in range(TT):
                own.did(nc.vector.tensor_tensor(gp_t[:, t, :], bank[0][:, t * 16:(t + 1) * 16], gate_b[:], ALU.add))
            dve.wait_ge(own_dve, own.n)
            for t in range(TT):
                i = nc.vector.scalar_tensor_tensor(out=af[:, t], in0=gp[:, t, :, 1, :], scalar=-1.0, in1=gp[:, t, :, 1, :],
                                                   op0=ALU.mult, op1=ALU.max)
            i.then_inc(ml["af"], 1)
            dve.wait_ge(ml["l"], 1)
            for t in range(TT):
                i = nc.vector.scalar_tensor_tensor(out=logf[:, t], in0=gp[:, t, :, 1, :], scalar=0.0, in1=lg1[:, t],
                                                   op0=ALU.min, op1=ALU.subtract)
            i.then_inc(ml["logf"], 1)
            dve.wait_ge(ml["cum"], 1)
            th(nc.vector.tensor_copy(gcum, bank[0][:, 64:80].rearrange("p (t d h) -> p t d h", t=TT, d=2)))
            for t in range(TT):
                own.did(nc.vector.tensor_tensor(b_t[:, t], gp[:, t, :, 0, :], gcum[:, t], ALU.subtract))
            dve.wait_ge(own_dve, own.n)
            for t in range(TT):
                bt = b_t[:, t].rearrange("p d h -> p (d h)")
                nc.vector.tensor_tensor(diag[:, t], ident[:].unsqueeze(1).broadcast_to((P, 8, P)),
                                        bt.unsqueeze(2).broadcast_to((P, 8, P)), ALU.mult).then_inc(ml["diag"], 1)
            for j in range(2):
                dve.wait_ge(ml["k"], j + 1)
                nc.vector.tensor_copy(k_T[:, 2 * j:2 * j + 2, :], bank[3 + j][:].rearrange("p (a t) -> p a t", a=2)).then_inc(ml["ks"], 1)
            for j in range(4):
                hf, t = j // 2, j % 2
                dve.wait_ge(ml["v"], j + 1)
                nc.vector.tensor_copy(v_tok[:, t, hf * HALF:(hf + 1) * HALF], bank[(5, 6, 7, 1)[j]][:]).then_inc(ml["vs"], 1)

            def weights(h):
                q = h % 2
                if h == 0:
                    dve.wait_ge(ml["mask"], 2)
                    dve.wait_ge(ml["b"], MLH)
                if h >= 2:
                    dve.wait_ge(ml["p"], h - 1)
                for t in range(TT):
                    off = P * (1 - t)
                    own.did(nc.vector.tensor_tensor(Wb[q][:, t], bank[B_bank[h]][:].rearrange("p (d s) -> p d s", d=2),
                                                    mask[:, :, off:off + T], ALU.add))
                dve.wait_ge(own_dve, own.n)
                th(nc.vector.tensor_reduce(mx[q], Wb[q], AX_X, ALU.max))
                own.did(nc.vector.tensor_scalar(n_m[q], mx[q], 0.0, -1.0, ALU.max, ALU.mult))
                dve.wait_ge(own_dve, own.n)
                nc.vector.tensor_tensor(floor[q], n_m[q], gcum[:, :, :, h], ALU.subtract).then_inc(ml["nm"], 1)

            def probs(h):
                q = h % 2
                dve.wait_ge(ml["exp"], h + 1)
                dve.wait_ge(ml["s"], h + 1)
                for t in range(TT):
                    for d in range(2):
                        w = Wb[q][:, t, d, :]
                        own.did(nc.vector.scalar_tensor_tensor(out=w, in0=bank[2 + q][:, t * T:(t + 1) * T], scalar=DQK ** -0.5,
                                                               in1=w, op0=ALU.mult, op1=ALU.mult,
                                                               accum_out=den[q][:, t, d:d + 1]))
                dve.wait_ge(own_dve, own.n)
                own.did(nc.vector.tensor_tensor(floor[q], floor[q], den[q], ALU.max))
                dve.wait_ge(own_dve, own.n)
                th(nc.vector.scalar_tensor_tensor(out=den[q], in0=den[q], scalar=-1.0, in1=floor[q], op0=ALU.mult, op1=ALU.max))
                th(nc.vector.reciprocal(den[q], den[q]))
                for t in range(TT):
                    own.did(nc.vector.tensor_scalar(p_tot[q][:, t, :], Wb[q][:, t, 0, :], den[q][:, t, 0:1], None, ALU.mult))
                dve.wait_ge(own_dve, own.n)
                for t in range(TT):
                    i = nc.vector.scalar_tensor_tensor(out=p_tot[q][:, t, :], in0=Wb[q][:, t, 1, :], scalar=den[q][:, t, 1:2],
                                                       in1=p_tot[q][:, t, :], op0=ALU.mult, op1=ALU.add)
                i.then_inc(ml["p"], 1)

            def head_norm(h):
                dve.wait_ge(ml["h"], h + 1)
                for t in range(TT):
                    own.did(nc.vector.bn_stats(stats[:, t, 0, :], bank[(5, 6)[h % 2]][:, t * T:(t + 1) * T]))
                dve.wait_ge(own_dve, own.n)
                for t in range(TT):
                    own.did(nc.vector.bn_aggr(mv4[:, t, :], stats[:, t, 0, :]))
                dve.wait_ge(own_dve, own.n)
                nc.vector.tensor_scalar(ve4, mv4[:, :, 1], EPS, None, ALU.add).then_inc(ml["ve"], 1)
                dve.wait_ge(ml["rs"], h + 1)
                for t in range(TT):
                    i = nc.vector.tensor_scalar(h_tok[:, t, h * DV:(h + 1) * DV], bank[(5, 6)[h % 2]][:, t * T:(t + 1) * T], mv4[:, t, 0:1],
                                                rs4[:, t:t + 1], ALU.subtract, ALU.mult)
                i.then_inc(ml["h3"], 1)
                dve.wait_ge(ml["h3"], h + 1)
                for t in range(TT):
                    v = h_tok[:, t, h * DV:(h + 1) * DV]
                    i = nc.vector.scalar_tensor_tensor(out=v, in0=o_t[:, t, h * DV:(h + 1) * DV], scalar=1.0, in1=v,
                                                       op0=ALU.add, op1=ALU.mult)
                i.then_inc(ml["y"], 1)

            weights(0)
            weights(1)
            for h in range(MLH):
                probs(h)
                if h + 2 < MLH:
                    weights(h + 2)
                if h:
                    head_norm(h - 1)
            head_norm(MLH - 1)
            for b in (1, 3):
                dve.wait_ge(mx_tr, b + 1)
                for k in (2 * b, 2 * b + 1):
                    i = nc.vector.tensor_scalar(y_T[:, k, :], bank[4 + b][:, (k % 2) * T:(k % 2) * T + T], ng_half[:, k:k + 1],
                                                None, ALU.mult)
                i.then_inc(mx_dve, 1)

        def ml_pool(pool, own):
            own.did(nc.gpsimd.memset(mask, 0.0))
            pool.wait_ge(own_pool, own.n)
            nc.gpsimd.affine_select(out=mask[:, 0, :], in_=mask[:, 0, :], compare_op=ALU.is_ge, fill=NEG, base=P,
                                    pattern=[[-1, 3 * P]], channel_multiplier=1).then_inc(ml["mask"], 1)
            nc.gpsimd.affine_select(out=mask[:, 1, :], in_=mask[:, 1, :], compare_op=ALU.is_ge, fill=NEG, base=-P,
                                    pattern=[[1, 3 * P]], channel_multiplier=-1).then_inc(ml["mask"], 1)
            for h in range(MLH):
                pool.wait_ge(ml["ve"], h + 1)
                nc.gpsimd.tensor_tensor(rs4, ve4, neg_half[:, 0:TT], ALU.pow).then_inc(ml["rs"], 1)

        qa_T = arena[:, 0:2048].rearrange("p (c t) -> p c t", c=8)
        ka_T = arena[:, 2048:3072].rearrange("p (g t) -> p g t", g=NKV)
        va_t = arena[:, 3072:3584].rearrange("p (t d) -> p t d", t=TT)
        NSB = 3
        pr = [arena[:, 3584 + i * 512:4096 + i * 512].rearrange("p (t s) -> p t s", t=TT) for i in range(NSB)]
        pa_T = [arena[:, 5120 + i * 512:5632 + i * 512].rearrange("p (s j) -> p s j", s=TT) for i in range(2)]
        o_tok = arena[:, 6144:8192].rearrange("p (t d) -> p t d", t=TT)
        y_Ta = arena[:, 8192:10240].rearrange("p (k t) -> p k t", k=KT)
        dist = x_parts[:, 0:384]
        dist_far = x_parts[:, 384:768]
        AT_U = lambda n: at_unit["at", n]

        def at_pe(pe):
            xT_ready(pe, 5)
            for j in range(2):
                here(pe, AT_U(j))
            kv = lambda k: unit_view(AT_U(k // 4), 4)[:, k % 4, :]
            for g in range(NKV):
                for k in range(KT):
                    for j in range(2):
                        i = nc.tensor.matmul(bank[g // 2][64 * j:64 * j + 64, (g % 2) * T:(g % 2) * T + T],
                                             kv(k)[:, g * HD:(g + 1) * HD], xT[:, k, :], start=(k == 0), stop=(k == KT - 1))
                if g % 2:
                    i.then_inc(at["k"], 1)
            for t in range(TT):
                for k in range(KT):
                    i = nc.tensor.matmul(bank[2][:, t * T:(t + 1) * T], xT[:, k, t * P:(t + 1) * P], kv(k)[:, 256:512],
                                         start=(k == 0), stop=(k == KT - 1))
            i.then_inc(at["v"], 1)
            for c in range(8):
                if c % 4 == 0:
                    for j in range(2):
                        here(pe, AT_U(2 + 2 * (c // 4) + j))
                for k in range(KT):
                    w = unit_view(AT_U(2 + 2 * (c // 4) + k // 4), 4)[:, k % 4, (c % 4) * P:(c % 4) * P + P]
                    i = nc.tensor.matmul(bank[3 + c // 2][:, (c % 2) * T:(c % 2) * T + T], w, xT[:, k, :],
                                         start=(k == 0), stop=(k == KT - 1))
                if c % 2:
                    i.then_inc(at["q"], 1)

            def scores(h):
                if h == 0:
                    pe.wait_ge(at["ka"], 1)
                    pe.wait_ge(at["kd"], 1)
                c, r0, g = h // 2, (h % 2) * HD, h // 4
                pe.wait_ge(at["qa"] if c // 2 % 2 == 0 else at["qd"], c // 4 + 1)
                for t in range(TT):
                    i = nc.tensor.matmul(bank[h % 2][:, t * T:(t + 1) * T], qa_T[r0:r0 + HD, c, t * P:(t + 1) * P],
                                         ka_T[r0:r0 + HD, g, :], start=True, stop=True)
                i.then_inc(at["s"], 1)

            def turn(h):
                if h == 0:
                    pe.wait_ge(at["vd"], 1)
                    pe.wait_ge(at["qa"], 2)
                    pe.wait_ge(at["qd"], 2)
                pe.wait_ge(at["p"], h + 1)
                if h >= 2:
                    pe.wait_ge(at["pt"], h - 1)
                for s_ in range(TT):
                    for t in range(TT):
                        i = nc.tensor.transpose(bank[2 + h % 2][:, s_ * T + t * P:s_ * T + t * P + P],
                                                pr[h % NSB][:, t, s_ * P:(s_ + 1) * P], ident[:])
                i.then_inc(at["tr"], 1)

            def mix(h):
                g = h // 4
                pe.wait_ge(at["pt"], h + 1)
                if h % 4 == 0 and g >= 2:
                    pe.wait_ge(at["oe"], g - 1)
                ob = bank[4 + g % 2][:].rearrange("p (t h d) -> p t h d", t=TT, h=4)
                for t in range(TT):
                    for s_ in range(TT):
                        i = nc.tensor.matmul(ob[:, t, h % 4, :], pa_T[h % 2][:, s_, t * P:(t + 1) * P],
                                             va_t[:, s_, g * HD:(g + 1) * HD], start=(s_ == 0), stop=(s_ == 1))
                i.then_inc(at["o"], 1)

            scores(0)
            for h in range(NH):
                if h + 1 < NH:
                    scores(h + 1)
                turn(h)
                if h:
                    mix(h - 1)
            mix(NH - 1)
            pe.wait_ge(at["oe"], NKV)
            branch_out(pe, o_tok, "at", 6, 1)

        def at_act(act):
            act.wait_ge(at["k"], 1)
            nc.scalar.activation(ka_T[:, 0:2, :], bank[0][:].rearrange("p (a t) -> p a t", a=2), ACT.Copy).then_inc(at["ka"], 1)
            for j in (0, 2):
                act.wait_ge(at["q"], j + 1)
                nc.scalar.activation(qa_T[:, 2 * j:2 * j + 2, :], bank[3 + j][:].rearrange("p (a t) -> p a t", a=2), ACT.Copy) \
                    .then_inc(at["qa"], 1)

            def evac(h):
                act.wait_ge(at["tr"], h + 1)
                if h >= 2:
                    act.wait_ge(at["o"], h - 1)
                nc.scalar.activation(pa_T[h % 2], bank[2 + h % 2][:].rearrange("p (s j) -> p s j", s=TT), ACT.Copy).then_inc(at["pt"], 1)

            for h in range(NH):
                act.wait_ge(at["nm"], h + 1)
                for t in range(TT):
                    i = nc.scalar.activation(pr[h % NSB][:, t, :], pr[h % NSB][:, t, :], ACT.Exp, scale=HD ** -0.5,
                                             bias=a_nm[:, t, h:h + 1], accum_out=a_sum[:, t, h:h + 1])
                i.then_inc(at["p"], 1)
                if h % 4 == 3:
                    act.wait_ge(at["ds"], h // 4 + 1)
                    v = a_ds[:, :, h - 3:h + 1]
                    nc.scalar.activation(v, v, ACT.Exp).then_inc(at["sum"], 1)
                if h:
                    evac(h - 1)
            evac(NH - 1)
            for b in (0, 2):
                act.wait_ge(mx_tr, 4 + b + 1)
                nc.scalar.activation(y_Ta[:, 2 * b:2 * b + 2, :], bank[4 + b][:].rearrange("p (a t) -> p a t", a=2), ACT.Copy) \
                    .then_inc(mx_act, 1)

        def at_dve(dve, own):
            th = own.then
            dve.wait_ge(at["iota"], 1)
            th(nc.vector.scalar_tensor_tensor(out=dist, in0=dist, scalar=-1.0, in1=dist, op0=ALU.mult, op1=ALU.max))
            th(nc.vector.tensor_scalar(dist_far, dist, float(WINDOW), 1e30, ALU.is_gt, ALU.mult))
            own.did(nc.vector.tensor_tensor(dist, dist, dist_far, ALU.add))
            own.did(nc.vector.tensor_scalar(a_nsink, sink[:], -1.0, None, ALU.mult))
            dve.wait_ge(own_dve, own.n)
            dve.wait_ge(at["k"], 2)
            nc.vector.tensor_copy(ka_T[:, 2:4, :], bank[1][:].rearrange("p (a t) -> p a t", a=2)).then_inc(at["kd"], 1)
            dve.wait_ge(at["v"], 1)
            nc.vector.tensor_copy(va_t, bank[2][:].rearrange("p (t d) -> p t d", t=TT)).then_inc(at["vd"], 1)
            for j in (1, 3):
                dve.wait_ge(at["q"], j + 1)
                nc.vector.tensor_copy(qa_T[:, 2 * j:2 * j + 2, :], bank[3 + j][:].rearrange("p (a t) -> p a t", a=2)).then_inc(at["qd"], 1)

            def finish(g):
                dve.wait_ge(at["sum"], g + 1)
                h4 = slice(4 * g, 4 * g + 4)
                th(nc.vector.tensor_tensor(a_rec[:, :, h4], a_sum[:, :, h4], a_ds[:, :, h4], ALU.add))
                th(nc.vector.reciprocal(a_rec[:, :, h4], a_rec[:, :, h4]))
                dve.wait_ge(at["o"], 4 * g + 4)
                for t in range(TT):
                    i = nc.vector.tensor_tensor(o_tok[:, t, g * 256:(g + 1) * 256].rearrange("p (h d) -> p h d", h=4),
                                                bank[4 + g % 2][:, t * T:(t + 1) * T].rearrange("p (h d) -> p h d", h=4),
                                                a_rec[:, t, h4].unsqueeze(2).broadcast_to((P, 4, HD)), ALU.mult)
                i.then_inc(at["oe"], 1)

            for h in range(NH):
                q = h % NSB
                slope = 2.0 ** (-8.0 * (h + 1) / NH)
                dve.wait_ge(at["s"], h + 1)
                if h >= NSB:
                    dve.wait_ge(at["tr"], h - NSB + 1)
                for t in range(TT):
                    off = P * (1 - t)
                    own.did(nc.vector.scalar_tensor_tensor(out=pr[q][:, t, :], in0=dist[:, off:off + T],
                                                           scalar=-slope * HD ** 0.5, in1=bank[h % 2][:, t * T:(t + 1) * T],
                                                           op0=ALU.mult, op1=ALU.add))
                dve.wait_ge(own_dve, own.n)
                th(nc.vector.tensor_reduce(a_mx[:, h % 2, :], pr[q], AX_X, ALU.max))
                nc.vector.tensor_scalar(a_nm[:, :, h], a_mx[:, h % 2, :], -HD ** -0.5, a_nsink[:, h:h + 1], ALU.mult, ALU.min) \
                    .then_inc(at["nm"], 1)
                if h % 4 == 3:
                    h4 = slice(h - 3, h + 1)
                    dve.wait_ge(at["nm"], h + 1)
                    nc.vector.tensor_tensor(a_ds[:, :, h4], a_nm[:, :, h4], sink[:, h4].unsqueeze(1).broadcast_to((P, TT, 4)),
                                            ALU.add).then_inc(at["ds"], 1)
                if h % 4 == 1 and h > 4:
                    finish(h // 4 - 1)
            finish(NKV - 1)
            for b in (1, 3):
                dve.wait_ge(mx_tr, 4 + b + 1)
                nc.vector.tensor_copy(y_Ta[:, 2 * b:2 * b + 2, :], bank[4 + b][:].rearrange("p (a t) -> p a t", a=2)).then_inc(mx_dve, 1)

        def at_pool(pool, own):
            nc.gpsimd.iota(dist, pattern=[[-1, 3 * P]], base=P, channel_multiplier=1,
                           allow_small_or_imprecise_dtypes=True).then_inc(at["iota"], 1)

        @block.tensor
        def _(pe):
            rec_pe(pe)
            norm_pe(pe, 0)
            moe_pe(pe)
            norm_pe(pe, 1)
            ffn_pe(pe, 0, 1)
            norm_pe(pe, 2)
            ml_pe(pe)
            norm_pe(pe, 3)
            ffn_pe(pe, 1, 3)
            norm_pe(pe, 4)
            ffn_pe(pe, 2, 4)
            norm_pe(pe, 5)
            at_pe(pe)
            norm_pe(pe, 6)
            ffn_pe(pe, 3, 6)

        @block.scalar
        def _(act):
            rec_act(act)
            norm_evac_act(act, 0)
            moe_act(act)
            ffn_first_act(act, 0)
            norm_evac_act(act, 1)
            ffn_act(act, 0)
            norm_evac_act(act, 2)
            ml_act(act)
            ffn_first_act(act, 1)
            norm_evac_act(act, 3)
            ffn_act(act, 1)
            ffn_first_act(act, 2)
            norm_evac_act(act, 4)
            ffn_act(act, 2)
            norm_evac_act(act, 5)
            at_act(act)
            ffn_first_act(act, 3)
            norm_evac_act(act, 6)
            ffn_act(act, 3)
            norm_act(act, 7)

        @block.vector
        def _(dve):
            own = Own(dve, own_dve)
            rec_dve(dve, own)
            norm_dve(dve, own, 0, ALPHA)
            moe_dve(dve, own)
            norm_dve(dve, own, 1, ALPHA)
            ffn_dve(dve, 0)
            norm_dve(dve, own, 2, ALPHA_2)
            ml_dve(dve, own)
            ffn_first_dve(dve, 1)
            norm_dve(dve, own, 3, ALPHA_2)
            ffn_dve(dve, 1)
            ffn_first_dve(dve, 2)
            norm_dve(dve, own, 4, ALPHA_2)
            ffn_dve(dve, 2)
            norm_dve(dve, own, 5, ALPHA_2)
            at_dve(dve, own)
            ffn_first_dve(dve, 3)
            norm_dve(dve, own, 6, ALPHA_2)
            ffn_dve(dve, 3)
            norm_dve(dve, own, 7, ALPHA_2)

        @block.sync
        def _(sp):
            sync_program(sp)

        @block.gpsimd
        def _(pool):
            pool_program(pool)


_INS = ['x', 'rec_w_in', 'rec_conv_w', 'rec_conv_b', 'rec_w_r', 'rec_b_r', 'rec_w_i', 'rec_b_i', 'rec_lambda',
        'rec_w_out', 'moe_w_group', 'moe_b_group', 'moe_w_expert', 'moe_b_expert', 'moe_w1', 'moe_w3', 'moe_w2',
        'ln_g', 'ln_b', 'ffn_w_in_2', 'ffn_w_out_2', 'ln_g_2', 'ln_b_2', 'ml_w_in_2', 'ml_gate_b_2', 'ml_norm_g_2',
        'ml_w_out_2', 'at_w_in_2', 'at_sink_2', 'at_w_out_2']


def kernel(**inputs):
    import numpy as _np
    import concourse.bacc as _bacc
    from concourse import mybir as _mybir
    from concourse.bass_utils import run_bass_kernel_spmd as _run

    nc = _bacc.Bacc("TRN2", target_bir_lowering=False, num_devices=1)
    arrays, args = {}, {}
    for name in _INS:
        a = _np.ascontiguousarray(inputs[name])
        arrays[f"in_{name}_dram"] = a
        args[name] = nc.dram_tensor(f"in_{name}_dram", a.shape, _mybir.dt.from_np(a.dtype), kind="ExternalInput").ap()
    out = nc.dram_tensor("out_0_dram", (1, T, D), F32, kind="ExternalOutput").ap()
    build(nc, args, out)
    r = _run(nc, [arrays], core_ids=[0])
    return r.results[0]["out_0_dram"]
```
